# Optimizing a Trainium2 kernel written in Bass

```python
import math
import jax, jax.numpy as jnp
from jax import lax
import numpy as np

D_MODEL = 2048
BATCH = 1
SEQ = 256
DEPTH = 4

N_MIXERS = 3
PLE_DIM = 256
NORM_EPS = 1e-6
MAX_POS_OFFSET = 1024

A_HEAD_DIM = 128
A_HEADS = D_MODEL // (2 * A_HEAD_DIM)
A_V_DIM = 2 * A_HEAD_DIM
A_WIDTH = A_HEADS * A_V_DIM
A_QK_WIDTH = A_HEADS * 2 * A_HEAD_DIM
A_IN_WIDTH = 2 * A_QK_WIDTH + 2 * A_WIDTH
ROT_DIM = A_HEAD_DIM // 4
ROPE_THETA = 500000.0
Q_BLOCK = 128
SUBLN_EPS = 1e-5

B_HEAD_DIM = 64
B_HEADS = D_MODEL // B_HEAD_DIM
B_DECAY_LORA = max(32, int(round(1.8 * D_MODEL ** 0.5 / 32)) * 32)
B_AAA_LORA = max(32, int(round(1.8 * D_MODEL ** 0.5 / 32)) * 32)
B_GN_EPS = 64e-5

C_HEAD_DIM = 128
C_K_HEADS = D_MODEL // C_HEAD_DIM
C_V_HEADS = 2 * C_K_HEADS
C_QK_WIDTH = C_K_HEADS * C_HEAD_DIM
C_V_WIDTH = C_V_HEADS * C_HEAD_DIM
C_CONV_CH = 2 * C_QK_WIDTH + C_V_WIDTH
C_IN_WIDTH = C_CONV_CH + C_V_WIDTH + 2 * C_V_HEADS
C_CONV_WIDTH = 4
C_CHUNK = 64

N_A_LAYERS = (DEPTH + 2) // 3
N_B_LAYERS = (DEPTH + 1) // 3
N_C_LAYERS = DEPTH // 3

kernel_name = 'hybrid_diffattn_rwkv7_gdn_trunk'

def rms_norm(x, g, eps=NORM_EPS):
    xf = x.astype(jnp.float32)
    y = xf * lax.rsqrt(jnp.mean(xf * xf, axis=-1, keepdims=True) + eps)
    return (y * g.astype(jnp.float32)).astype(x.dtype)

def l2_normalize(x, eps=1e-6):
    xf = x.astype(jnp.float32)
    return xf * lax.rsqrt(jnp.sum(xf * xf, axis=-1, keepdims=True) + eps)

def partial_rope(t, cos, sin):
    half = ROT_DIM // 2
    c = cos[:, :, None, None, :]
    s = sin[:, :, None, None, :]
    t1, t2, rest = t[..., :half], t[..., half:ROT_DIM], t[..., ROT_DIM:]
    return jnp.concatenate([t1 * c - t2 * s, t2 * c + t1 * s, rest.astype(jnp.float32)], axis=-1)

def diff_attention(h, positions, w_in, lam, subln_g, w_out, lam_init):
    B, T, _ = h.shape
    nb = T // Q_BLOCK
    q, k, v, z = jnp.split(h @ w_in, [A_QK_WIDTH, 2 * A_QK_WIDTH, 2 * A_QK_WIDTH + A_WIDTH], axis=-1)
    q = q.reshape(B, T, A_HEADS, 2, A_HEAD_DIM)
    k = k.reshape(B, T, A_HEADS, 2, A_HEAD_DIM)
    v = v.reshape(B, T, A_HEADS, A_V_DIM)
    inv_freq = ROPE_THETA ** (-jnp.arange(0, ROT_DIM, 2, dtype=jnp.float32) / ROT_DIM)
    ang = positions.astype(jnp.float32)[..., None] * inv_freq
    cos, sin = jnp.cos(ang), jnp.sin(ang)
    q = partial_rope(q.astype(jnp.float32), cos, sin) * (A_HEAD_DIM ** -0.5)
    k = partial_rope(k.astype(jnp.float32), cos, sin)
    lam32 = lam.astype(jnp.float32)
    lam_full = jnp.exp(jnp.sum(lam32[0] * lam32[1])) - jnp.exp(jnp.sum(lam32[2] * lam32[3])) + lam_init
    q_blocks = q.reshape(B, nb, Q_BLOCK, A_HEADS, 2, A_HEAD_DIM).transpose(1, 0, 3, 4, 2, 5)
    k_t = k.transpose(0, 2, 3, 1, 4)
    v_t = v.astype(jnp.float32).transpose(0, 2, 1, 3)
    key_pos = jnp.arange(T)

    def one_block(args):
        q_blk, blk = args
        s = jnp.einsum('bhcqd,bhckd->bhcqk', q_blk, k_t)
        q_pos = blk * Q_BLOCK + jnp.arange(Q_BLOCK)
        causal = key_pos[None, :] <= q_pos[:, None]
        p_attn = jax.nn.softmax(jnp.where(causal, s, -jnp.inf), axis=-1)
        diff_map = p_attn[:, :, 0] - lam_full * p_attn[:, :, 1]
        return jnp.einsum('bhqk,bhkv->bhqv', diff_map, v_t)

    o = lax.map(one_block, (q_blocks, jnp.arange(nb)))
    o = o.transpose(1, 0, 3, 2, 4).reshape(B, T, A_HEADS, A_V_DIM)
    o = rms_norm(o, subln_g, SUBLN_EPS) * (1.0 - lam_init)
    o = o.reshape(B, T, A_WIDTH) * jax.nn.silu(z.astype(jnp.float32))
    return (o @ w_out).astype(h.dtype)

def rwkv7_time_mix(h, mu, w_rkvg, w0, w_w1, w_w2, a0, w_a1, w_a2, k_k, k_a, r_k, ln_w, ln_b, w_out):
    B, T, D = h.shape
    H, N = B_HEADS, B_HEAD_DIM
    xx = jnp.pad(h, ((0, 0), (1, 0), (0, 0)))[:, :-1] - h
    x_r, x_w, x_k, x_v, x_a, x_g = [h + xx * mu[c] for c in range(6)]

    def heads(t):
        return t.reshape(B, T, H, N).astype(jnp.float32)

    r = heads(x_r @ w_rkvg[0])
    k = heads(x_k @ w_rkvg[1])
    v = heads(x_v @ w_rkvg[2])
    g = x_g @ w_rkvg[3]
    log_w = -jax.nn.softplus(-(w0 + jnp.tanh(x_w @ w_w1) @ w_w2).astype(jnp.float32)) - 0.5
    decay = heads(jnp.exp(-jnp.exp(log_w)))
    a = heads(jax.nn.sigmoid((a0 + (x_a @ w_a1) @ w_a2).astype(jnp.float32)))
    kk = l2_normalize(k * k_k.reshape(H, N))
    k = k * (1.0 + (a - 1.0) * k_a.reshape(H, N))

    def step(S, inp):
        r_t, w_t, k_t, v_t, kk_t, b_t = inp
        sa = jnp.einsum('bhvk,bhk->bhv', S, kk_t)
        S = S * w_t[:, :, None, :] - sa[..., None] * b_t[:, :, None, :] + v_t[..., None] * k_t[:, :, None, :]
        return S, jnp.einsum('bhvk,bhk->bhv', S, r_t)

    xs = tuple(jnp.swapaxes(t, 0, 1) for t in (r, decay, k, v, kk, kk * a))
    S0 = jnp.zeros((B, H, N, N), jnp.float32)
    _, o = lax.scan(step, S0, xs)
    o = jnp.swapaxes(o, 0, 1)
    mean = jnp.mean(o, axis=-1, keepdims=True)
    var = jnp.mean(jnp.square(o - mean), axis=-1, keepdims=True)
    o = (o - mean) * lax.rsqrt(var + B_GN_EPS) * ln_w.reshape(H, N) + ln_b.reshape(H, N)
    o = o + jnp.sum(r * k * r_k, axis=-1, keepdims=True) * v
    o = o.reshape(B, T, D) * jax.nn.silu(g.astype(jnp.float32))
    return (o @ w_out).astype(h.dtype)

def causal_conv(x, w):
    K = w.shape[0]
    T = x.shape[1]
    xp = jnp.pad(x, ((0, 0), (K - 1, 0), (0, 0)))
    return sum(xp[:, j:j + T] * w[j] for j in range(K))

def chunk_gated_delta_rule(q, k, v, g, beta):
    B, T, H, Dk = q.shape
    Dv = v.shape[-1]
    C = C_CHUNK
    N = T // C

    def chunks(t):
        return t.astype(jnp.float32).reshape(B, N, C, H, -1).transpose(1, 0, 3, 2, 4)

    qc, kc, vc = chunks(q), chunks(k), chunks(v)
    gc = jnp.cumsum(g.astype(jnp.float32).reshape(B, N, C, H).transpose(1, 0, 3, 2), axis=-1)
    bc = beta.astype(jnp.float32).reshape(B, N, C, H).transpose(1, 0, 3, 2)
    tri = jnp.tril(jnp.ones((C, C), dtype=bool))
    strict = jnp.tril(jnp.ones((C, C), dtype=bool), k=-1)
    decay = jnp.exp(jnp.where(tri, gc[..., :, None] - gc[..., None, :], -jnp.inf))
    kb = kc * bc[..., None]
    A = jnp.where(strict, jnp.einsum('nbhcd,nbhsd->nbhcs', kb, kc) * decay, 0.0)
    rhs = jnp.concatenate([vc * bc[..., None], kb * jnp.exp(gc)[..., None]], axis=-1)
    sol = lax.linalg.triangular_solve(A, rhs, left_side=True, lower=True, unit_diagonal=True)
    u, w = sol[..., :Dv], sol[..., Dv:]
    intra = jnp.where(tri, jnp.einsum('nbhcd,nbhsd->nbhcs', qc, kc) * decay, 0.0)

    def step(S, inp):
        q_, k_, u_, w_, g_, att = inp
        v_new = u_ - jnp.einsum('bhck,bhkv->bhcv', w_, S)
        o = jnp.einsum('bhck,bhkv->bhcv', q_ * jnp.exp(g_)[..., None], S) + jnp.einsum('bhcs,bhsv->bhcv', att, v_new)
        g_last = g_[..., -1:]
        S = S * jnp.exp(g_last)[..., None] + jnp.einsum('bhck,bhcv->bhkv', k_ * jnp.exp(g_last - g_)[..., None], v_new)
        return S, o

    S0 = jnp.zeros((B, H, Dk, Dv), jnp.float32)
    _, o = lax.scan(step, S0, (qc, kc, u, w, gc, intra))
    return o.transpose(1, 0, 3, 2, 4).reshape(B, T, H, Dv)

def gated_deltanet(h, w_in, conv_w, A_log, dt_bias, norm_g, w_out):
    B, T, _ = h.shape
    qkv, z, b, a = jnp.split(h @ w_in, [C_CONV_CH, C_CONV_CH + C_V_WIDTH, C_CONV_CH + C_V_WIDTH + C_V_HEADS], axis=-1)
    qkv = jax.nn.silu(causal_conv(qkv, conv_w))
    q, k, v = jnp.split(qkv, [C_QK_WIDTH, 2 * C_QK_WIDTH], axis=-1)
    rep = C_V_HEADS // C_K_HEADS
    q = jnp.repeat(l2_normalize(q.reshape(B, T, C_K_HEADS, C_HEAD_DIM)) * (C_HEAD_DIM ** -0.5), rep, axis=2)
    k = jnp.repeat(l2_normalize(k.reshape(B, T, C_K_HEADS, C_HEAD_DIM)), rep, axis=2)
    v = v.reshape(B, T, C_V_HEADS, C_HEAD_DIM)
    beta = jax.nn.sigmoid(b.astype(jnp.float32))
    g = -jnp.exp(A_log.astype(jnp.float32)) * jax.nn.softplus((a + dt_bias).astype(jnp.float32))
    o = chunk_gated_delta_rule(q, k, v, g, beta)
    o = rms_norm(o, norm_g) * jax.nn.silu(z.reshape(B, T, C_V_HEADS, C_HEAD_DIM).astype(jnp.float32))
    return (o.reshape(B, T, C_V_WIDTH) @ w_out).astype(h.dtype)

def setup_inputs(seed: int = 0) -> dict:
    key = jax.random.key(seed)
    keys = iter(jax.random.split(key, 40))

    def normal(shape, scale):
        return jax.random.normal(next(keys), shape, jnp.float32) * scale

    def gain(shape):
        return 1.0 + normal(shape, 0.02)

    d = D_MODEL
    x = normal((BATCH, SEQ, d), 1.0)
    p = normal((DEPTH, BATCH, SEQ, PLE_DIM), 1.0)
    positions = jnp.arange(SEQ, dtype=jnp.int32)[None, :] + jax.random.randint(next(keys), (BATCH, 1), 0, MAX_POS_OFFSET, dtype=jnp.int32)
    norm_g = gain((DEPTH, d))
    pe_norm_g = gain((DEPTH, d))
    pe_w_gate = normal((DEPTH, d, d), d ** -0.5)
    pe_w_proj = normal((DEPTH, PLE_DIM, d), PLE_DIM ** -0.5)
    final_norm_g = gain((d,))
    a_w_in = normal((N_A_LAYERS, d, A_IN_WIDTH), d ** -0.5)
    a_lam = normal((N_A_LAYERS, 4, A_HEAD_DIM), 0.1)
    a_subln_g = gain((N_A_LAYERS, A_V_DIM))
    a_w_out = normal((N_A_LAYERS, A_WIDTH, d), A_WIDTH ** -0.5)
    b_mu = jax.random.uniform(next(keys), (N_B_LAYERS, 6, d), jnp.float32)
    b_w_rkvg = normal((N_B_LAYERS, 4, d, d), d ** -0.5)
    b_w0 = jax.random.uniform(next(keys), (N_B_LAYERS, d), jnp.float32, -6.0, 1.0)
    b_w_w1 = normal((N_B_LAYERS, d, B_DECAY_LORA), d ** -0.5)
    b_w_w2 = normal((N_B_LAYERS, B_DECAY_LORA, d), 0.1 * B_DECAY_LORA ** -0.5)
    b_a0 = normal((N_B_LAYERS, d), 0.1)
    b_w_a1 = normal((N_B_LAYERS, d, B_AAA_LORA), d ** -0.5)
    b_w_a2 = normal((N_B_LAYERS, B_AAA_LORA, d), B_AAA_LORA ** -0.5)
    b_k_k = 0.85 + normal((N_B_LAYERS, d), 0.02)
    b_k_a = 1.0 + normal((N_B_LAYERS, d), 0.02)
    b_r_k = normal((N_B_LAYERS, B_HEADS, B_HEAD_DIM), 0.1)
    b_ln_w = gain((N_B_LAYERS, d))
    b_ln_b = normal((N_B_LAYERS, d), 0.01)
    b_w_out = normal((N_B_LAYERS, d, d), d ** -0.5)
    c_w_in = normal((N_C_LAYERS, d, C_IN_WIDTH), d ** -0.5)
    c_conv_w = normal((N_C_LAYERS, C_CONV_WIDTH, C_CONV_CH), C_CONV_WIDTH ** -0.5)
    c_A_log = jnp.log(jax.random.uniform(next(keys), (N_C_LAYERS, C_V_HEADS), jnp.float32, 1.0, 16.0))
    dt = jnp.exp(jax.random.uniform(next(keys), (N_C_LAYERS, C_V_HEADS), jnp.float32, math.log(1e-3), math.log(1e-1)))
    c_dt_bias = dt + jnp.log(-jnp.expm1(-dt))
    c_norm_g = gain((N_C_LAYERS, C_HEAD_DIM))
    c_w_out = normal((N_C_LAYERS, C_V_WIDTH, d), C_V_WIDTH ** -0.5)
    return {'x': x, 'p': p, 'positions': positions, 'norm_g': norm_g, 'pe_norm_g': pe_norm_g,
            'pe_w_gate': pe_w_gate, 'pe_w_proj': pe_w_proj, 'final_norm_g': final_norm_g,
            'a_w_in': a_w_in, 'a_lam': a_lam, 'a_subln_g': a_subln_g, 'a_w_out': a_w_out,
            'b_mu': b_mu, 'b_w_rkvg': b_w_rkvg, 'b_w0': b_w0, 'b_w_w1': b_w_w1, 'b_w_w2': b_w_w2,
            'b_a0': b_a0, 'b_w_a1': b_w_a1, 'b_w_a2': b_w_a2, 'b_k_k': b_k_k, 'b_k_a': b_k_a,
            'b_r_k': b_r_k, 'b_ln_w': b_ln_w, 'b_ln_b': b_ln_b, 'b_w_out': b_w_out,
            'c_w_in': c_w_in, 'c_conv_w': c_conv_w, 'c_A_log': c_A_log, 'c_dt_bias': c_dt_bias,
            'c_norm_g': c_norm_g, 'c_w_out': c_w_out}

def reference(x, p, positions, norm_g, pe_norm_g, pe_w_gate, pe_w_proj, final_norm_g,
              a_w_in, a_lam, a_subln_g, a_w_out,
              b_mu, b_w_rkvg, b_w0, b_w_w1, b_w_w2, b_a0, b_w_a1, b_w_a2, b_k_k, b_k_a,
              b_r_k, b_ln_w, b_ln_b, b_w_out,
              c_w_in, c_conv_w, c_A_log, c_dt_bias, c_norm_g, c_w_out):
    for i in range(DEPTH):
        kind = i % N_MIXERS
        j = i // N_MIXERS
        hn = rms_norm(x, norm_g[i])
        if kind == 0:
            lam_init = 0.8 - 0.6 * math.exp(-0.3 * i)
            y = diff_attention(hn, positions, a_w_in[j], a_lam[j], a_subln_g[j], a_w_out[j], lam_init)
        elif kind == 1:
            y = rwkv7_time_mix(hn, b_mu[j], b_w_rkvg[j], b_w0[j], b_w_w1[j], b_w_w2[j], b_a0[j],
                               b_w_a1[j], b_w_a2[j], b_k_k[j], b_k_a[j], b_r_k[j], b_ln_w[j],
                               b_ln_b[j], b_w_out[j])
        else:
            y = gated_deltanet(hn, c_w_in[j], c_conv_w[j], c_A_log[j], c_dt_bias[j], c_norm_g[j], c_w_out[j])
        x = x + y.astype(x.dtype)
        gate = jax.nn.sigmoid((rms_norm(x, pe_norm_g[i]) @ pe_w_gate[i]).astype(jnp.float32))
        x = x + (gate * (p[i] @ pe_w_proj[i]).astype(jnp.float32)).astype(x.dtype)
    return rms_norm(x, final_norm_g)


_drawn_inputs = setup_inputs


def setup_inputs(seed=0):
    import zlib

    import numpy as np

    out = dict(_drawn_inputs(seed))
    spreads = {}
    factors = {'pe_norm_g': 25.656,
     'final_norm_g': 7.989,
     'a_subln_g': 5.59,
     'b_w_w1': 8.0,
     'b_w_w2': 8.0,
     'b_a0': 4.117,
     'b_k_k': 27.516,
     'b_k_a': 7.001,
     'b_ln_w': 8.0,
     'b_ln_b': 38.859,
     'c_norm_g': 31.219}
    for name, (base, spread) in spreads.items():
        noise = np.random.default_rng([zlib.crc32(name.encode()), seed]).standard_normal(out[name].shape)
        drawn = base * np.exp(spread * noise) if base else spread * noise
        out[name] = __import__('jax').numpy.asarray(drawn.astype(out[name].dtype))
    for name, factor in factors.items():
        out[name] = (out[name] * factor).astype(out[name].dtype)
    return out
```

```python
from contextlib import ExitStack
import math

import numpy as np
import concourse.bass as bass
from concourse import mybir

F32 = mybir.dt.float32
F32R = mybir.dt.float32r
I32 = mybir.dt.int32
ALU = mybir.AluOpType
ACT = mybir.ActivationFunctionType
AX = mybir.AxisListType

P = 128
D = 2048
SEQ = 256
NT = SEQ // P
KT = D // P
NC = 512
CK = 4
CHUNK = CK * NC
RAW = 4
SPLIT = 2
DEPTH = 4
PLE = 256
EPS = 1e-6
LN_LIMIT = 44.0
LIMIT = 85.0

A_HD = 128
A_GROUPS = 4
A_HC = 4
A_VD = 256
A_SUBLN_EPS = 1e-5
ROT_HALF = 16
ROPE_THETA = 500000.0

B_HD = 64
B_LORA = 96
B_GN_EPS = 64e-5
B_C = math.exp(-0.5)
B_GROUPS = 4

C_HD = 128
C_GROUPS = 4
C_VH = 32
C_QK = 2048
C_VW = 4096
C_TAPS = 4

COL = {}
_at = 0
for _name, _n in (("norm_g", DEPTH * KT), ("pe_norm_g", DEPTH * KT), ("mu", 6 * KT), ("subln_g", 2 * 2),
                  ("c_norm_g", 1), ("conv", 64 * C_TAPS)):
    COL[_name] = _at
    _at += _n
NCOLS = _at

CON = {}
_at = 0
for _name, _n in (("ident", P), ("tri", P), ("tri_incl_mid", P), ("tri_excl_mid", P), ("ones", P), ("mask4", 4 * P),
                  ("negmask", 3 * P), ("level1_t", P), ("levels", 7 * P), ("first_half", 1), ("second_half", 1),
                  ("inv_freq", ROT_HALF)):
    CON[_name] = _at
    _at += _n
NCONS = _at


def constants():
    c = np.zeros((P, NCONS), np.float32)
    i, j = np.arange(P)[:, None], np.arange(P)[None, :]

    def put(name, a):
        c[:, CON[name]:CON[name] + a.shape[1]] = a

    put("ident", i == j)
    put("tri", i <= j)
    mid = (i < P // 2).astype(np.float32)
    put("tri_incl_mid", (i <= j) - mid)
    put("tri_excl_mid", (i < j) - mid)
    put("ones", np.ones((P, P)))
    put("mask4", np.concatenate([i < j, i <= j, i < j, i <= j], 1))
    neg = np.where(j <= i, 0.0, -1e30)
    put("negmask", np.concatenate([neg, np.zeros((P, P)), neg], 1))
    levels = []
    for n in range(7):
        m = 1 << n
        levels.append((i // (2 * m) == j // (2 * m)) & (i // m % 2 == 1) & (j // m % 2 == 0))
    put("levels", np.concatenate(levels, 1))
    put("level1_t", levels[0].T)
    put("first_half", i < P // 2)
    put("second_half", i >= P // 2)
    f = (np.float32(ROPE_THETA) ** (-np.arange(0, 2 * ROT_HALF, 2, dtype=np.float32) / np.float32(2 * ROT_HALF)))
    put("inv_freq", np.broadcast_to(f.astype(np.float32), (P, ROT_HALF)))
    return c


SHARED = ("act_steps", "dve_steps", "out_turned", "out_hi", "out_lo", "gated", "inv_pe", "inv_dve")


class Signal:

    def __init__(self, sem):
        self.sem, self.base, self.per, self.n = sem, 0, 0, 0

    def count(self, turn, n):
        return self.base + self.per * turn + n

    def inc(self, ins, k=1):
        ins.then_inc(self.sem, k)
        self.n += k
        return self.n


class Kernel:
    def __init__(self, nc, ctx, t):
        self.nc, self.ctx, self.t = nc, ctx, t
        self.signals = {}
        self.names = 0
        self.stage = []
        self.pos = 0
        self.tiles = 0
        sb, sig = self.sb, self.sig
        self.x = sb("x", [P, NT, D])
        self.raw = sb("raw", [P, RAW, CHUNK])
        self.whi = sb("whi", [P, SPLIT, CHUNK], F32R)
        self.wlo = sb("wlo", [P, SPLIT, CHUNK], F32R)
        self.con = sb("con", [P, NCONS])
        self.cols = sb("cols", [P, NCOLS])
        self.eps = sb("eps", [P, 4])
        self.stat = sb("stat", [P, 8])
        self.psum = ctx.enter_context(nc.psum_tensor("psum", [P, 8, NC], F32))
        self.landed = [self.sem(f"chunk_landed{i}") for i in range(RAW)]
        self.split_hi = Signal(self.sem("chunk_split_hi"))
        self.split_lo = Signal(self.sem("chunk_split_lo"))
        self.used = Signal(self.sem("chunk_used"))
        self.acc_free = Signal(self.sem("acc_free"))

    def sb(self, name, shape, dt=F32, ctx=None):
        self.names += 1
        return (ctx or self.ctx).enter_context(self.nc.sbuf_tensor(f"{name}_{self.names}", shape, dt))

    def sem(self, name):
        return self.ctx.enter_context(self.nc.semaphore(name))

    def sig(self, name, per):
        if name.split("_", 1)[-1] in SHARED:
            name = name.split("_", 1)[-1]
        if name not in self.signals:
            self.signals[name] = Signal(self.sem(name))
        s = self.signals[name]
        s.per, s.n = per, 0
        self.stage.append((name, s))
        return s

    def con_(self, name, n):
        return self.con[:, CON[name]:CON[name] + n]

    def col(self, name, i, n=1):
        return self.cols[:, COL[name] + i:COL[name] + i + n]

    def begin(self, no, tiles):
        self.stage_no, self.stage, self.tiles_per = no, [], tiles
        self.chunks, self.turns, self.source = (0, 1, None) if no is None else self.plan[no]

    def end(self):
        wrong = [(name, s.n, s.per) for name, s in self.stage if s.n != s.per]
        assert not wrong, wrong
        for name, s in self.stage:
            s.base += s.per * self.turns
        self.pos += self.chunks * self.turns
        self.tiles += self.tiles_per * self.turns

    def index(self, turn, k):
        return self.pos + self.chunks * turn + k

    def load(self, sp, turn, k, parts, wait=True):
        slot = (self.pos + k) % RAW
        if wait:
            sp.wait_ge(self.split_hi.sem, self.index(turn, k) - RAW + 1)
            sp.wait_ge(self.split_lo.sem, self.index(turn, k) - RAW + 1)
        dst, src = parts(self.raw[:, slot, :])
        sp.dma_start(dst, src).then_inc(self.landed[slot], 16)

    def stream(self, sp, turns=1):
        if turns > 1:
            with sp.Fori(0, turns - 1) as g:
                for k in range(RAW, self.chunks + RAW):
                    self.load(sp, g, k, self.source(k % self.chunks, g + k // self.chunks))
        for k in range(min(RAW, self.chunks), self.chunks + RAW) if turns > 1 else range(RAW, self.chunks + RAW):
            if turns > 1 and k < RAW:
                continue
            if k < self.chunks:
                self.load(sp, turns - 1, k, self.source(k, turns - 1))
            else:
                src = self.following(k - self.chunks)
                if src is not None:
                    self.load(sp, turns - 1, k, src)

    def following(self, i):
        for chunks, turns, source in self.plan[self.stage_no + 1:]:
            if i < chunks * turns:
                return source(i % chunks, i // chunks)
            i -= chunks * turns
        return None

    def split_act(self, act, turn, k):
        if self.no_chunk(turn, k):
            return
        slot, s = (self.pos + k) % RAW, (self.pos + k) % SPLIT
        act.wait_ge(self.landed[slot], 16 * ((self.pos + k) // RAW + 1) + 16 * (self.chunks // RAW) * turn
                    if self.chunks % RAW == 0 else 16 * ((self.pos + k) // RAW + 1))
        act.wait_ge(self.used.sem, self.index(turn, k) - SPLIT + 1 + SPLIT)
        act.activation(self.whi[:, s, :], self.raw[:, slot, :], ACT.Copy).then_inc(self.split_hi.sem, 1)

    def split_dve(self, dve, turn, k):
        if self.no_chunk(turn, k):
            return
        slot, s = (self.pos + k) % RAW, (self.pos + k) % SPLIT
        dve.wait_ge(self.split_hi.sem, self.index(turn, k) + 1)
        dve.tensor_tensor(self.wlo[:, s, :], self.raw[:, slot, :], self.whi[:, s, :].bitcast(F32),
                          ALU.subtract).then_inc(self.split_lo.sem, 1)

    def pair(self, t):
        return 2 * ((self.tiles + t) % 2)

    def acc(self, t, half):
        return self.psum[:, self.pair(t) + half, :]

    def acc2(self, t):
        a = self.pair(t)
        return self.psum[:, a:a + 2, :]

    def acc_open(self, pe, turn, t):
        pe.wait_ge(self.acc_free.sem, self.tiles + t + 1 + self.tiles_per * turn)

    def acc_wait(self, eng, turn, k):
        eng.wait_ge(self.used.sem, self.index(turn, k) + 1 + SPLIT)

    def acc_was_read(self, eng, turn, t):
        eng.wait_ge(self.acc_free.sem, self.tiles + t + 3 + self.tiles_per * turn)

    def loop(self, eng, body):
        whole = self.turns - (self.following(0) is None)
        before = [s.n for _, s in self.stage]
        if whole > 0:
            with eng.Fori(0, whole) as g:
                body(g)
        if whole < self.turns:
            for (_, s), n in zip(self.stage, before):
                s.n = n
            body(self.turns - 1)

    def no_chunk(self, turn, k):
        return isinstance(turn, int) and k >= self.chunks * (self.turns - turn) and self.following(0) is None

    def product(self, pe, turn, k, t, hi, lo, kts, cols=NC, rows=P, first=True, last=True, at=0, step=None, release=True):
        s = (self.pos + k) % SPLIT
        pe.wait_ge(self.split_lo.sem, self.index(turn, k) + 1)
        for n, kt in enumerate(kts):
            a = at + n * (step or cols)
            wh, wl = self.whi[0:rows, s, a:a + cols], self.wlo[0:rows, s, a:a + cols]
            for half in range(NT):
                o = self.acc(t, half)[:, 0:cols]
                h, l = hi[0:rows, kt, half * P:half * P + P], lo[0:rows, kt, half * P:half * P + P]
                pe.matmul(o, h, wh, start=first and n == 0, stop=False)
                pe.matmul(o, h, wl, start=False, stop=False)
                mm = pe.matmul(o, l, wh, start=False, stop=last and n == len(kts) - 1)
        if release:
            mm.then_inc(self.used.sem, 1)
        return mm

    def product_t(self, pe, turn, k, t, hi, lo, kts, first=True, last=True):
        s = (self.pos + k) % SPLIT
        pe.wait_ge(self.split_lo.sem, self.index(turn, k) + 1)
        for n, kt in enumerate(kts):
            for ct in range(4):
                a = n * NC + ct * P
                wh, wl = self.whi[:, s, a:a + P], self.wlo[:, s, a:a + P]
                o = self.acc(t, ct // 2)[:, ct % 2 * SEQ:ct % 2 * SEQ + SEQ]
                pe.matmul(o, wh, hi[:, kt, :], start=first and n == 0 and ct % 2 == 0, stop=False, skip_group_check=True)
                pe.matmul(o, wl, hi[:, kt, :], start=False, stop=False, skip_group_check=True)
                mm = pe.matmul(o, wh, lo[:, kt, :], start=False, stop=last and n == len(kts) - 1, skip_group_check=True)
        mm.then_inc(self.used.sem, 1)
        return mm


class Turn:

    def __init__(self, eng, turn, steps):
        self.eng, self.turn, self.steps = eng, turn, steps

    def wait(self, signal, n=1):
        self.eng.wait_ge(signal.sem, signal.count(self.turn, n))

    def step(self, ins):
        n = self.steps.inc(ins)
        self.wait(self.steps, n)


def dma_parts(w, k0, nk, c0, width=NC):
    def parts(slot):
        src = w[bass.ds(k0 * P, nk * P), bass.ds(c0, width)].rearrange("(k p) n -> p k n", p=P)
        return slot[:, 0:nk * width].rearrange("p (k n) -> p k n", k=nk), src
    return parts


def start_stage(K):
    nc, t = K.nc, K.t
    inputs = K.sem("inputs_landed")
    with nc.Block() as block:
        @block.sync
        def _(sp):
            for k in range(RAW):
                K.load(sp, 0, k, K.plan[0][2](k, 0), wait=False)

        @block.scalar
        def _(act):
            act.dma_start(K.x[:, :, :], t["x"].rearrange("(t p) d -> p t d", p=P)).then_inc(inputs, 16)
            act.dma_start(K.con[:, :], t["con"]).then_inc(inputs, 16)
            act.dma_start(K.cols[:, :], t["cols"]).then_inc(inputs, 16)
            act.preload_act_table_set("natural_log_exp_and_others")
            act.wait_ge(K.landed[0], 16)
            act.activation(K.whi[:, 0, :], K.raw[:, 0, :], ACT.Copy).then_inc(K.split_hi.sem, 1)
            act.wait_ge(inputs, 48)

        @block.vector
        def _(dve):
            for i, v in enumerate((EPS, A_SUBLN_EPS, B_GN_EPS, 1.0)):
                ins = dve.memset(K.eps[:, i:i + 1], v)
                ins.then_inc(K.acc_free.sem if i < 2 else K.used.sem, 1)
            dve.wait_ge(K.split_hi.sem, 1)
            dve.tensor_tensor(K.wlo[:, 0, :], K.raw[:, 0, :], K.whi[:, 0, :].bitcast(F32),
                              ALU.subtract).then_inc(K.split_lo.sem, 1)


def norm_stage(K, no, gcol, hi, lo, plain=None, embed=None):
    nc = K.nc
    K.begin(no, 4 if embed else 0)
    squared, normed, turned = K.sig("squared", NT), K.sig("normed", NT), K.sig("turned", KT // 2)
    his, los = K.sig("norm_hi", KT // 2), K.sig("norm_lo", KT // 2 if plain is None else 0)
    read = los if plain is None else his
    own = K.sig("act_chain", 2 + (2 if embed else 0))
    if embed:
        p_in, p_hi, p_lo = K.sig("p_landed", 16), K.sig("p_hi", 1), K.sig("p_lo", 1)
    with ExitStack() as st:
        xn = K.sb("xn", [P, NT, D], ctx=st)
        if embed:
            layer, out = embed
            pt = K.sb("pt", [P, 2, SEQ], ctx=st)
            pt_hi = K.sb("pt_hi", [P, 2, SEQ], F32R, ctx=st)
            pt_lo = K.sb("pt_lo", [P, 2, SEQ], F32R, ctx=st)
        block = st.enter_context(nc.Block())

        def bank(i):
            return K.psum[:, 4 + i % 4, :]

        @block.sync
        def _(sp):
            if embed:
                p_in.inc(sp.dma_start(pt[:, :, :], K.t["p_t"][layer].rearrange("(k p) t -> p k t", p=P)), 16)
                K.stream(sp)

        @block.scalar
        def _(act):
            for half in range(NT):
                squared.inc(act.activation(xn[:, half, :], K.x[:, half, :], ACT.Square,
                                           accum_out=K.stat[:, half:half + 1]))
            act.wait_ge(squared.sem, squared.count(0, NT))
            own.inc(act.activation(K.stat[:, 2:4], K.stat[:, 0:2], ACT.Ln, bias=K.eps[:, 0:1], scale=1.0 / D))
            act.wait_ge(own.sem, own.count(0, 1))
            own.inc(act.activation(K.stat[:, 4:6], K.stat[:, 2:4], ACT.Exp, scale=-0.5))
            if embed:
                act.wait_ge(p_in.sem, p_in.count(0, 16))
                p_hi.inc(act.activation(pt_hi[:, :, :], pt[:, :, :], ACT.Copy))
                for k in range(1, K.chunks + 1):
                    K.split_act(act, 0, k)
                for t in range(4):
                    K.acc_wait(act, 0, t // 2)
                    act.activation(out[:, :, t * NC:(t + 1) * NC], K.acc2(t), ACT.Copy).then_inc(K.acc_free.sem, 1)
                    if t < 2:
                        own.inc(act.activation(K.stat[:, 6 + t:7 + t], K.stat[:, 4:5], ACT.Copy))
            for i in range(KT // 2):
                act.wait_ge(turned.sem, turned.count(0, i + 1))
                for kk in range(2):
                    k = 2 * i + kk
                    src = bank(i)[:, kk * SEQ:(kk + 1) * SEQ]
                    dst = plain if plain is not None else hi
                    ins = act.activation(dst[:, k, :], src, ACT.Copy, scale=K.col(gcol[0], gcol[1] + k))
                his.inc(ins)

        @block.vector
        def _(dve):
            if embed:
                dve.wait_ge(p_hi.sem, p_hi.count(0, 1))
                p_lo.inc(dve.tensor_tensor(pt_lo[:, :, :], pt[:, :, :], pt_hi[:, :, :].bitcast(F32), ALU.subtract))
                for k in range(1, K.chunks + 1):
                    K.split_dve(dve, 0, k)
            dve.wait_ge(own.sem, own.count(0, 2))
            for half in range(NT):
                normed.inc(dve.tensor_scalar(xn[:, half, :], K.x[:, half, :], K.stat[:, 4 + half:5 + half], None,
                                             ALU.mult))
            for i in range(KT // 2 if plain is None else 0):
                dve.wait_ge(his.sem, his.count(0, i + 1))
                for kk in range(2):
                    k = 2 * i + kk
                    src = bank(i)[:, kk * SEQ:(kk + 1) * SEQ]
                    ins = dve.scalar_tensor_tensor(out=lo[:, k, :], in0=src, scalar=K.col(gcol[0], gcol[1] + k),
                                                   in1=hi[:, k, :].bitcast(F32), op0=ALU.mult, op1=ALU.subtract)
                los.inc(ins)

        @block.tensor
        def _(pe):
            if embed:
                pe.wait_ge(p_lo.sem, p_lo.count(0, 1))
                for t in range(4):
                    K.acc_open(pe, 0, t)
                    K.product(pe, 0, t // 2, t, pt_hi, pt_lo, (0, 1), at=t % 2 * NC, step=2 * NC, release=t % 2 == 1)
            pe.wait_ge(normed.sem, normed.count(0, NT))
            for i in range(KT // 2):
                if i >= 4:
                    pe.wait_ge(read.sem, read.count(0, i - 3))
                for kk in range(2):
                    for half in range(NT):
                        c = kk * SEQ + half * P
                        k = 2 * i + kk
                        mm = pe.transpose(bank(i)[:, c:c + P], xn[:, half, k * P:(k + 1) * P], K.con_("ident", P))
                turned.inc(mm)
    K.end()


def gate_stage(K, no, hi, lo, pp):
    nc = K.nc
    K.begin(no, 2)
    expd = K.sig("gate_exp", 2)
    steps = K.sig("gate_steps", 8)
    with ExitStack() as st:
        e = K.sb("gate_e", [P, 2, NT, NC], ctx=st)
        block = st.enter_context(nc.Block())

        @block.sync
        def _(sp):
            K.stream(sp, K.turns)

        @block.scalar
        def _(act):
            def turn(g):
                for t in range(2):
                    for k in range(4 * t + 1, 4 * t + 5):
                        K.split_act(act, g, k)
                    K.acc_was_read(act, g, t)
                    expd.inc(act.activation(e[:, t, :, :], e[:, t, :, :], ACT.Exp, scale=-1.0))

            K.loop(act, turn)

        @block.vector
        def _(dve):
            def turn(g):
                def step(ins):
                    dve.wait_ge(steps.sem, steps.count(g, steps.inc(ins)))

                for t in range(2):
                    for k in range(4 * t + 1, 4 * t + 5):
                        K.split_dve(dve, g, k)
                    K.acc_wait(dve, g, 4 * t + 3)
                    dve.tensor_scalar(e[:, t, :, :], K.acc2(t), -LIMIT, None, ALU.max).then_inc(K.acc_free.sem, 1)
                    dve.wait_ge(expd.sem, expd.count(g, t + 1))
                    c = bass.ds(g * 2 * NC + t * NC, NC)
                    et = e[:, t, :, :]
                    step(dve.tensor_scalar(et, et, 1.0, None, ALU.add))
                    step(dve.reciprocal(et, et))
                    step(dve.tensor_tensor(et, et, pp[:, :, c], ALU.mult))
                    step(dve.tensor_tensor(K.x[:, :, c], K.x[:, :, c], et, ALU.add))

            K.loop(dve, turn)

        @block.tensor
        def _(pe):
            def turn(g):
                for t in range(2):
                    K.acc_open(pe, g, t)
                    for c in range(4):
                        K.product(pe, g, 4 * t + c, t, hi, lo, range(4 * c, 4 * c + 4), first=c == 0, last=c == 3)

            K.loop(pe, turn)
    K.end()


def final_stage(K):
    nc = K.nc
    g_in, squared, steps, out_done = K.sem("final_g_landed"), K.sem("final_squared"), K.sem("final_steps"), K.sem("out_done")
    scaled = K.sem("final_scaled")
    with ExitStack() as st:
        y = K.sb("y", [P, NT, D], ctx=st)
        gain = K.sb("gain", [P, D], ctx=st)
        block = st.enter_context(nc.Block())

        @block.sync
        def _(sp):
            sp.dma_start(gain[:, :], K.t["final_norm_g"].partition_broadcast(P)).then_inc(g_in, 16)
            out = K.t["out"].rearrange("(t p) d -> t p d", p=P)
            for half in range(NT):
                sp.wait_ge(scaled, half + 1)
                sp.dma_start(out[half], y[:, half, :]).then_inc(out_done, 16)
            sp.wait_ge(out_done, 16 * NT)

        @block.scalar
        def _(act):
            for half in range(NT):
                act.activation(y[:, half, :], K.x[:, half, :], ACT.Square,
                               accum_out=K.stat[:, half:half + 1]).then_inc(squared, 1)
            act.wait_ge(squared, NT)
            act.activation(K.stat[:, 2:4], K.stat[:, 0:2], ACT.Ln, bias=K.eps[:, 0:1], scale=1.0 / D).then_inc(steps, 1)
            act.wait_ge(steps, 1)
            act.activation(K.stat[:, 4:6], K.stat[:, 2:4], ACT.Exp, scale=-0.5).then_inc(steps, 1)

        @block.vector
        def _(dve):
            dve.wait_ge(g_in, 16)
            dve.wait_ge(steps, 2)
            for half in range(NT):
                dve.scalar_tensor_tensor(out=y[:, half, :], in0=K.x[:, half, :], scalar=K.stat[:, 4 + half:5 + half],
                                         in1=gain[:, :], op0=ALU.mult, op1=ALU.mult).then_inc(scaled, 1)


def rotary_table_stage(K, cs):
    nc = K.nc
    pos_in, steps, done = K.sem("positions_landed"), K.sem("rotary_steps"), K.sem("rotary_done")
    with ExitStack() as st:
        pos_i = K.sb("pos_i", [P, NT], I32, ctx=st)
        pos = K.sb("pos", [P, NT], ctx=st)
        ang = K.sb("ang", [P, 2, NT, ROT_HALF], ctx=st)
        turns = K.sb("turns", [P, 2, NT, ROT_HALF], ctx=st)
        block = st.enter_context(nc.Block())
        flat_a = ang[:, :, :, :].rearrange("p c t f -> p (c t f)")
        flat_n = turns[:, :, :, :].rearrange("p c t f -> p (c t f)")

        @block.sync
        def _(sp):
            sp.dma_start(pos_i[:, :], K.t["positions"]).then_inc(pos_in, 16)

        @block.vector
        def _(dve):
            n = [0]

            def step(ins):
                n[0] += 1
                ins.then_inc(steps, 1)
                dve.wait_ge(steps, n[0])

            dve.wait_ge(pos_in, 16)
            step(dve.tensor_copy(pos[:, :], pos_i[:, :]))
            for half in range(NT):
                step(dve.tensor_scalar(ang[:, 1, half, :], K.con_("inv_freq", ROT_HALF), pos[:, half:half + 1], None,
                                       ALU.mult))
            step(dve.tensor_copy(ang[:, 0, :, :], ang[:, 1, :, :]))
            big = 1.5 * 2.0 ** 23
            step(dve.tensor_scalar(turns[:, 1, :, :], ang[:, 1, :, :], 1.0 / (2 * math.pi), None, ALU.mult))
            step(dve.tensor_scalar(turns[:, 0, :, :], ang[:, 0, :, :], 1.0 / (2 * math.pi), 0.25, ALU.mult, ALU.add))
            step(dve.tensor_scalar(flat_n, flat_n, big, None, ALU.add))
            step(dve.tensor_scalar(flat_n, flat_n, big, None, ALU.subtract))
            c1 = 6.28125
            c2 = float(np.float32(math.floor((2 * math.pi - c1) * 2 ** 20) / 2 ** 20))
            for c in (c1, c2, 2 * math.pi - c1 - c2):
                step(dve.scalar_tensor_tensor(out=flat_a, in0=flat_n, scalar=-c, in1=flat_a, op0=ALU.mult, op1=ALU.add))
            step(dve.tensor_scalar(ang[:, 0, :, :], ang[:, 0, :, :], math.pi / 2, None, ALU.add))
            dve.tensor_scalar(flat_a, flat_a, 3.14159, -3.14159, ALU.min, ALU.max).then_inc(done, 1)

        @block.scalar
        def _(act):
            act.wait_ge(done, 1)
            act.activation(cs[:, :, :, :].rearrange("p c t f -> p (c t f)"), flat_a, ACT.Sin).then_inc(done, 1)
            act.preload_act_table_set("natural_log_exp_and_others")


def attention_stage(K, no, layer_a, lam_init, hi, lo, cs):
    nc = K.nc
    K.begin(no, 8)
    SC = A_HD ** -0.5
    roped = K.sig("a_roped", 2)
    qk_t = K.sig("a_qk_turned", 2)
    qk_t_out = K.sig("a_qk_turned_out", 2)
    scored = K.sig("a_scored", 1)
    maxed = K.sig("a_maxed", 1)
    expd = K.sig("a_exp", 1)
    mixed = K.sig("a_mixed", 1)
    mixed_t = K.sig("a_mixed_turned", 1)
    mixed_t_out = K.sig("a_mixed_turned_out", 1)
    attended = K.sig("a_attended", 1)
    rstd_done = K.sig("a_rstd", 1)
    gated = K.sig("a_gated", 1)
    out_t = K.sig("a_out_turned", 1)
    out_hi, out_lo = K.sig("a_out_hi", 1), K.sig("a_out_lo", 1)
    z_held, z_exp = K.sig("a_z_held", 1), K.sig("a_z_exp", 1)
    act_steps = K.sig("a_act_steps", 12)
    dve_steps = K.sig("a_dve_steps", 40)
    lam_in, lam_steps = K.sem(f"lambda_landed{layer_a}"), K.sem(f"lambda_steps{layer_a}")
    with ExitStack() as st:
        def sb(name, shape, dt=F32):
            return K.sb(name, shape, dt, ctx=st)
        q, k_, v, z = (sb(n, [P, NT, NC]) for n in ("a_q", "a_k", "a_v", "a_z"))
        ez = sb("a_ez", [P, NT, NC])
        rot = sb("a_rot", [P, 4, NT, A_HC, ROT_HALF])
        q_t, k_t = sb("a_qt", [P, A_HC, SEQ]), sb("a_kt", [P, A_HC, SEQ])
        s = sb("a_s", [P, A_HC, 3 * P])
        mx, sums, coef = (sb(n, [P, 2 * A_HC]) for n in ("a_mx", "a_sums", "a_coef"))
        m_t = sb("a_mt", [P, 2, 3 * P])
        o = sb("a_o", [P, NT, NC])
        ss = sb("a_ss", [P, 4])
        rs = sb("a_rs", [P, 4])
        o_hi, o_lo = sb("a_ohi", [P, CK, SEQ], F32R), sb("a_olo", [P, CK, SEQ], F32R)
        lam = sb("a_lam", [P, 4, A_HD])
        lv = sb("a_lv", [P, 8])
        sg = sb("a_sg", [P, 2])
        block = st.enter_context(nc.Block())
        bank = [K.psum[:, 4 + i, :] for i in range(4)]

        @block.sync
        def _(sp):
            sp.dma_start(lam[:, :, :].rearrange("p a d -> p (a d)"), K.t["a_lam"][layer_a].partition_broadcast(P)).then_inc(lam_in, 16)
            K.stream(sp, K.turns)

        @block.scalar
        def _(act):
            act.wait_ge(lam_steps, 4)
            act.activation(lv[:, 2:4], lv[:, 0:2], ACT.Exp).then_inc(lam_steps, 1)

            def turn(g):
                def step(ins):
                    act.wait_ge(act_steps.sem, act_steps.count(g, act_steps.inc(ins)))

                for t, dst in enumerate((q, k_, v)):
                    for k in range(4 * t + 1, 4 * t + 5):
                        K.split_act(act, g, k)
                    K.acc_wait(act, g, 4 * t + 3)
                    act.activation(dst[:, :, :], K.acc2(t), ACT.Copy).then_inc(K.acc_free.sem, 1)
                for n, dst in enumerate((q_t, k_t)):
                    act.wait_ge(qk_t.sem, qk_t.count(g, n + 1))
                    qk_t_out.inc(act.activation(dst[:, :, :], K.psum[:, 4 + 2 * n:6 + 2 * n, :], ACT.Copy))
                for k in (13, 14, 15):
                    K.split_act(act, g, k)
                act.wait_ge(maxed.sem, maxed.count(g, 1))
                for hc in range(A_HC):
                    for qt in range(NT):
                        c = slice(0, P) if qt == 0 else slice(P, 3 * P)
                        i = 2 * hc + qt
                        ins = act.activation(s[:, hc, c], s[:, hc, c], ACT.Exp, bias=mx[:, i:i + 1], scale=SC,
                                             accum_out=sums[:, i:i + 1])
                        if i < 2 * A_HC - 1:
                            act_steps.inc(ins)
                        else:
                            expd.inc(ins)
                K.split_act(act, g, 16)
                K.acc_wait(act, g, 15)
                act.activation(z[:, :, :], K.acc2(3), ACT.Copy).then_inc(K.acc_free.sem, 1)
                act.wait_ge(z_held.sem, z_held.count(g, 1))
                z_exp.inc(act.activation(ez[:, :, :], ez[:, :, :], ACT.Exp, scale=-1.0))
                act.wait_ge(attended.sem, attended.count(g, 1))
                for h in range(2):
                    for qt in range(NT):
                        i = 2 * h + qt
                        src = bank[2 + h][:, qt * A_VD:(qt + 1) * A_VD]
                        ins = act.activation(o[:, qt, h * A_VD:(h + 1) * A_VD], src, ACT.Square,
                                             accum_out=ss[:, i:i + 1])
                        act_steps.inc(ins)
                act.wait_ge(act_steps.sem, act_steps.count(g, act_steps.n))
                step(act.activation(rs[:, :], ss[:, :], ACT.Ln, bias=K.eps[:, 1:2], scale=1.0 / A_VD))
                rstd_done.inc(act.activation(rs[:, :], rs[:, :], ACT.Exp, scale=-0.5))
                act.wait_ge(out_t.sem, out_t.count(g, 1))
                for kt in range(CK):
                    ins = act.activation(o_hi[:, kt, :], bank[kt // 2][:, kt % 2 * SEQ:(kt % 2 + 1) * SEQ], ACT.Copy,
                                         scale=sg[:, kt % 2:kt % 2 + 1])
                out_hi.inc(ins)
                for k in (17, 18, 19, 20):
                    K.split_act(act, g, k)

            K.loop(act, turn)

        @block.vector
        def _(dve):
            n = [0]

            def first_step(ins):
                n[0] += 1
                ins.then_inc(lam_steps, 1)
                dve.wait_ge(lam_steps, n[0])

            dve.wait_ge(lam_in, 16)
            first_step(dve.tensor_tensor(lam[:, 0, :], lam[:, 0, :], lam[:, 1, :], ALU.mult))
            first_step(dve.tensor_tensor(lam[:, 2, :], lam[:, 2, :], lam[:, 3, :], ALU.mult))
            first_step(dve.tensor_reduce(lv[:, 0:1], lam[:, 0, :], AX.X, ALU.add))
            first_step(dve.tensor_reduce(lv[:, 1:2], lam[:, 2, :], AX.X, ALU.add))
            dve.wait_ge(lam_steps, 5)
            n[0] = 5
            first_step(dve.tensor_tensor(lv[:, 4:5], lv[:, 3:4], lv[:, 2:3], ALU.subtract))
            first_step(dve.tensor_scalar(lv[:, 5:6], lv[:, 4:5], -lam_init, None, ALU.add))
            first_step(dve.tensor_scalar(sg[:, :], K.col("subln_g", 2 * layer_a, 2), 1.0 - lam_init, None, ALU.mult))
            first_step(dve.memset(m_t[:, :, :], 0.0))

            def turn(g):
                def step(ins):
                    dve.wait_ge(dve_steps.sem, dve_steps.count(g, dve_steps.inc(ins)))

                def split(*ks):
                    for k in ks:
                        K.split_dve(dve, g, k)

                cos = [cs[:, 0, half, :].unsqueeze(1).broadcast_to([P, A_HC, ROT_HALF]) for half in range(NT)]
                sin = [cs[:, 1, half, :].unsqueeze(1).broadcast_to([P, A_HC, ROT_HALF]) for half in range(NT)]
                for t, src in enumerate((q, k_)):
                    split(*range(4 * t + 1, 4 * t + 5))
                    K.acc_was_read(dve, g, t)
                    for half in range(NT):
                        m = src[:, half, :].rearrange("p (a d) -> p a d", a=A_HC)
                        t1, t2 = m[:, :, 0:ROT_HALF], m[:, :, ROT_HALF:2 * ROT_HALF]
                        for i, (a, b) in enumerate(((t1, cos), (t2, sin), (t2, cos), (t1, sin))):
                            ins = dve.tensor_tensor(rot[:, i, half, :, :], a, b[half], ALU.mult)
                            if i < 3:
                                dve_steps.inc(ins)
                            else:
                                step(ins)
                        step(dve.tensor_tensor(t1, rot[:, 0, half, :, :], rot[:, 1, half, :, :], ALU.subtract))
                        ins = dve.tensor_tensor(t2, rot[:, 2, half, :, :], rot[:, 3, half, :, :], ALU.add)
                        if half == 0:
                            step(ins)
                    roped.inc(ins)
                split(9, 10, 11, 12, 13, 14)
                dve.wait_ge(scored.sem, scored.count(g, 1))
                for hc in range(A_HC):
                    step(dve.tensor_tensor(s[:, hc, :], bank[hc][:, 0:3 * P], K.con_("negmask", 3 * P), ALU.add))
                mxv = mx[:, :].rearrange("p (a t) -> p a t", t=NT)
                step(dve.tensor_reduce(mxv[:, :, 0], s[:, :, 0:P], AX.X, ALU.max))
                step(dve.tensor_reduce(mxv[:, :, 1], s[:, :, P:3 * P], AX.X, ALU.max))
                maxed.inc(dve.tensor_scalar(mx[:, :], mx[:, :], -SC, None, ALU.mult))
                split(15, 16)
                dve.wait_ge(expd.sem, expd.count(g, 1))
                step(dve.reciprocal(coef[:, :], sums[:, :]))
                cv = coef[:, :].rearrange("p (h c t) -> p h c t", h=2, c=2)
                step(dve.tensor_scalar(cv[:, :, 1, :], cv[:, :, 1, :], lv[:, 5:6], None, ALU.mult))
                for h in range(2):
                    for qt in range(NT):
                        c = slice(0, P) if qt == 0 else slice(P, 3 * P)
                        i = 4 * h + qt
                        step(dve.tensor_scalar(s[:, 2 * h, c], s[:, 2 * h, c], coef[:, i:i + 1], None, ALU.mult))
                        ins = dve.scalar_tensor_tensor(out=s[:, 2 * h, c], in0=s[:, 2 * h + 1, c],
                                                       scalar=coef[:, i + 2:i + 3], in1=s[:, 2 * h, c],
                                                       op0=ALU.mult, op1=ALU.add)
                        if i < 5:
                            step(ins)
                mixed.inc(ins)
                K.acc_was_read(dve, g, 3)
                z_held.inc(dve.tensor_scalar(ez[:, :, :], z[:, :, :], -LIMIT, None, ALU.max))
                dve.wait_ge(z_exp.sem, z_exp.count(g, 1))
                step(dve.tensor_scalar(ez[:, :, :], ez[:, :, :], 1.0, None, ALU.add))
                step(dve.reciprocal(ez[:, :, :], ez[:, :, :]))
                dve.wait_ge(mixed_t.sem, mixed_t.count(g, 1))
                mixed_t_out.inc(dve.tensor_copy(m_t[:, :, :], K.psum[:, 4:6, 0:3 * P]))
                step(dve.tensor_tensor(z[:, :, :], z[:, :, :], ez[:, :, :], ALU.mult))
                dve.wait_ge(rstd_done.sem, rstd_done.count(g, 1))
                for h in range(2):
                    for qt in range(NT):
                        i = 2 * h + qt
                        c = slice(h * A_VD, (h + 1) * A_VD)
                        ins = dve.scalar_tensor_tensor(out=o[:, qt, c], in0=bank[2 + h][:, qt * A_VD:(qt + 1) * A_VD],
                                                       scalar=rs[:, i:i + 1], in1=z[:, qt, c], op0=ALU.mult,
                                                       op1=ALU.mult)
                gated.inc(ins)
                dve.wait_ge(out_hi.sem, out_hi.count(g, 1))
                for kt in range(CK):
                    ins = dve.scalar_tensor_tensor(out=o_lo[:, kt, :], in0=bank[kt // 2][:, kt % 2 * SEQ:(kt % 2 + 1) * SEQ],
                                                   scalar=sg[:, kt % 2:kt % 2 + 1], in1=o_hi[:, kt, :].bitcast(F32),
                                                   op0=ALU.mult, op1=ALU.subtract)
                out_lo.inc(ins)
                for t in range(4):
                    split(17 + t)
                    K.acc_wait(dve, g, 16 + t)
                    xs = K.x[:, :, t * NC:(t + 1) * NC]
                    dve.tensor_tensor(xs, K.acc2(4 + t), xs, ALU.add).then_inc(K.acc_free.sem, 1)

            K.loop(dve, turn)

        @block.tensor
        def _(pe):
            ident = K.con_("ident", P)

            def turn(g):
                def project(k, t):
                    K.product(pe, g, k, t, hi, lo, range(k % 4 * 4, k % 4 * 4 + 4), first=k % 4 == 0, last=k % 4 == 3)

                for t in range(3):
                    K.acc_open(pe, g, t)
                    for c in range(4):
                        project(4 * t + c, t)
                for n, src in enumerate((q, k_)):
                    pe.wait_ge(roped.sem, roped.count(g, n + 1))
                    for hc in range(A_HC):
                        for half in range(NT):
                            c = hc % 2 * SEQ + half * P
                            mm = pe.transpose(bank[2 * n + hc // 2][:, c:c + P], src[:, half, hc * P:(hc + 1) * P], ident)
                    qk_t.inc(mm)
                K.acc_open(pe, g, 3)
                project(12, 3)
                project(13, 3)
                pe.wait_ge(qk_t_out.sem, qk_t_out.count(g, 2))
                for hc in range(A_HC):
                    pe.matmul(bank[hc][:, 0:P], q_t[:, hc, 0:P], k_t[:, hc, 0:P], start=True, stop=True)
                    mm = pe.matmul(bank[hc][:, P:3 * P], q_t[:, hc, P:SEQ], k_t[:, hc, :], start=True, stop=True)
                scored.inc(mm)
                project(14, 3)
                project(15, 3)
                pe.wait_ge(mixed.sem, mixed.count(g, 1))
                for h in range(2):
                    for b in range(3):
                        mm = pe.transpose(bank[h][:, b * P:(b + 1) * P], s[:, 2 * h, b * P:(b + 1) * P], ident)
                mixed_t.inc(mm)
                pe.wait_ge(mixed_t_out.sem, mixed_t_out.count(g, 1))
                for h in range(2):
                    vh = slice(h * A_VD, (h + 1) * A_VD)
                    pe.matmul(bank[2 + h][:, 0:A_VD], m_t[:, h, 0:P], v[:, 0, vh], start=True, stop=True)
                    pe.matmul(bank[2 + h][:, A_VD:2 * A_VD], m_t[:, h, P:2 * P], v[:, 0, vh], start=True, stop=False)
                    mm = pe.matmul(bank[2 + h][:, A_VD:2 * A_VD], m_t[:, h, 2 * P:3 * P], v[:, 1, vh], start=False,
                                   stop=True)
                attended.inc(mm)
                pe.wait_ge(gated.sem, gated.count(g, 1))
                for kt in range(CK):
                    for half in range(NT):
                        c = kt % 2 * SEQ + half * P
                        mm = pe.transpose(bank[kt // 2][:, c:c + P], o[:, half, kt * P:(kt + 1) * P], ident)
                out_t.inc(mm)
                pe.wait_ge(out_lo.sem, out_lo.count(g, 1))
                for t in range(4):
                    K.acc_open(pe, g, 4 + t)
                    K.product(pe, g, 16 + t, 4 + t, o_hi, o_lo, range(CK))

            K.loop(pe, turn)
    K.end()


def plan_rwkv(t):
    w = t["b_w_rkvg"]

    def lora(k, g):
        if k % 2 == 0:
            w1 = t[("b_w_w1", "b_w_a1")[k // 2]][0].rearrange("(k p) n -> p k n", p=P)
            return lambda slot: (slot[:, 0:KT * B_LORA].rearrange("p (k n) -> p k n", k=KT), w1)
        w2 = t[("b_w_w2", "b_w_a2")[k // 2]][0]
        return lambda slot: (slot[0:B_LORA, :], w2)

    def rkvg(k, g):
        rows = w[0].rearrange("c k n -> (c k) n")
        return dma_parts(rows, g * KT + k % 4 * 4, 4, k // 4 * NC)

    return [(4, 1, lora), (16, 4, rkvg), (4, B_GROUPS, lambda k, g: dma_parts(t["b_w_out"][0], g * CK, CK, k * NC))]


def rows_of(scratch, c, c0):
    return scratch[bass.ds(c * SEQ, SEQ), bass.ds(c0, NC)].rearrange("(t p) d -> p t d", p=P)


def rwkv_lora_stage(K, no, h, xx, scratch):
    nc = K.nc
    K.begin(no, 10)
    mixed, mixed_hi, mixed_lo = K.sig("bl_mixed", 2), K.sig("bl_hi", 2), K.sig("bl_lo", 2)
    in_hi, in_lo = K.sig("bl_inner_hi", 2), K.sig("bl_inner_lo", 2)
    bias_in, tile_done = K.sig("bl_bias_landed", 32), K.sig("bl_tile_done", 6)
    held, expd = K.sig("bl_held", 8), K.sig("bl_exp", 8)
    ready, stored = K.sig("bl_ready", 8), [K.sig(f"bl_stored{i}", 4 * 16) for i in range(2)]
    act_steps, dve_steps = K.sig("bl_act_steps", 2), K.sig("bl_dve_steps", 2 + 8)
    with ExitStack() as st:
        def sb(name, shape, dt=F32):
            return K.sb(name, shape, dt, ctx=st)
        xc = sb("bl_xc", [P, KT, SEQ])
        hi, lo = sb("bl_xhi", [P, KT, SEQ], F32R), sb("bl_xlo", [P, KT, SEQ], F32R)
        u = sb("bl_u", [P, 2, SEQ])
        u_hi, u_lo = sb("bl_uhi", [P, 2, SEQ], F32R), sb("bl_ulo", [P, 2, SEQ], F32R)
        y = sb("bl_y", [P, 2, NT, NC])
        bias = sb("bl_bias", [P, 2, D])
        block = st.enter_context(nc.Block())

        @block.sync
        def _(sp):
            for n, name in enumerate(("b_w0", "b_a0")):
                bias_in.inc(sp.dma_start(bias[:, n, :], K.t[name][0].partition_broadcast(P)), 16)
            K.stream(sp)

        @block.gpsimd
        def _(pool):
            tp = Turn(pool, 0, None)
            for n in range(8):
                tp.wait(ready, n + 1)
                stored[n % 2].inc(pool.dma_start(rows_of(scratch, 4 + n // 4, n % 4 * NC), y[:, n % 2, :, :]), 16)
            for s in stored:
                tp.wait(s, 4 * 16)

        @block.scalar
        def _(act):
            ta = Turn(act, 0, act_steps)
            for n in range(2):
                if n == 1:
                    K.acc_wait(act, 0, 0)
                ta.wait(mixed, n + 1)
                mixed_hi.inc(act.activation(hi[:, :, :], xc[:, :, :], ACT.Copy))
                K.split_act(act, 0, 2 * n + 1)
                K.acc_wait(act, 0, 2 * n)
                ta.step(act.activation(u[0:B_LORA, n, :], K.acc(5 * n, 0)[0:B_LORA, 0:SEQ],
                                       ACT.Tanh if n == 0 else ACT.Copy))
                in_hi.inc(act.activation(u_hi[0:B_LORA, n, :], u[0:B_LORA, n, :], ACT.Copy))
                if n == 0:
                    act.preload_act_table_set("natural_log_exp_and_others")
                K.split_act(act, 0, 2 * n + 2)
                for m in range(4):
                    i = 4 * n + m
                    ta.wait(held, i + 1)
                    expd.inc(act.activation(y[:, i % 2, :, :], y[:, i % 2, :, :], ACT.Exp, scale=-1.0))

        @block.vector
        def _(dve):
            td = Turn(dve, 0, dve_steps)
            td.step(dve.tensor_tensor(xx[:, :, 1:SEQ], h[:, :, 0:SEQ - 1], h[:, :, 1:SEQ], ALU.subtract))
            td.step(dve.tensor_scalar(xx[:, :, 0:1], h[:, :, 0:1], -1.0, None, ALU.mult))
            for n, c in enumerate((1, 4)):
                if n == 1:
                    td.wait(mixed_lo, 1)
                for kt in range(KT):
                    ins = dve.scalar_tensor_tensor(out=xc[:, kt, :], in0=xx[:, kt, :],
                                                   scalar=K.col("mu", c * KT + kt), in1=h[:, kt, :],
                                                   op0=ALU.mult, op1=ALU.add)
                mixed.inc(ins)
                td.wait(mixed_hi, n + 1)
                td.wait(mixed, n + 1)
                mixed_lo.inc(dve.tensor_tensor(lo[:, :, :], xc[:, :, :], hi[:, :, :].bitcast(F32), ALU.subtract))
                K.split_dve(dve, 0, 2 * n + 1)
                td.wait(in_hi, n + 1)
                in_lo.inc(dve.tensor_tensor(u_lo[0:B_LORA, n, :], u[0:B_LORA, n, :],
                                            u_hi[0:B_LORA, n, :].bitcast(F32), ALU.subtract))
                dve.memset(K.stat[:, 7:8], 0.0).then_inc(K.acc_free.sem, 1)
                K.split_dve(dve, 0, 2 * n + 2)
                if n == 0:
                    td.wait(bias_in, 32)
                for m in range(4):
                    i = 4 * n + m
                    yi = y[:, i % 2, :, :]
                    if m < 3:
                        td.wait(tile_done, 3 * n + m + 1)
                    else:
                        K.acc_wait(dve, 0, 2 * n + 1)
                    if i >= 2:
                        td.wait(stored[i % 2], 16 * (i // 2))
                    row = bias[:, n, m * NC:(m + 1) * NC].unsqueeze(1).broadcast_to([P, NT, NC])
                    dve.tensor_tensor(yi, K.acc2(5 * n + 1 + m), row, ALU.add).then_inc(K.acc_free.sem, 1)
                    K.acc_was_read(dve, 0, 5 * n + 1 + m)
                    held.inc(dve.tensor_scalar(yi, yi, -LIMIT, None, ALU.max))
                    td.wait(expd, i + 1)
                    td.step(dve.tensor_scalar(yi, yi, 1.0, None, ALU.add))
                    ready.inc(dve.reciprocal(yi, yi))

        @block.tensor
        def _(pe):
            tt = Turn(pe, 0, None)
            for n in range(2):
                k, s = 2 * n, (K.pos + 2 * n) % SPLIT
                tt.wait(mixed_lo, n + 1)
                K.acc_open(pe, 0, 5 * n)
                pe.wait_ge(K.split_lo.sem, K.index(0, k) + 1)
                o = K.acc(5 * n, 0)[0:B_LORA, 0:SEQ]
                for kt in range(KT):
                    c = slice(kt * B_LORA, (kt + 1) * B_LORA)
                    pe.matmul(o, K.whi[:, s, c], hi[:, kt, :], start=kt == 0, stop=False)
                    pe.matmul(o, K.wlo[:, s, c], hi[:, kt, :], start=False, stop=False)
                    mm = pe.matmul(o, K.whi[:, s, c], lo[:, kt, :], start=False, stop=kt == KT - 1)
                mm.then_inc(K.used.sem, 1)
                tt.wait(in_lo, n + 1)
                for m in range(4):
                    K.acc_open(pe, 0, 5 * n + 1 + m)
                    mm = K.product(pe, 0, k + 1, 5 * n + 1 + m, u_hi, u_lo, (n,), rows=B_LORA, at=m * NC,
                                   release=m == 3)
                    if m < 3:
                        tile_done.inc(mm)
    K.end()


def rwkv_rkvg_stage(K, no, h, xx, scratch):
    nc = K.nc
    K.begin(no, 4)
    Q = 4
    mixed, mixed_hi, mixed_lo = K.sig("bp_mixed", Q), K.sig("bp_hi", Q), K.sig("bp_lo", Q)
    copied, stored = K.sig("bp_copied", 4), K.sig("bp_stored", 4 * 16)
    with ExitStack() as st:
        xc = K.sb("bp_xc", [P, KT, SEQ], ctx=st)
        hi, lo = K.sb("bp_xhi", [P, KT, SEQ], F32R, ctx=st), K.sb("bp_xlo", [P, KT, SEQ], F32R, ctx=st)
        y = K.sb("bp_y", [P, 4, NT, NC], ctx=st)
        mu = K.sb("bp_mu", [P, 4 * KT], ctx=st)
        mu_set = K.sem("bp_mu_set")
        block = st.enter_context(nc.Block())

        @block.sync
        def _(sp):
            K.stream(sp, K.turns)

        @block.gpsimd
        def _(pool):
            def turn(g):
                tp = Turn(pool, g, None)
                for m in range(4):
                    tp.wait(copied, m + 1)
                    stored.inc(pool.dma_start(rows_of(scratch, g, m * NC), y[:, m, :, :]), 16)
                tp.wait(stored, 4 * 16)

            K.loop(pool, turn)

        @block.scalar
        def _(act):
            def turn(g):
                ta = Turn(act, g, None)
                for i in range(Q):
                    ta.wait(mixed, i + 1)
                    c = slice(4 * i, 4 * i + 4)
                    mixed_hi.inc(act.activation(hi[:, c, :], xc[:, c, :], ACT.Copy))
                for m in range(4):
                    for k in range(4 * m + 1, 4 * m + 5):
                        K.split_act(act, g, k)
                    K.acc_wait(act, g, 4 * m + 3)
                    ta.wait(stored, 0)
                    copied.inc(act.activation(y[:, m, :, :], K.acc2(m), ACT.Copy))

            K.loop(act, turn)

        @block.vector
        def _(dve):
            for i, c in enumerate((0, 2, 3, 5)):
                dve.tensor_copy(mu[:, i * KT:(i + 1) * KT], K.col("mu", c * KT, KT)).then_inc(mu_set, 1)
            dve.wait_ge(mu_set, 4)

            def turn(g):
                td = Turn(dve, g, None)
                for i in range(Q):
                    for kt in range(4 * i, 4 * i + 4):
                        ins = dve.scalar_tensor_tensor(out=xc[:, kt, :], in0=xx[:, kt, :],
                                                       scalar=mu[:, bass.ds(g * KT + kt, 1)], in1=h[:, kt, :],
                                                       op0=ALU.mult, op1=ALU.add)
                    mixed.inc(ins)
                for i in range(Q):
                    td.wait(mixed_hi, i + 1)
                    c = slice(4 * i, 4 * i + 4)
                    mixed_lo.inc(dve.tensor_tensor(lo[:, c, :], xc[:, c, :], hi[:, c, :].bitcast(F32), ALU.subtract))
                for m in range(4):
                    for k in range(4 * m + 1, 4 * m + 5):
                        K.split_dve(dve, g, k)
                    td.wait(copied, m + 1)
                    dve.memset(K.stat[:, 7:8], 0.0).then_inc(K.acc_free.sem, 1)

            K.loop(dve, turn)

        @block.tensor
        def _(pe):
            def turn(g):
                tt = Turn(pe, g, None)
                for m in range(4):
                    K.acc_open(pe, g, m)
                    for c in range(4):
                        if m == 0:
                            tt.wait(mixed_lo, c + 1)
                        K.product(pe, g, 4 * m + c, m, hi, lo, range(4 * c, 4 * c + 4), first=c == 0, last=c == 3)

            K.loop(pe, turn)
    K.end()


def rwkv_heads_stage(K, no, scratch):
    nc = K.nc
    K.begin(no, 4)
    NH, NPAIR, HALVES = 8, 4, 2

    def sig(name, per=1):
        return K.sig("bh_" + name, per)
    loaded, params = sig("loaded", 6 * 16), sig("params", 5 * 16)
    kk_raw, kk_sq, kk_ss, kk_rn = sig("kk_raw"), sig("kk_sq"), sig("kk_ss"), sig("kk_rn")
    cum, exps = sig("cum"), sig("exps", 3)
    arrays = sig("arrays", 4)
    turned, turned_a, turned_v = sig("turned", 2), sig("turned_a"), sig("turned_v")
    sums, masked = sig("products", 16), sig("masked", 16)
    inv_pe, inv_dve = sig("inv_pe", HALVES * 2 * 13), sig("inv_dve", HALVES * 2 * 13)
    rhs, rhs_out, sa, sa_out = sig("rhs", 4), sig("rhs_out", 4), sig("sa", 4), sig("sa_out", 4)
    decay, decay_out, state, state_out = sig("decay"), sig("decay_out"), sig("state", 2), sig("state_out", 2)
    o_done, o_out = sig("o", 4), sig("o_out", 4)
    cen, cen_sq, var, gn = sig("centred"), sig("centred_sq"), sig("variance"), sig("gn_rstd")
    g_held, g_exp, gated = sig("g_held"), sig("g_exp"), sig("gated")
    out_t, out_hi, out_lo = sig("out_turned"), sig("out_hi"), sig("out_lo")
    act_steps, dve_steps = sig("act_steps", 3), sig("dve_steps", 26)
    zeroed = K.sem("bh_zeroed")
    with ExitStack() as st:
        def sb(name, shape, dt=F32):
            return K.sb("bh_" + name, shape, dt, ctx=st)
        ld = sb("ld", [P, 6, NT, NC])
        r, k_, v, g_in, w, a = (ld[:, i, :, :] for i in range(6))
        pr = sb("params", [P, 5, NC])
        kk, t1, t2 = (sb(n, [P, NT, NC]) for n in ("kk", "t1", "t2"))
        o = kk
        stat = sb("stat", [P, 4, 2 * NH])
        arr = sb("arr", [P, NT, 4, NC])
        tr = sb("tr", [P, NPAIR, NT, 4, P])
        gm = sb("gm", [P, 8, 4 * P])
        ym = sb("ym", [P, 8, P])
        tm, xm = (a_[:, :, :].rearrange("p t (m c) -> p (t m) c", c=P) for a_ in (t1, t2))
        rh, nsa = sb("rh", [P, NT, 4, B_HD]), sb("nsa", [P, NT, 4, B_HD])
        sblk = sb("sblk", [P, NPAIR, P])
        dec = sb("dec", [P, NPAIR])
        o_hi, o_lo = sb("ohi", [P, CK, SEQ], F32R), sb("olo", [P, CK, SEQ], F32R)
        aside = sb("aside", [P, 16])
        block = st.enter_context(nc.Block())
        bank = [K.psum[:, i, :] for i in range(8)]
        ident = K.con_("ident", P)

        def bc(row):
            return row.unsqueeze(1).broadcast_to([P, NT, NC])

        def heads(ap):
            return ap.rearrange("p t (h c) -> p (t h) c", c=B_HD)

        def per_head(col):
            return col.unsqueeze(2).broadcast_to([P, 2 * NH, B_HD])

        @block.sync
        def _(sp):
            def turn(g):
                tp = Turn(sp, g, None)
                tp.wait(gated, 0)
                for i, c in ((1, 1), (5, 5), (4, 4), (0, 0), (2, 2), (3, 3)):
                    loaded.inc(sp.dma_start(ld[:, i, :, :], rows_of(scratch, c, g * NC)), 16)
                    if i == 1:
                        for n, name in enumerate(("b_k_k", "b_k_a", "b_r_k", "b_ln_w", "b_ln_b")):
                            params.inc(sp.dma_start(pr[:, n, :], K.t[name][0][bass.ds(g * NC, NC)].partition_broadcast(P)), 16)
                for k in range(RAW, 2 * RAW):
                    if isinstance(g, int):
                        src = K.following(k - RAW)
                        if src is not None:
                            K.load(sp, g, k, src)
                    else:
                        K.load(sp, g, k, K.source(k - RAW, g + 1))

            with sp.Fori(0, K.turns - 1) as g:
                turn(g)
            for s in (loaded, params):
                s.n = 0
            turn(K.turns - 1)

        @block.scalar
        def _(act):
            def turn(g):
                ta = Turn(act, g, act_steps)
                ta.wait(kk_raw)
                kk_sq.inc(act.activation(t1[:, :, :], kk[:, :, :], ACT.Square))
                ta.wait(kk_ss)
                ta.step(act.activation(stat[:, 0, :], stat[:, 0, :], ACT.Ln, bias=K.eps[:, 0:1]))
                kk_rn.inc(act.activation(stat[:, 0, :], stat[:, 0, :], ACT.Exp, scale=-0.5))
                ta.wait(cum)
                for n, (b, s) in enumerate(((4, -B_C), (6, -B_C), (6, B_C))):
                    exps.inc(act.activation(arr[:, :, n, :], K.psum[:, b:b + 2, :], ACT.Exp, scale=s))
                ta.wait(turned, 1)
                turned_a.inc(act.activation(tr[:, 0:2, :, :, :], K.psum[:, 0:4, :], ACT.Copy))
                ta.wait(decay)
                decay_out.inc(act.activation(dec[:, :], bank[7][:, 0:NPAIR], ACT.Exp, scale=-B_C))
                for hf in range(HALVES):
                    for tt in range(NT):
                        n = 2 * hf + tt + 1
                        ta.wait(rhs, n)
                        rhs_out.inc(act.activation(rh[:, tt, :, :], bank[6 + tt][:, 0:4 * B_HD], ACT.Copy))
                        ta.wait(sa, n)
                        sa_out.inc(act.activation(nsa[:, tt, :, :], bank[0 + 3 * tt][:, 0:4 * B_HD], ACT.Copy, scale=-1.0))
                        if tt == 0:
                            ta.wait(state, hf + 1)
                            for p in range(2):
                                for u in range(2):
                                    rows, c = slice(64 * u, 64 * u + 64), slice(64 * u, 64 * u + 64)
                                    ins = act.activation(sblk[rows, 2 * hf + p, c],
                                                         bank[2][rows, p * P + 64 * u:p * P + 64 * u + 64], ACT.Copy,
                                                         scale=dec[rows, 2 * hf + p:2 * hf + p + 1])
                            state_out.inc(ins)
                        ta.wait(o_done, n)
                        o_out.inc(act.activation(o[:, tt, hf * SEQ:(hf + 1) * SEQ], bank[1 + 3 * tt][:, 0:4 * B_HD],
                                                 ACT.Copy))
                ta.wait(cen)
                cen_sq.inc(act.activation(t1[:, :, :], o[:, :, :], ACT.Square))
                ta.wait(g_held)
                g_exp.inc(act.activation(t2[:, :, :], t2[:, :, :], ACT.Exp, scale=-1.0))
                ta.wait(var)
                ta.step(act.activation(stat[:, 2, :], stat[:, 2, :], ACT.Ln, bias=K.eps[:, 2:3], scale=1.0 / B_HD))
                gn.inc(act.activation(stat[:, 2, :], stat[:, 2, :], ACT.Exp, scale=-0.5))
                ta.wait(out_t)
                ta.step(act.activation(o_hi[:, 0:2, :], bank[4], ACT.Copy))
                out_hi.inc(act.activation(o_hi[:, 2:4, :], bank[5], ACT.Copy))
                for k in (1, 2, 3, 4):
                    K.split_act(act, g, k)

            K.loop(act, turn)

        @block.vector
        def _(dve):
            dve.memset(gm[:, :, :], 0.0).then_inc(zeroed, 1)
            dve.memset(sblk[:, :, :], 0.0).then_inc(zeroed, 1)
            dve.wait_ge(zeroed, 2)
            mask = K.con_("mask4", 4 * P).bitcast(I32)
            eye4 = ident.unsqueeze(1).broadcast_to([P, 4, P])

            def level(n, name="levels"):
                return K.con[:, CON[name] + n * P:CON[name] + (n + 1) * P].unsqueeze(1).broadcast_to([P, 4, P])

            def turn(g):
                td = Turn(dve, g, dve_steps)
                td.wait(loaded, 6 * 16)
                td.wait(params, 5 * 16)
                kk_raw.inc(dve.tensor_tensor(kk[:, :, :], k_, bc(pr[:, 0, :]), ALU.mult))
                td.step(dve.scalar_tensor_tensor(out=t2[:, :, :], in0=a, scalar=1.0, in1=bc(pr[:, 1, :]),
                                                 op0=ALU.subtract, op1=ALU.mult))
                td.step(dve.scalar_tensor_tensor(out=k_, in0=t2[:, :, :], scalar=1.0, in1=k_, op0=ALU.add, op1=ALU.mult))
                td.wait(kk_sq)
                kk_ss.inc(dve.tensor_reduce(stat[:, 0, :], heads(t1[:, :, :]), AX.X, ALU.add))
                td.step(dve.tensor_tensor(t2[:, :, :], r, k_, ALU.mult))
                td.step(dve.tensor_tensor(t2[:, :, :], t2[:, :, :], bc(pr[:, 2, :]), ALU.mult))
                td.step(dve.tensor_reduce(stat[:, 1, :], heads(t2[:, :, :]), AX.X, ALU.add))
                td.wait(kk_rn)
                td.step(dve.tensor_tensor(heads(kk[:, :, :]), heads(kk[:, :, :]), per_head(stat[:, 0, :]), ALU.mult))
                td.step(dve.tensor_tensor(t1[:, :, :], kk[:, :, :], a, ALU.mult))
                td.wait(exps, 3)
                for n, (dst, e, src) in enumerate(((3, 2, k_), (2, 2, t1[:, :, :]), (0, 0, kk[:, :, :]), (1, 1, r))):
                    ins = dve.tensor_tensor(arr[:, :, dst, :], arr[:, :, e, :], src, ALU.mult)
                    arrays.inc(ins)
                td.wait(turned, 2)
                turned_v.inc(dve.tensor_copy(tr[:, 2:4, :, :, :], K.psum[:, 4:8, :]))
                for hf in range(HALVES):
                    for i in range(8):
                        td.wait(sums, 8 * hf + i + 1)
                        dve.memset(aside[:, 8 * hf + i:8 * hf + i + 1], 0.0)
                        masked.inc(dve.copy_predicated(gm[:, i, :], mask, bank[i]))
                    for b in range(2):
                        q = slice(4 * b, 4 * b + 4)
                        base = 26 * hf
                        td.wait(inv_pe, base + b + 1)
                        td.step(dve.scalar_tensor_tensor(out=xm[:, q, :], in0=bank[3 * b], scalar=-1.0, in1=level(0),
                                                         op0=ALU.mult, op1=ALU.mult))
                        td.step(dve.scalar_tensor_tensor(out=ym[:, q, :], in0=gm[:, q, 0:P], scalar=-1.0,
                                                         in1=level(0, "level1_t"), op0=ALU.mult, op1=ALU.mult))
                        dve.tensor_tensor(xm[:, q, :], xm[:, q, :], eye4, ALU.add)
                        inv_dve.inc(dve.tensor_tensor(ym[:, q, :], ym[:, q, :], eye4, ALU.add))
                    for lv in range(1, 7):
                        for b in range(2):
                            q = slice(4 * b, 4 * b + 4)
                            td.wait(inv_pe, base + 4 * lv - 2 + b + 1)
                            inv_dve.inc(dve.tensor_tensor(tm[:, q, :], bank[3 * b], level(lv), ALU.mult))
                        for b in range(2):
                            q = slice(4 * b, 4 * b + 4)
                            td.wait(inv_pe, base + 4 * lv + b + 1)
                            if lv < 6:
                                dve.tensor_tensor(xm[:, q, :], xm[:, q, :], bank[3 * b + 1], ALU.subtract)
                            inv_dve.inc(dve.tensor_tensor(ym[:, q, :], ym[:, q, :], bank[3 * b + 2], ALU.subtract))
                td.wait(o_out, 4)
                td.step(dve.tensor_reduce(stat[:, 3, :], heads(o[:, :, :]), AX.X, ALU.add))
                td.step(dve.tensor_scalar(stat[:, 3, :], stat[:, 3, :], 1.0 / B_HD, None, ALU.mult))
                cen.inc(dve.tensor_tensor(heads(o[:, :, :]), heads(o[:, :, :]), per_head(stat[:, 3, :]), ALU.subtract))
                g_held.inc(dve.tensor_scalar(t2[:, :, :], g_in, -LIMIT, None, ALU.max))
                td.wait(cen_sq)
                var.inc(dve.tensor_reduce(stat[:, 2, :], heads(t1[:, :, :]), AX.X, ALU.add))
                td.wait(g_exp)
                td.step(dve.tensor_scalar(t2[:, :, :], t2[:, :, :], 1.0, None, ALU.add))
                td.step(dve.reciprocal(t2[:, :, :], t2[:, :, :]))
                td.step(dve.tensor_tensor(t2[:, :, :], t2[:, :, :], g_in, ALU.mult))
                td.step(dve.tensor_tensor(heads(t1[:, :, :]), heads(v), per_head(stat[:, 1, :]), ALU.mult))
                td.step(dve.tensor_tensor(t1[:, :, :], t1[:, :, :], bc(pr[:, 4, :]), ALU.add))
                td.wait(gn)
                td.step(dve.tensor_tensor(heads(o[:, :, :]), heads(o[:, :, :]), per_head(stat[:, 2, :]), ALU.mult))
                td.step(dve.tensor_tensor(o[:, :, :], o[:, :, :], bc(pr[:, 3, :]), ALU.mult))
                td.step(dve.tensor_tensor(o[:, :, :], o[:, :, :], t1[:, :, :], ALU.add))
                gated.inc(dve.tensor_tensor(o[:, :, :], o[:, :, :], t2[:, :, :], ALU.mult))
                td.wait(out_hi)
                td.step(dve.tensor_tensor(o_lo[:, 0:2, :], bank[4], o_hi[:, 0:2, :].bitcast(F32), ALU.subtract))
                out_lo.inc(dve.tensor_tensor(o_lo[:, 2:4, :], bank[5], o_hi[:, 2:4, :].bitcast(F32), ALU.subtract))
                for t in range(4):
                    K.split_dve(dve, g, 1 + t)
                    K.acc_wait(dve, g, t)
                    xs = K.x[:, :, t * NC:(t + 1) * NC]
                    dve.tensor_tensor(xs, K.acc2(t), xs, ALU.add).then_inc(K.acc_free.sem, 1)

            K.loop(dve, turn)

        @block.tensor
        def _(pe):
            def turn(g):
                tt_ = Turn(pe, g, None)
                K.acc_open(pe, g, 0)
                K.acc_open(pe, g, 1)
                tt_.wait(loaded, 6 * 16)
                for half in range(NT):
                    pe.matmul(bank[4 + half], K.con_("tri_excl_mid", P), w[:, half, :], start=True, stop=True)
                    mm = pe.matmul(bank[6 + half], K.con_("tri_incl_mid", P), w[:, half, :], start=True, stop=True)
                cum.inc(mm)
                tt_.wait(arrays, 4)
                for p in range(NPAIR):
                    for half in range(NT):
                        for i in range(4):
                            mm = pe.transpose(bank[2 * p + half][:, i * P:(i + 1) * P],
                                              arr[:, half, i, p * P:(p + 1) * P], ident)
                    if p % 2 == 1:
                        turned.inc(mm)
                tt_.wait(turned_v)
                for p in range(NPAIR):
                    pe.matmul(bank[7][:, p:p + 1], w[:, 0, p * P:(p + 1) * P], K.con_("second_half", 1),
                              start=p == 0, stop=False, skip_group_check=True)
                    mm = pe.matmul(bank[7][:, p:p + 1], w[:, 1, p * P:(p + 1) * P], K.con_("first_half", 1),
                                   start=False, stop=True, skip_group_check=True)
                decay.inc(mm)
                tt_.wait(turned_a)
                tt_.wait(decay_out)
                for hf in range(HALVES):
                    for i in range(8):
                        half, hh = i // 4, i % 4
                        p, rows = 2 * hf + hh // 2, slice(64 * (hh % 2), 64 * (hh % 2) + 64)
                        if hf == 1 and i == 0:
                            tt_.wait(o_out, 2)
                        both = tr[rows, p, half, 0:2, :]
                        pe.matmul(bank[i][:, 0:2 * P], tr[rows, p, half, 2, :], both, start=True, stop=True)
                        sums.inc(pe.matmul(bank[i][:, 2 * P:4 * P], tr[rows, p, half, 3, :], both, start=True, stop=True))
                    base, mbase = 26 * hf, 8 * hf
                    for b in range(2):
                        tt_.wait(masked, mbase + 8)
                        for j in range(4):
                            mm = pe.matmul(bank[3 * b][:, j * P:(j + 1) * P], gm[:, 4 * b + j, 0:P], ident,
                                           start=True, stop=True)
                        inv_pe.inc(mm)
                    for lv in range(1, 7):
                        for b in range(2):
                            tt_.wait(inv_dve, base + 4 * (lv - 1) + b + 1)
                            for j in range(4):
                                mm = pe.matmul(bank[3 * b][:, j * P:(j + 1) * P], gm[:, 4 * b + j, 0:P],
                                               xm[:, 4 * b + j, :], start=True, stop=True)
                            inv_pe.inc(mm)
                        for b in range(2):
                            tt_.wait(inv_dve, base + 4 * lv - 2 + b + 1)
                            for j in range(4):
                                c = slice(j * P, (j + 1) * P)
                                if lv < 6:
                                    pe.matmul(bank[3 * b + 1][:, c], ym[:, 4 * b + j, :], tm[:, 4 * b + j, :],
                                              start=True, stop=True)
                                mm = pe.matmul(bank[3 * b + 2][:, c], tm[:, 4 * b + j, :], ym[:, 4 * b + j, :],
                                               start=True, stop=True)
                            inv_pe.inc(mm)
                    for half in range(NT):
                        n = 2 * hf + half + 1
                        i0 = 4 * half
                        tt_.wait(inv_dve, base + 26)
                        for j in range(4):
                            ch = slice((4 * hf + j) * B_HD, (4 * hf + j + 1) * B_HD)
                            mm = pe.matmul(bank[6 + half][:, j * B_HD:(j + 1) * B_HD], gm[:, i0 + j, 2 * P:3 * P],
                                           v[:, half, ch], start=j == 0, stop=half == 0, skip_group_check=True)
                        if half == 1:
                            tt_.wait(state_out, hf + 1)
                            for p in range(2):
                                mm = pe.matmul(bank[7][:, p * P:(p + 1) * P], tr[:, 2 * hf + p, 1, 0, :],
                                               sblk[:, 2 * hf + p, :], start=False, stop=True, skip_group_check=True)
                        rhs.inc(mm)
                        tt_.wait(rhs_out, n)
                        for j in range(4):
                            mm = pe.matmul(bank[3 * half][:, j * B_HD:(j + 1) * B_HD], ym[:, i0 + j, :],
                                           rh[:, half, j, :], start=True, stop=True)
                        sa.inc(mm)
                        tt_.wait(sa_out, n)
                        if half == 0:
                            for p in range(2):
                                ch = slice((2 * hf + p) * P, (2 * hf + p + 1) * P)
                                o_ = bank[2][:, p * P:(p + 1) * P]
                                pe.matmul(o_, arr[:, 0, 3, ch], v[:, 0, ch], start=True, stop=False)
                                mm = pe.matmul(o_, arr[:, 0, 2, ch], nsa[:, 0, 2 * p:2 * p + 2, :], start=False, stop=True)
                            state.inc(mm)
                        for j in range(4):
                            ch = slice((4 * hf + j) * B_HD, (4 * hf + j + 1) * B_HD)
                            o_ = bank[1 + 3 * half][:, j * B_HD:(j + 1) * B_HD]
                            pe.matmul(o_, gm[:, i0 + j, P:2 * P], nsa[:, half, j, :], start=j == 0, stop=False,
                                      skip_group_check=True)
                            mm = pe.matmul(o_, gm[:, i0 + j, 3 * P:4 * P], v[:, half, ch], start=False, stop=half == 0,
                                           skip_group_check=True)
                        if half == 1:
                            for p in range(2):
                                mm = pe.matmul(bank[4][:, p * P:(p + 1) * P], tr[:, 2 * hf + p, 1, 1, :],
                                               sblk[:, 2 * hf + p, :], start=False, stop=True, skip_group_check=True)
                        o_done.inc(mm)
                tt_.wait(gated)
                for kt in range(CK):
                    for half in range(NT):
                        c = kt % 2 * SEQ + half * P
                        mm = pe.transpose(bank[4 + kt // 2][:, c:c + P], o[:, half, kt * P:(kt + 1) * P], ident)
                out_t.inc(mm)
                tt_.wait(out_lo)
                for t in range(4):
                    if t >= 2:
                        K.acc_open(pe, g, t)
                    K.product(pe, g, t, t, o_hi, o_lo, range(CK))

            K.loop(pe, turn)
    K.end()


def rwkv(K, no, layer, st):
    scratch = K.nc.dram_tensor("rwkv_rows", (6 * SEQ, D), F32).ap()
    with ExitStack() as hs:
        h, xx = K.sb("h", [P, KT, SEQ], ctx=hs), K.sb("xx", [P, KT, SEQ], ctx=hs)
        norm_stage(K, None, ("norm_g", layer * KT), None, None, plain=h)
        rwkv_lora_stage(K, no, h, xx, scratch)
        rwkv_rkvg_stage(K, no + 1, h, xx, scratch)
    rwkv_heads_stage(K, no + 2, scratch)
    return no + 3


def plan_deltanet(t):
    w, wo = t["c_w_in"][0], t["c_w_out"][0]

    def gates(k, g):
        src = w[:, 2 * C_QK + 2 * C_VW:2 * C_QK + 2 * C_VW + 2 * C_VH].rearrange("(k p) n -> p k n", p=P)
        return lambda slot: (slot[:, 0:KT * 2 * C_VH].rearrange("p (k n) -> p k n", k=KT), src)

    def source(k, g):
        if k < 24:
            tile, k0 = k // 4, k % 4 * 4
            start = (0, C_QK, 2 * C_QK, 2 * C_QK + NC, 2 * C_QK + C_VW, 2 * C_QK + C_VW + NC)[tile]
            return dma_parts(w, k0, 4, g * (NC if tile < 2 else 2 * NC) + start)
        k -= 24
        return dma_parts(wo, g * 2 * CK + k // 4 * CK, CK, k % 4 * NC)

    return [(1, 1, gates), (32, C_GROUPS, source)]


def deltanet_gates_stage(K, no, hi, lo, G):
    nc = K.nc
    K.begin(no, 1)
    H = C_VH
    rows_in = K.sig("cg_rows", 32)
    d1, a1, d2, a2, d3 = (K.sig("cg_" + n, 1) for n in ("held", "exp", "plus_one", "log", "g"))
    cum, cum_out, e_out = K.sig("cg_cum", 1), K.sig("cg_cum_out", 1), K.sig("cg_e", 1)
    dve_steps, act_steps = K.sig("cg_dve_steps", 5), K.sig("cg_act_steps", 1)
    with ExitStack() as st:
        ab = K.sb("cg_ab", [P, NT, 2 * H], ctx=st)
        e = K.sb("cg_e", [P, NT, 2 * H], ctx=st)
        rows = K.sb("cg_rows", [P, 2, H], ctx=st)
        block = st.enter_context(nc.Block())

        def bc(row):
            return row.unsqueeze(1).broadcast_to([P, NT, H])

        @block.sync
        def _(sp):
            for n, name in enumerate(("c_A_log", "c_dt_bias")):
                rows_in.inc(sp.dma_start(rows[:, n, :], K.t[name][0].partition_broadcast(P)), 16)
            K.stream(sp)

        @block.scalar
        def _(act):
            ta = Turn(act, 0, act_steps)
            K.split_act(act, 0, 1)
            ta.wait(rows_in, 32)
            ta.step(act.activation(rows[:, 0, :], rows[:, 0, :], ACT.Exp))
            ta.wait(d1)
            a1.inc(act.activation(e[:, :, :], e[:, :, :], ACT.Exp, scale=-1.0))
            ta.wait(d2)
            a2.inc(act.activation(e[:, :, H:2 * H], e[:, :, H:2 * H], ACT.Ln))
            ta.wait(cum)
            cum_out.inc(act.activation(G["gc"][:, :, :], K.psum[:, 4, 0:NT * H], ACT.Copy))
            e_out.inc(act.activation(G["egc"][:, :, :], K.psum[:, 4, 0:NT * H], ACT.Exp))

        @block.vector
        def _(dve):
            td = Turn(dve, 0, dve_steps)
            K.split_dve(dve, 0, 1)
            K.acc_wait(dve, 0, 0)
            td.wait(rows_in, 32)
            dve.tensor_copy(ab[:, :, :], K.acc2(0)[:, :, 0:2 * H]).then_inc(K.acc_free.sem, 1)
            K.acc_was_read(dve, 0, 0)
            a_, b_ = ab[:, :, H:2 * H], ab[:, :, 0:H]
            ea = e[:, :, H:2 * H]
            td.step(dve.tensor_tensor(a_, a_, bc(rows[:, 1, :]), ALU.add))
            td.step(dve.scalar_tensor_tensor(out=ea, in0=a_, scalar=-1.0, in1=a_, op0=ALU.mult, op1=ALU.max))
            d1.inc(dve.tensor_scalar(e[:, :, 0:H], b_, -LIMIT, None, ALU.max))
            td.wait(a1)
            d2.inc(dve.tensor_scalar(e[:, :, :], e[:, :, :], 1.0, None, ALU.add))
            td.wait(d2)
            dve.reciprocal(G["beta"][:, :, :], e[:, :, 0:H])
            td.wait(a2)
            td.step(dve.scalar_tensor_tensor(out=ea, in0=a_, scalar=0.0, in1=ea, op0=ALU.max, op1=ALU.add))
            d3.inc(dve.scalar_tensor_tensor(out=G["g"][:, :, :], in0=ea, scalar=-1.0, in1=bc(rows[:, 0, :]), op0=ALU.mult,
                                            op1=ALU.mult))
            td.wait(e_out)
            td.step(dve.tensor_scalar(G["negegc"][:, :, :], G["egc"][:, :, :], -1.0, None, ALU.mult))
            td.wait(cum_out)
            td.step(dve.memset(K.stat[:, 7:8], 0.0))

        @block.tensor
        def _(pe):
            tt = Turn(pe, 0, None)
            K.acc_open(pe, 0, 0)
            K.product(pe, 0, 0, 0, hi, lo, range(KT), cols=2 * H)
            tt.wait(d3)
            for half in range(NT):
                mm = pe.matmul(K.psum[:, 4, half * H:(half + 1) * H], K.con_("tri", P), G["g"][:, half, :], start=True,
                               stop=True)
            cum.inc(mm)
    K.end()


def deltanet_heads_stage(K, no, hi, lo, G):
    nc = K.nc
    K.begin(no, 14)
    QS = C_HD ** -0.5

    def sig(name, per=1):
        return K.sig("ch_" + name, per)
    conv, sigm, silu = sig("conv", 4), sig("sigmoid", 4), sig("silu", 4)
    squared, normsum, rnorm, qk_done = sig("squared", 2), sig("normsum", 2), sig("rnorm", 2), sig("qk_done", 2)
    k_turned, k_tok = sig("k_turned"), sig("k_tok")
    v_turned, v_tok = sig("v_turned", 2), sig("v_tok", 2)
    z_held, z_sig, z_done = sig("z_held", 2), sig("z_sigmoid", 2), sig("z_done", 2)
    kq, kq_out, rows, rows_out, dec = sig("kq", 4), sig("kq_out", 4), sig("rows", 4), sig("rows_out", 4), sig("decay", 4)
    n_done, g_spread = sig("n", 4), sig("g_spread", 2)
    inv_pe, inv_dve = sig("inv_pe", 2 * 26), sig("inv_dve", 2 * 26)
    u_, vnew = sig("u", 4), sig("vnew", 4)
    vs_, s_, s_out, o1 = sig("vs", 2), sig("state", 2), sig("state_out", 2), sig("o1", 4)
    o_out, ks, rhs = sig("o_out", 2), sig("ks", 2), sig("rhs", 2)
    o_full, o_sq, o_ss, o_rs, gated = sig("o_full", 2), sig("o_sq", 2), sig("o_ss", 2), sig("o_rstd", 2), sig("gated", 2)
    out_t, out_hi, out_lo = sig("out_turned", 2), sig("out_hi", 2), sig("out_lo", 2)
    act_steps, dve_steps = sig("act_steps", 18), sig("dve_steps", 74)
    FILL = {1: 0, 2: 1, 3: 2, 4: 3}
    with ExitStack() as st:
        def sb(name, shape, dt=F32):
            return K.sb("ch_" + name, shape, dt, ctx=st)
        q_t, k_t, v_t, e = (sb(n, [P, 4, SEQ]) for n in ("qt", "kt", "vt", "e"))
        v, z = sb("v", [P, NT, 2 * NC]), sb("z", [P, NT, 2 * NC])
        ktok = sb("ktok", [P, NC])
        kqm = sb("kqm", [P, NT, 2, 2 * P])
        dm, nm, pm, xm, ym, tm = (sb(n, [P, 8, P]) for n in ("d", "n", "p", "x", "y", "t"))
        rh, vn, vs, state = (sb(n, [P, 4, P]) for n in ("rhs", "vnew", "vs", "state"))
        o = sb("o", [P, NT, NC])
        stat = sb("stat", [P, 2 * 4])
        g_wide = tm[:, :, :]
        o_hi, o_lo = sb("ohi", [P, CK, SEQ], F32R), sb("olo", [P, CK, SEQ], F32R)
        block = st.enter_context(nc.Block())
        bank = [K.psum[:, 4 + i, :] for i in range(4)]
        ident = K.con_("ident", P)

        def ebuf():
            return e[:, :, :].rearrange("p a b -> p (a b)").rearrange("p (t c) -> p t c", t=NT)

        def gate(name, g, hf, half):
            return G[name][:, half, bass.ds(g * 8 + hf * 4, 4)]

        def per_head(col):
            return col.unsqueeze(2).broadcast_to([P, 4, P])

        def t1_bank(lv, b):
            return (0 if lv % 2 else 2) + b

        def xy_bank(lv, b):
            return ((2 if lv % 2 else 0) if b == 0 else (0 if lv % 2 else 2))

        @block.sync
        def _(sp):
            K.stream(sp, K.turns)

        @block.scalar
        def _(act):
            def turn(g):
                ta = Turn(act, g, act_steps)

                def split(*ks_):
                    for k in ks_:
                        K.split_act(act, g, k)

                def sigmoid(buf, mark):
                    ta.step(act.activation(buf, buf, ACT.Exp, scale=-1.0))
                    ta.step(act.activation(buf, buf, ACT.Ln, bias=K.eps[:, 3:4]))
                    mark.inc(act.activation(buf, buf, ACT.Exp, scale=-1.0))

                def after(t):
                    k = 4 * t + 4
                    split(k + 1, k + 2)
                    ta.wait(conv, t + 1)
                    sigmoid(e[:, :, :], sigm)
                    split(k + 3)
                    ta.wait(silu, t + 1)
                    if t < 2:
                        squared.inc(act.activation(e[:, :, :], (q_t, k_t)[t][:, :, :], ACT.Square))
                        ta.wait(normsum, t + 1)
                        ta.step(act.activation(ebuf(), K.psum[:, 4:6, :], ACT.Ln, bias=K.eps[:, 0:1]))
                        rnorm.inc(act.activation(e[:, :, :], e[:, :, :], ACT.Exp, scale=-0.5))
                    else:
                        ta.wait(v_turned, t - 1)
                        c = slice((t - 2) * NC, (t - 1) * NC)
                        v_tok.inc(act.activation(v[:, :, c], K.psum[:, 4:6, :], ACT.Copy))
                    split(k + 4)

                def z_copy(n):
                    K.acc_wait(act, g, 19 + 4 * n)
                    act.activation(z[:, :, n * NC:(n + 1) * NC], K.acc2(4 + n), ACT.Copy).then_inc(K.acc_free.sem, 1)

                def z_sigmoid(n):
                    ta.wait(z_held, n + 1)
                    sigmoid(ebuf(), z_sig)

                split(1, 2, 3, 4)
                for t in range(4):
                    after(t)
                ta.wait(k_turned)
                k_tok.inc(act.activation(ktok[:, :], bank[2], ACT.Copy))
                for hf in range(2):
                    for half in range(NT):
                        ta.wait(rows_out, 2 * hf + half + 1)
                        d = dm[:, 4 * half:4 * half + 4, :]
                        dec.inc(act.activation(d, d, ACT.Exp))
                    if hf == 0:
                        z_copy(0)
                        z_sigmoid(0)
                    for n in range(4):
                        split(21 + 4 * hf + n)
                    if hf == 0:
                        z_copy(1)
                    ta.wait(s_, hf + 1)
                    s_out.inc(act.activation(state[:, :, :], bank[2], ACT.Copy))
                    ta.wait(o1, 2 * hf + 1)
                    o_out.inc(act.activation(o[:, 0, :], bank[1], ACT.Copy))
                    if hf == 0:
                        z_sigmoid(1)
                    ta.wait(o_full, hf + 1)
                    o_sq.inc(act.activation(ebuf(), o[:, :, :], ACT.Square))
                    ta.wait(o_ss, hf + 1)
                    ta.step(act.activation(stat[:, :], stat[:, :], ACT.Ln, bias=K.eps[:, 0:1], scale=1.0 / C_HD))
                    o_rs.inc(act.activation(stat[:, :], stat[:, :], ACT.Exp, scale=-0.5))
                    ta.wait(out_t, hf + 1)
                    act_steps.inc(act.activation(o_hi[:, 0:2, :], bank[0], ACT.Copy, scale=K.col("c_norm_g", 0)))
                    out_hi.inc(act.activation(o_hi[:, 2:4, :], bank[1], ACT.Copy, scale=K.col("c_norm_g", 0)))
                for n in range(4):
                    split(29 + n)

            K.loop(act, turn)

        @block.vector
        def _(dve):
            mask2 = K.con_("mask4", 2 * P).unsqueeze(1).broadcast_to([P, 2, 2 * P])
            eye4 = ident.unsqueeze(1).broadcast_to([P, 4, P])

            def level(n, name="levels"):
                return K.con[:, CON[name] + n * P:CON[name] + (n + 1) * P].unsqueeze(1).broadcast_to([P, 4, P])

            def turn(g):
                td = Turn(dve, g, dve_steps)

                def split(*ks_):
                    for k in ks_:
                        K.split_dve(dve, g, k)

                def taps(t, dst, cts):
                    first = (0, 16, 32, 36)[t]
                    for ct in cts:
                        src = K.acc(t, ct // 2)[:, ct % 2 * SEQ:ct % 2 * SEQ + SEQ]
                        for j in range(C_TAPS - 1, -1, -1):
                            w = K.cols[:, bass.ds(g * (16 if t < 2 else 32) + (COL["conv"] + (first + ct) * C_TAPS + j), 1)]
                            lag = C_TAPS - 1 - j
                            if lag == 0:
                                ins = dve.tensor_scalar(dst[:, ct, :], src, w, None, ALU.mult)
                            else:
                                ins = dve.scalar_tensor_tensor(out=dst[:, ct, lag:SEQ], in0=src[:, 0:SEQ - lag], scalar=w,
                                                               in1=dst[:, ct, lag:SEQ], op0=ALU.mult, op1=ALU.add)
                            if ct == 3 and j == 0:
                                ins.then_inc(K.acc_free.sem, 1)
                                K.acc_was_read(dve, g, t)
                            else:
                                td.step(ins)

                def after(t):
                    k = 4 * t + 4
                    dst = (q_t, k_t, v_t, v_t)[t]
                    K.acc_wait(dve, g, 4 * t + 3)
                    if t == 3:
                        td.wait(v_turned, 1)
                    taps(t, dst, (0, 1))
                    split(k + 1)
                    taps(t, dst, (2, 3))
                    conv.inc(dve.tensor_scalar(e[:, :, :], dst[:, :, :], -LN_LIMIT, None, ALU.max))
                    split(k + 2)
                    td.wait(sigm, t + 1)
                    silu.inc(dve.tensor_tensor(dst[:, :, :], dst[:, :, :], e[:, :, :], ALU.mult))
                    split(k + 3)
                    if t < 2:
                        td.wait(rnorm, t + 1)
                        qk_done.inc(dve.scalar_tensor_tensor(out=dst[:, :, :], in0=dst[:, :, :], scalar=(QS, 1.0)[t],
                                                             in1=e[:, :, :], op0=ALU.mult, op1=ALU.mult))
                    split(k + 4)

                def z_hold(n):
                    K.acc_was_read(dve, g, 4 + n)
                    z_held.inc(dve.tensor_scalar(ebuf(), z[:, :, n * NC:(n + 1) * NC], -LN_LIMIT, None, ALU.max))

                def z_mult(n):
                    td.wait(z_sig, n + 1)
                    zt = z[:, :, n * NC:(n + 1) * NC]
                    z_done.inc(dve.tensor_tensor(zt, zt, ebuf(), ALU.mult))

                split(1, 2, 3, 4)
                for t in range(4):
                    after(t)
                for hf in range(2):
                    gh = G["g"][:, :, bass.ds(g * 8 + hf * 4, 4)].unsqueeze(3).broadcast_to([P, NT, 4, P])
                    g_spread.inc(dve.tensor_copy(g_wide.rearrange("p (t h) c -> p t h c", t=NT), gh))
                    for half in range(NT):
                        n = 2 * hf + half + 1
                        td.wait(kq, n)
                        kq_out.inc(dve.tensor_tensor(kqm[:, half, :, :], bank[half].rearrange("p (a b) -> p a b", a=2),
                                                     mask2, ALU.mult))
                        td.wait(rows, n)
                        for j in range(4):
                            i = 4 * half + j
                            ins = dve.tensor_scalar(dm[:, i, :], bank[2 + half][:, j * P:(j + 1) * P],
                                                    G["gc"][:, half, bass.ds(g * 8 + hf * 4 + j, 1)], 0.0,
                                                    ALU.subtract, ALU.min)
                        rows_out.inc(ins)
                    if hf == 0:
                        z_hold(0)
                    for half in range(NT):
                        n = 2 * hf + half + 1
                        td.wait(dec, n)
                        td.wait(kq_out, n)
                        for j in range(4):
                            i = 4 * half + j
                            dve.scalar_tensor_tensor(out=nm[:, i, :], in0=kqm[:, half, j // 2, 0:P],
                                                     scalar=G["beta"][:, half, bass.ds(g * 8 + hf * 4 + j, 1)],
                                                     in1=dm[:, i, :], op0=ALU.mult, op1=ALU.mult)
                        for kh in range(2):
                            i = 4 * half + 2 * kh
                            qk = kqm[:, half, kh, P:2 * P].unsqueeze(1).broadcast_to([P, 2, P])
                            ins = dve.tensor_tensor(pm[:, i:i + 2, :], dm[:, i:i + 2, :], qk, ALU.mult)
                        n_done.inc(ins)
                    if hf == 0:
                        z_mult(0)
                    base = 26 * hf
                    for b in range(2):
                        q = slice(4 * b, 4 * b + 4)
                        td.wait(inv_pe, base + b + 1)
                        td.wait(n_done, 2 * hf + b + 1)
                        td.step(dve.scalar_tensor_tensor(out=xm[:, q, :], in0=bank[t1_bank(0, b)], scalar=-1.0, in1=level(0),
                                                         op0=ALU.mult, op1=ALU.mult))
                        td.step(dve.scalar_tensor_tensor(out=ym[:, q, :], in0=nm[:, q, :], scalar=-1.0,
                                                         in1=level(0, "level1_t"), op0=ALU.mult, op1=ALU.mult))
                        dve.tensor_tensor(xm[:, q, :], xm[:, q, :], eye4, ALU.add)
                        inv_dve.inc(dve.tensor_tensor(ym[:, q, :], ym[:, q, :], eye4, ALU.add))
                    for lv in range(1, 7):
                        if lv in FILL:
                            split(21 + 4 * hf + FILL[lv])
                        for b in range(2):
                            q = slice(4 * b, 4 * b + 4)
                            td.wait(inv_pe, base + 4 * lv - 2 + b + 1)
                            inv_dve.inc(dve.tensor_tensor(tm[:, q, :], bank[t1_bank(lv, b)], level(lv), ALU.mult))
                        for b in range(2):
                            q = slice(4 * b, 4 * b + 4)
                            td.wait(inv_pe, base + 4 * lv + b + 1)
                            if lv < 6:
                                dve.tensor_tensor(xm[:, q, :], xm[:, q, :], bank[xy_bank(lv, b)], ALU.subtract)
                            inv_dve.inc(dve.tensor_tensor(ym[:, q, :], ym[:, q, :], bank[xy_bank(lv, b) + 1], ALU.subtract))
                        if hf == 1 and lv in FILL:
                            t = FILL[lv]
                            K.acc_wait(dve, g, 24 + t)
                            xs = K.x[:, :, t * NC:(t + 1) * NC]
                            dve.tensor_tensor(xs, K.acc2(6 + t), xs, ALU.add).then_inc(K.acc_free.sem, 1)
                    if hf == 0:
                        z_hold(1)
                    c4 = slice(hf * NC, (hf + 1) * NC)

                    def four(ap):
                        return ap.rearrange("p (h c) -> p h c", c=P)

                    td.wait(u_, 2 * hf + 1)
                    vnew.inc(dve.tensor_tensor(vn[:, :, :], four(bank[0]), per_head(gate("beta", g, hf, 0)), ALU.mult))
                    td.wait(vnew, 2 * hf + 1)
                    last = dm[:, 0:4, P - 1:P].broadcast_to([P, 4, P])
                    vs_.inc(dve.tensor_tensor(vs[:, :, :], vn[:, :, :], last, ALU.mult))
                    td.wait(ks, hf + 1)
                    td.step(dve.tensor_tensor(rh[:, :, :], four(bank[3]), per_head(gate("negegc", g, hf, 1)), ALU.mult))
                    rhs.inc(dve.tensor_tensor(rh[:, :, :], rh[:, :, :], four(v[:, 1, c4]), ALU.add))
                    td.step(dve.tensor_tensor(vs[:, :, :], four(bank[0]), per_head(gate("egc", g, hf, 1)), ALU.mult))
                    td.wait(u_, 2 * hf + 2)
                    vnew.inc(dve.tensor_tensor(vn[:, :, :], four(bank[1]), per_head(gate("beta", g, hf, 1)), ALU.mult))
                    if hf == 0:
                        z_mult(1)
                    td.wait(o1, 2 * hf + 2)
                    td.wait(o_out, hf + 1)
                    o_full.inc(dve.tensor_tensor(four(o[:, 1, :]), vs[:, :, :], four(bank[2]), ALU.add))
                    ov = o[:, :, :].rearrange("p t (h c) -> p (t h) c", c=P)
                    td.wait(o_sq, hf + 1)
                    o_ss.inc(dve.tensor_reduce(stat[:, :], ebuf().rearrange("p t (h c) -> p (t h) c", c=P), AX.X, ALU.add))
                    td.wait(o_rs, hf + 1)
                    td.step(dve.tensor_tensor(ov, ov, stat[:, :].unsqueeze(2).broadcast_to([P, 8, P]), ALU.mult))
                    gated.inc(dve.tensor_tensor(o[:, :, :], o[:, :, :], z[:, :, c4], ALU.mult))
                    td.wait(out_hi, hf + 1)
                    for i in range(2):
                        ins = dve.scalar_tensor_tensor(out=o_lo[:, 2 * i:2 * i + 2, :], in0=bank[i].rearrange("p (a b) -> p a b", a=2),
                                                       scalar=K.col("c_norm_g", 0),
                                                       in1=o_hi[:, 2 * i:2 * i + 2, :].bitcast(F32), op0=ALU.mult,
                                                       op1=ALU.subtract)
                    out_lo.inc(ins)
                for t in range(4):
                    split(29 + t)
                    K.acc_wait(dve, g, 28 + t)
                    xs = K.x[:, :, t * NC:(t + 1) * NC]
                    dve.tensor_tensor(xs, K.acc2(10 + t), xs, ALU.add).then_inc(K.acc_free.sem, 1)

            K.loop(dve, turn)

        @block.tensor
        def _(pe):
            def turn(g):
                tt = Turn(pe, g, None)

                def project(k, t):
                    f = K.product_t if t < 4 else K.product
                    f(pe, g, k, t, hi, lo, range(k % 4 * 4, k % 4 * 4 + 4), first=k % 4 == 0, last=k % 4 == 3)

                def after(t):
                    if t < 2:
                        tt.wait(squared, t + 1)
                        for i in range(2):
                            mm = pe.matmul(bank[i], K.con_("ones", P), e[:, 2 * i:2 * i + 2, :], start=True, stop=True)
                        normsum.inc(mm)
                    else:
                        tt.wait(silu, t + 1)
                        for half in range(NT):
                            for ct in range(4):
                                mm = pe.transpose(bank[half][:, ct * P:(ct + 1) * P], v_t[:, ct, half * P:(half + 1) * P],
                                                  ident)
                        v_turned.inc(mm)

                for t in range(5):
                    K.acc_open(pe, g, t)
                    for c in range(4):
                        if c == 3 and t > 0:
                            after(t - 1)
                        project(4 * t + c, t)
                tt.wait(qk_done, 2)
                for ct in range(4):
                    mm = pe.transpose(bank[2][:, ct * P:(ct + 1) * P], k_t[:, ct, 0:P], ident)
                k_turned.inc(mm)
                tt.wait(v_tok, 2)
                tt.wait(k_tok)
                for hf in range(2):
                    for half in range(NT):
                        tok = slice(half * P, (half + 1) * P)
                        for kh in range(2):
                            h = 2 * hf + kh
                            o_ = bank[half][:, kh * 2 * P:(kh + 1) * 2 * P]
                            pe.matmul(o_[:, 0:P], k_t[:, h, tok], k_t[:, h, tok], start=True, stop=True)
                            mm = pe.matmul(o_[:, P:2 * P], k_t[:, h, tok], q_t[:, h, tok], start=True, stop=True)
                        kq.inc(mm)
                        tt.wait(g_spread, hf + 1)
                        for j in range(4):
                            mm = pe.matmul(bank[2 + half][:, j * P:(j + 1) * P], g_wide[:, 4 * half + j, :], K.con_("tri", P),
                                           start=True, stop=True)
                        rows.inc(mm)
                    base = 26 * hf
                    for b in range(2):
                        tt.wait(n_done, 2 * hf + b + 1)
                        tt.wait(rows_out, 2 * hf + 2)
                        for j in range(4):
                            mm = pe.matmul(bank[t1_bank(0, b)][:, j * P:(j + 1) * P], nm[:, 4 * b + j, :], ident,
                                           start=True, stop=True)
                        inv_pe.inc(mm)
                    for lv in range(1, 7):
                        for b in range(2):
                            tt.wait(inv_dve, base + 4 * (lv - 1) + b + 1)
                            for j in range(4):
                                mm = pe.matmul(bank[t1_bank(lv, b)][:, j * P:(j + 1) * P], nm[:, 4 * b + j, :],
                                               xm[:, 4 * b + j, :], start=True, stop=True)
                            inv_pe.inc(mm)
                        if lv in FILL:
                            n = FILL[lv]
                            if hf == 0:
                                if n == 0:
                                    K.acc_open(pe, g, 5)
                                project(20 + n, 5)
                            else:
                                K.acc_open(pe, g, 6 + n)
                                K.product(pe, g, 24 + n, 6 + n, o_hi, o_lo, range(CK))
                        for b in range(2):
                            tt.wait(inv_dve, base + 4 * lv - 2 + b + 1)
                            for j in range(4):
                                c = slice(j * P, (j + 1) * P)
                                if lv < 6:
                                    pe.matmul(bank[xy_bank(lv, b)][:, c], ym[:, 4 * b + j, :], tm[:, 4 * b + j, :],
                                              start=True, stop=True)
                                mm = pe.matmul(bank[xy_bank(lv, b) + 1][:, c], tm[:, 4 * b + j, :], ym[:, 4 * b + j, :],
                                               start=True, stop=True)
                            inv_pe.inc(mm)
                    tt.wait(inv_dve, base + 26)
                    for j in range(4):
                        c = slice(j * P, (j + 1) * P)
                        mm = pe.matmul(bank[0][:, c], ym[:, j, :], v[:, 0, hf * NC + j * P:hf * NC + (j + 1) * P], start=True,
                                       stop=True)
                    u_.inc(mm)
                    tt.wait(vs_, hf + 1)
                    for j in range(4):
                        h = 2 * hf + j // 2
                        mm = pe.matmul(bank[2][:, j * P:(j + 1) * P], ktok[:, h * P:(h + 1) * P], vs[:, j, :], start=True,
                                       stop=True)
                    s_.inc(mm)
                    for j in range(4):
                        mm = pe.matmul(bank[1][:, j * P:(j + 1) * P], pm[:, j, :], vn[:, j, :], start=True, stop=True)
                    o1.inc(mm)
                    tt.wait(s_out, hf + 1)
                    for src, b in ((k_t, 3), (q_t, 0)):
                        for kh in range(2):
                            mm = pe.matmul(bank[b][:, kh * 2 * P:(kh + 1) * 2 * P], src[:, 2 * hf + kh, P:2 * P],
                                           state[:, 2 * kh:2 * kh + 2, :], start=True, stop=True)
                    ks.inc(mm)
                    tt.wait(rhs, hf + 1)
                    tt.wait(o_out, hf + 1)
                    for j in range(4):
                        mm = pe.matmul(bank[1][:, j * P:(j + 1) * P], ym[:, 4 + j, :], rh[:, j, :], start=True, stop=True)
                    u_.inc(mm)
                    tt.wait(vnew, 2 * hf + 2)
                    for j in range(4):
                        mm = pe.matmul(bank[2][:, j * P:(j + 1) * P], pm[:, 4 + j, :], vn[:, j, :], start=True, stop=True)
                    o1.inc(mm)
                    tt.wait(gated, hf + 1)
                    for kt in range(CK):
                        for half in range(NT):
                            c = kt % 2 * SEQ + half * P
                            mm = pe.transpose(bank[kt // 2][:, c:c + P], o[:, half, kt * P:(kt + 1) * P], ident)
                    out_t.inc(mm)
                    tt.wait(out_lo, hf + 1)
                for t in range(4):
                    K.acc_open(pe, g, 10 + t)
                    K.product(pe, g, 28 + t, 10 + t, o_hi, o_lo, range(CK))

            K.loop(pe, turn)
    K.end()


def deltanet(K, no, layer, st):
    hi, lo = K.sb("h_hi", [P, KT, SEQ], F32R, ctx=st), K.sb("h_lo", [P, KT, SEQ], F32R, ctx=st)
    G = {n: K.sb("c_" + n, [P, NT, C_VH], ctx=st) for n in ("beta", "g", "gc", "egc", "negegc")}
    norm_stage(K, None, ("norm_g", layer * KT), hi, lo)
    deltanet_gates_stage(K, no, hi, lo, G)
    deltanet_heads_stage(K, no + 1, hi, lo, G)
    return no + 2


def plan_attention(t, a):
    w, wo = t["a_w_in"][a], t["a_w_out"][a]

    def source(k, g):
        if k < 16:
            return dma_parts(w, k % 4 * 4, 4, k // 4 * D + g * NC)
        return dma_parts(wo, g * CK, CK, (k - 16) * NC)
    return (20, A_GROUPS, source)


def plan_embed(t, layer):
    return ((2, 1, lambda k, g: dma_parts(t["pe_w_proj"][layer], 0, 2, k * 2 * NC, 2 * NC)),
            (8, 2, lambda k, g: dma_parts(t["pe_w_gate"][layer], k % 4 * 4, 4, g * 2 * NC + k // 4 * NC)))


def trunk(nc, t, depth=DEPTH):
    with ExitStack() as ctx:
        K = Kernel(nc, ctx, t)
        K.plan = []
        for i in range(depth):
            if i % 3 == 0:
                K.plan.append(plan_attention(t, i // 3))
            elif i % 3 == 1:
                K.plan += plan_rwkv(t)
            else:
                K.plan += plan_deltanet(t)
            K.plan += plan_embed(t, i)
        cs = K.sb("cs", [P, 2, NT, ROT_HALF])
        start_stage(K)
        rotary_table_stage(K, cs)
        no = 0
        for i in range(depth):
            j = i // 3
            with ExitStack() as st:
                if i % 3 == 0:
                    hi, lo = K.sb("h_hi", [P, KT, SEQ], F32R, ctx=st), K.sb("h_lo", [P, KT, SEQ], F32R, ctx=st)
                    norm_stage(K, None, ("norm_g", i * KT), hi, lo)
                    attention_stage(K, no, j, 0.8 - 0.6 * math.exp(-0.3 * i), hi, lo, cs)
                    no += 1
                elif i % 3 == 1:
                    no = rwkv(K, no, i, st)
                else:
                    no = deltanet(K, no, i, st)
            with ExitStack() as st:
                hi, lo = K.sb("h_hi", [P, KT, SEQ], F32R, ctx=st), K.sb("h_lo", [P, KT, SEQ], F32R, ctx=st)
                pp = K.sb("pp", [P, NT, D], ctx=st)
                norm_stage(K, no, ("pe_norm_g", i * KT), hi, lo, embed=(i, pp))
                gate_stage(K, no + 1, hi, lo, pp)
                no += 2
        final_stage(K)


OUT = (1, SEQ, D)
WHOLE = ["pe_w_gate", "pe_w_proj", "final_norm_g", "a_w_in", "a_w_out", "b_w_rkvg", "b_w_w1", "b_w_w2", "b_w_a1",
         "b_w_a2", "b_w_out", "c_w_in", "c_w_out", "b_w0", "b_a0", "b_k_k", "b_k_a", "b_ln_w", "b_ln_b", "c_A_log",
         "c_dt_bias"]


def lay_out(inputs):
    a = {n: np.ascontiguousarray(inputs[n]) for n in WHOLE}
    a["x"] = np.ascontiguousarray(inputs["x"]).reshape(SEQ, D)
    a["p_t"] = np.ascontiguousarray(np.asarray(inputs["p"]).reshape(DEPTH, SEQ, PLE).transpose(0, 2, 1))
    a["positions"] = np.ascontiguousarray(np.asarray(inputs["positions"]).reshape(NT, P).T)
    a["a_lam"] = np.ascontiguousarray(inputs["a_lam"]).reshape(2, 4 * A_HD)
    a["b_r_k"] = np.ascontiguousarray(inputs["b_r_k"]).reshape(1, D)

    def per_partition(name):
        v = np.asarray(inputs[name])
        return v.reshape(-1, P).T

    conv = np.asarray(inputs["c_conv_w"]).reshape(C_TAPS, 64, P).transpose(2, 1, 0).reshape(P, 64 * C_TAPS)
    parts = [per_partition(n) for n in ("norm_g", "pe_norm_g", "b_mu", "a_subln_g", "c_norm_g")] + [conv]
    a["cols"] = np.ascontiguousarray(np.concatenate(parts, 1))
    a["con"] = constants()
    return a


def build(nc, arrays, depth=DEPTH):
    t = {n: nc.dram_tensor(f"in_{n}", a.shape, mybir.dt.from_np(a.dtype), kind="ExternalInput").ap() for n, a in arrays.items()}
    t["out"] = nc.dram_tensor("out", (SEQ, D), F32, kind="ExternalOutput").ap()
    trunk(nc, t, depth)


def kernel(**inputs):
    import concourse.bacc as bacc
    from concourse.bass_utils import run_bass_kernel_spmd

    nc = bacc.Bacc("TRN2", target_bir_lowering=False, num_devices=1)
    arrays = lay_out(inputs)
    build(nc, arrays)
    r = run_bass_kernel_spmd(nc, [{f"in_{n}": a for n, a in arrays.items()}], core_ids=[0])
    return r.results[0]["out"].reshape(OUT)
```

```python
from contextlib import ExitStack
import math

import numpy as np
import concourse.bass as bass
from concourse import mybir

F32 = mybir.dt.float32
F32R = mybir.dt.float32r
I32 = mybir.dt.int32
ALU = mybir.AluOpType
ACT = mybir.ActivationFunctionType
AX = mybir.AxisListType

P = 128
D = 2048
SEQ = 256
NT = SEQ // P
KT = D // P
NC = 512
CK = 4
CHUNK = CK * NC
RAW = 4
SPLIT = 2
HALF = CHUNK // 2
DEPTH = 4
PLE = 256
EPS = 1e-6
LN_LIMIT = 44.0
LIMIT = 85.0

A_HD = 128
A_GROUPS = 4
A_HC = 4
A_VD = 256
A_SUBLN_EPS = 1e-5
ROT_HALF = 16
ROPE_THETA = 500000.0

B_HD = 64
B_LORA = 96
B_GN_EPS = 64e-5
B_C = math.exp(-0.5)
B_GROUPS = 4

C_HD = 128
C_GROUPS = 4
C_VH = 32
C_QK = 2048
C_VW = 4096
C_TAPS = 4

COL = {}
_at = 0
for _name, _n in (("norm_g", DEPTH * KT), ("pe_norm_g", DEPTH * KT), ("mu", 6 * KT), ("subln_g", 2 * 2),
                  ("c_norm_g", 1), ("conv", 64 * C_TAPS)):
    COL[_name] = _at
    _at += _n
NCOLS = _at

CON = {}
_at = 0
for _name, _n in (("ident", P), ("tri", P), ("tri_incl_mid", P), ("tri_excl_mid", P), ("ones", P), ("mask4", 4 * P),
                  ("negmask", 3 * P), ("level1_t", P), ("levels", 7 * P), ("first_half", 1), ("second_half", 1),
                  ("inv_freq", ROT_HALF)):
    CON[_name] = _at
    _at += _n
NCONS = _at


def constants():
    c = np.zeros((P, NCONS), np.float32)
    i, j = np.arange(P)[:, None], np.arange(P)[None, :]

    def put(name, a):
        c[:, CON[name]:CON[name] + a.shape[1]] = a

    put("ident", i == j)
    put("tri", i <= j)
    mid = (i < P // 2).astype(np.float32)
    put("tri_incl_mid", (i <= j) - mid)
    put("tri_excl_mid", (i < j) - mid)
    put("ones", np.ones((P, P)))
    put("mask4", np.concatenate([i < j, i <= j, i < j, i <= j], 1))
    neg = np.where(j <= i, 0.0, -1e30)
    put("negmask", np.concatenate([neg, np.zeros((P, P)), neg], 1))
    levels = []
    for n in range(7):
        m = 1 << n
        levels.append((i // (2 * m) == j // (2 * m)) & (i // m % 2 == 1) & (j // m % 2 == 0))
    put("levels", np.concatenate(levels, 1))
    put("level1_t", levels[0].T)
    put("first_half", i < P // 2)
    put("second_half", i >= P // 2)
    f = (np.float32(ROPE_THETA) ** (-np.arange(0, 2 * ROT_HALF, 2, dtype=np.float32) / np.float32(2 * ROT_HALF)))
    put("inv_freq", np.broadcast_to(f.astype(np.float32), (P, ROT_HALF)))
    return c


SHARED = ("act_steps", "dve_steps", "out_turned", "out_hi", "out_lo", "gated", "inv_pe", "inv_dve")


class Signal:

    def __init__(self, sem):
        self.sem, self.base, self.per, self.n = sem, 0, 0, 0

    def count(self, turn, n):
        return self.base + self.per * turn + n

    def inc(self, ins, k=1):
        ins.then_inc(self.sem, k)
        self.n += k
        return self.n


class Kernel:
    def __init__(self, nc, ctx, t):
        self.nc, self.ctx, self.t = nc, ctx, t
        self.signals = {}
        self.names = 0
        self.stage = []
        self.pos = 0
        self.tiles = 0
        sb = self.sb
        self.x = sb("x", [P, NT, D])
        self.raw = sb("raw", [P, RAW, CHUNK])
        self.whi = sb("whi", [P, SPLIT, CHUNK], F32R)
        self.wlo = sb("wlo", [P, SPLIT, CHUNK], F32R)
        self.con = sb("con", [P, NCONS])
        self.cols = sb("cols", [P, NCOLS])
        self.eps = sb("eps", [P, 4])
        self.stat = sb("stat", [P, 8])
        self.psum = ctx.enter_context(nc.psum_tensor("psum", [P, 8, NC], F32))
        self.landed = [self.sem(f"chunk_landed{i}") for i in range(RAW)]
        self.split_hi = Signal(self.sem("chunk_split_hi"))
        self.split_lo = Signal(self.sem("chunk_split_lo"))
        self.used = Signal(self.sem("chunk_used"))
        self.acc_free = Signal(self.sem("acc_free"))

    def sb(self, name, shape, dt=F32, ctx=None):
        self.names += 1
        return (ctx or self.ctx).enter_context(self.nc.sbuf_tensor(f"{name}_{self.names}", shape, dt))

    def sem(self, name):
        return self.ctx.enter_context(self.nc.semaphore(name))

    def sig(self, name, per):
        if name.split("_", 1)[-1] in SHARED:
            name = name.split("_", 1)[-1]
        if name not in self.signals:
            self.signals[name] = Signal(self.sem(name))
        s = self.signals[name]
        s.per, s.n = per, 0
        self.stage.append((name, s))
        return s

    def con_(self, name, n):
        return self.con[:, CON[name]:CON[name] + n]

    def col(self, name, i, n=1):
        return self.cols[:, COL[name] + i:COL[name] + i + n]

    def begin(self, no, tiles):
        self.stage_no, self.stage, self.tiles_per = no, [], tiles
        self.chunks, self.turns, self.source = (0, 1, None) if no is None else self.plan[no]

    def end(self):
        wrong = [(name, s.n, s.per) for name, s in self.stage if s.n != s.per]
        assert not wrong, wrong
        for name, s in self.stage:
            s.base += s.per * self.turns
        self.pos += self.chunks * self.turns
        self.tiles += self.tiles_per * self.turns

    def halves(self, turn, k):
        return 2 * (self.pos + k) + 2 * self.chunks * turn

    def load(self, sp, turn, k, parts, wait=True):
        slot = (self.pos + k) % RAW
        if wait:
            sp.wait_ge(self.split_hi.sem, self.halves(turn, k - RAW + 1))
            sp.wait_ge(self.split_lo.sem, self.halves(turn, k - RAW + 1))
        dst, src = parts(self.raw[:, slot, :])
        sp.dma_start(dst, src).then_inc(self.landed[slot], 16)

    def stream(self, sp, turns=1):
        if turns > 1:
            with sp.Fori(0, turns - 1) as g:
                for k in range(RAW, self.chunks + RAW):
                    self.load(sp, g, k, self.source(k % self.chunks, g + k // self.chunks))
        for k in range(min(RAW, self.chunks), self.chunks + RAW) if turns > 1 else range(RAW, self.chunks + RAW):
            if turns > 1 and k < RAW:
                continue
            if k < self.chunks:
                self.load(sp, turns - 1, k, self.source(k, turns - 1))
            else:
                src = self.following(k - self.chunks)
                if src is not None:
                    self.load(sp, turns - 1, k, src)

    def following(self, i):
        for chunks, turns, source in self.plan[self.stage_no + 1:]:
            if i < chunks * turns:
                return source(i % chunks, i // chunks)
            i -= chunks * turns
        return None

    def split_act(self, act, turn, k):
        if self.no_chunk(turn, k):
            return
        slot, s = (self.pos + k) % RAW, (self.pos + k) % SPLIT
        act.wait_ge(self.landed[slot], 16 * ((self.pos + k) // RAW + 1) + 16 * (self.chunks // RAW) * turn
                    if self.chunks % RAW == 0 else 16 * ((self.pos + k) // RAW + 1))
        for h in range(2):
            c = slice(h * HALF, (h + 1) * HALF)
            act.wait_ge(self.used.sem, self.halves(turn, k) + h + 1)
            act.activation(self.whi[:, s, c], self.raw[:, slot, c], ACT.Copy).then_inc(self.split_hi.sem, 1)

    def split_dve(self, dve, turn, k):
        if self.no_chunk(turn, k):
            return
        slot, s = (self.pos + k) % RAW, (self.pos + k) % SPLIT
        for h in range(2):
            c = slice(h * HALF, (h + 1) * HALF)
            dve.wait_ge(self.split_hi.sem, self.halves(turn, k) + h + 1)
            dve.tensor_tensor(self.wlo[:, s, c], self.raw[:, slot, c], self.whi[:, s, c].bitcast(F32),
                              ALU.subtract).then_inc(self.split_lo.sem, 1)

    def pair(self, t):
        return 2 * ((self.tiles + t) % 2)

    def acc(self, t, half):
        return self.psum[:, self.pair(t) + half, :]

    def acc2(self, t):
        a = self.pair(t)
        return self.psum[:, a:a + 2, :]

    def acc_open(self, pe, turn, t):
        pe.wait_ge(self.acc_free.sem, self.tiles + t + 1 + self.tiles_per * turn)

    def acc_wait(self, eng, turn, k):
        eng.wait_ge(self.used.sem, self.halves(turn, k + 1) + 2 * SPLIT)

    def acc_was_read(self, eng, turn, t):
        eng.wait_ge(self.acc_free.sem, self.tiles + t + 3 + self.tiles_per * turn)

    def loop(self, eng, body):
        whole = self.turns - (self.following(0) is None)
        before = [s.n for _, s in self.stage]
        if whole > 0:
            with eng.Fori(0, whole) as g:
                body(g)
        if whole < self.turns:
            for (_, s), n in zip(self.stage, before):
                s.n = n
            body(self.turns - 1)

    def no_chunk(self, turn, k):
        return isinstance(turn, int) and k >= self.chunks * (self.turns - turn) and self.following(0) is None

    def product(self, pe, turn, k, t, hi, lo, kts, cols=NC, rows=P, first=True, last=True, at=0, step=None, release=True):
        s = (self.pos + k) % SPLIT
        last_a = at + (len(kts) - 1) * (step or cols)
        halves = [h for h in range(2) if at < (h + 1) * HALF and last_a >= h * HALF]
        for n, kt in enumerate(kts):
            a = at + n * (step or cols)
            if n == 0 or a // HALF > (a - (step or cols)) // HALF:
                pe.wait_ge(self.split_lo.sem, self.halves(turn, k) + a // HALF + 1)
            wh, wl = self.whi[0:rows, s, a:a + cols], self.wlo[0:rows, s, a:a + cols]
            for half in range(NT):
                o = self.acc(t, half)[:, 0:cols]
                h, l = hi[0:rows, kt, half * P:half * P + P], lo[0:rows, kt, half * P:half * P + P]
                pe.matmul(o, h, wh, start=first and n == 0, stop=False)
                pe.matmul(o, h, wl, start=False, stop=False)
                mm = pe.matmul(o, l, wh, start=False, stop=last and n == len(kts) - 1)
            if release and halves == [0, 1] and a < HALF <= a + (step or cols):
                mm.then_inc(self.used.sem, 1)
        if release:
            mm.then_inc(self.used.sem, 1 if halves == [0, 1] else 2)
        return mm

    def product_t(self, pe, turn, k, t, hi, lo, kts, first=True, last=True):
        s = (self.pos + k) % SPLIT
        for n, kt in enumerate(kts):
            if n % 2 == 0:
                pe.wait_ge(self.split_lo.sem, self.halves(turn, k) + n // 2 + 1)
            for ct in range(4):
                a = n * NC + ct * P
                wh, wl = self.whi[:, s, a:a + P], self.wlo[:, s, a:a + P]
                o = self.acc(t, ct // 2)[:, ct % 2 * SEQ:ct % 2 * SEQ + SEQ]
                pe.matmul(o, wh, hi[:, kt, :], start=first and n == 0 and ct % 2 == 0, stop=False, skip_group_check=True)
                pe.matmul(o, wl, hi[:, kt, :], start=False, stop=False, skip_group_check=True)
                mm = pe.matmul(o, wh, lo[:, kt, :], start=False, stop=last and n == len(kts) - 1, skip_group_check=True)
            if n % 2 == 1:
                mm.then_inc(self.used.sem, 1)
        return mm


def block_half(ap, lv, which):
    return ap.rearrange("p h (a t m) -> p h a t m", t=2, m=1 << lv)[:, :, :, which, :]


def first(ap, lv):
    return block_half(ap, lv, 0)


def second(ap, lv):
    return block_half(ap, lv, 1)


def four(bank):
    return bank.rearrange("p (h c) -> p h c", c=P)


def sigmoid(K, ta, buf, mark):
    ta.step(ta.eng.activation(buf, buf, ACT.Exp, scale=-1.0))
    ta.step(ta.eng.activation(buf, buf, ACT.Ln, bias=K.eps[:, 3:4]))
    mark.inc(ta.eng.activation(buf, buf, ACT.Exp, scale=-1.0))


class Turn:

    def __init__(self, eng, turn, steps):
        self.eng, self.turn, self.steps = eng, turn, steps

    def wait(self, signal, n=1):
        self.eng.wait_ge(signal.sem, signal.count(self.turn, n))

    def step(self, ins):
        n = self.steps.inc(ins)
        self.wait(self.steps, n)


def dma_parts(w, k0, nk, c0, width=NC):
    def parts(slot):
        src = w[bass.ds(k0 * P, nk * P), bass.ds(c0, width)].rearrange("(k p) n -> p k n", p=P)
        return slot[:, 0:nk * width].rearrange("p (k n) -> p k n", k=nk), src
    return parts


def start_stage(K, cs):
    nc, t = K.nc, K.t
    inputs, pos_in, steps, done = (K.sem(n) for n in ("inputs_landed", "positions_landed", "rotary_steps", "rotary_done"))
    with ExitStack() as st:
        pos_i = K.sb("pos_i", [P, NT], I32, ctx=st)
        freq = K.sb("freq", [P, ROT_HALF], ctx=st)
        pos = K.sb("pos", [P, NT], ctx=st)
        ang = K.sb("ang", [P, 2, NT, ROT_HALF], ctx=st)
        turns = K.sb("turns", [P, 2, NT, ROT_HALF], ctx=st)
        block = st.enter_context(nc.Block())
        flat_a = ang[:, :, :, :].rearrange("p c t f -> p (c t f)")
        flat_n = turns[:, :, :, :].rearrange("p c t f -> p (c t f)")

        @block.sync
        def _(sp):
            sp.dma_start(pos_i[:, :], t["positions"]).then_inc(pos_in, 16)
            sp.dma_start(freq[:, :], t["con"][:, CON["inv_freq"]:CON["inv_freq"] + ROT_HALF]).then_inc(pos_in, 16)
            for k in range(RAW):
                if k == 1:
                    sp.wait_ge(inputs, 48)
                K.load(sp, 0, k, K.plan[0][2](k, 0), wait=False)

        @block.scalar
        def _(act):
            act.dma_start(K.x[:, :, :], t["x"].rearrange("(t p) d -> p t d", p=P)).then_inc(inputs, 16)
            act.dma_start(K.con[:, :], t["con"]).then_inc(inputs, 16)
            act.dma_start(K.cols[:, :], t["cols"]).then_inc(inputs, 16)
            act.wait_ge(done, 1)
            act.activation(cs[:, :, :, :].rearrange("p c t f -> p (c t f)"), flat_a, ACT.Sin).then_inc(done, 1)
            act.preload_act_table_set("natural_log_exp_and_others")
            act.wait_ge(K.landed[0], 16)
            act.activation(K.whi[:, 0, :], K.raw[:, 0, :], ACT.Copy).then_inc(K.split_hi.sem, 2)
            act.wait_ge(inputs, 48)

        @block.vector
        def _(dve):
            for i, v in enumerate((EPS, A_SUBLN_EPS, B_GN_EPS, 1.0)):
                ins = dve.memset(K.eps[:, i:i + 1], v)
                ins.then_inc(K.acc_free.sem if i < 2 else K.used.sem, 1 if i < 2 else SPLIT)
            n = [0]

            def step(ins):
                n[0] += 1
                ins.then_inc(steps, 1)
                dve.wait_ge(steps, n[0])

            dve.wait_ge(pos_in, 32)
            step(dve.tensor_copy(pos[:, :], pos_i[:, :]))
            for half in range(NT):
                step(dve.tensor_scalar(ang[:, 1, half, :], freq[:, :], pos[:, half:half + 1], None,
                                       ALU.mult))
            step(dve.tensor_copy(ang[:, 0, :, :], ang[:, 1, :, :]))
            big = 1.5 * 2.0 ** 23
            step(dve.tensor_scalar(turns[:, 1, :, :], ang[:, 1, :, :], 1.0 / (2 * math.pi), None, ALU.mult))
            step(dve.tensor_scalar(turns[:, 0, :, :], ang[:, 0, :, :], 1.0 / (2 * math.pi), 0.25, ALU.mult, ALU.add))
            step(dve.tensor_scalar(flat_n, flat_n, big, None, ALU.add))
            step(dve.tensor_scalar(flat_n, flat_n, big, None, ALU.subtract))
            c1 = 6.28125
            c2 = float(np.float32(math.floor((2 * math.pi - c1) * 2 ** 20) / 2 ** 20))
            for c in (c1, c2, 2 * math.pi - c1 - c2):
                step(dve.scalar_tensor_tensor(out=flat_a, in0=flat_n, scalar=-c, in1=flat_a, op0=ALU.mult, op1=ALU.add))
            step(dve.tensor_scalar(ang[:, 0, :, :], ang[:, 0, :, :], math.pi / 2, None, ALU.add))
            dve.tensor_scalar(flat_a, flat_a, 3.14159, -3.14159, ALU.min, ALU.max).then_inc(done, 1)
            dve.wait_ge(K.split_hi.sem, 2)
            dve.tensor_tensor(K.wlo[:, 0, :], K.raw[:, 0, :], K.whi[:, 0, :].bitcast(F32),
                              ALU.subtract).then_inc(K.split_lo.sem, 2)


def norm_stage(K, no, gcol, hi, lo, plain=None, embed=None):
    nc = K.nc
    K.begin(no, 4 if embed else 0)
    squared, scaled, turned = K.sig("squared", NT), K.sig("scaled", NT), K.sig("turned", KT // 2)
    his, los = K.sig("norm_hi", KT // 2), K.sig("norm_lo", KT // 2 if plain is None else 0)
    read = los if plain is None else his
    own = K.sig("norm_chain", 4)
    if embed:
        p_in, p_hi, p_lo = K.sig("p_landed", 16), K.sig("p_hi", 1), K.sig("p_lo", 1)
    with ExitStack() as st:
        xn = K.sb("xn", [P, NT, D], ctx=st)
        if embed:
            layer, out = embed
            pt = K.sb("pt", [P, 2, SEQ], ctx=st)
            pt_hi = K.sb("pt_hi", [P, 2, SEQ], F32R, ctx=st)
            pt_lo = K.sb("pt_lo", [P, 2, SEQ], F32R, ctx=st)
        block = st.enter_context(nc.Block())

        def bank(i):
            return K.psum[:, 4 + i % 4, :]

        @block.sync
        def _(sp):
            if embed:
                p_in.inc(sp.dma_start(pt[:, :, :], K.t["p_t"][layer].rearrange("(k p) t -> p k t", p=P)), 16)
                K.stream(sp)

        @block.scalar
        def _(act):
            for half in range(NT):
                squared.inc(act.activation(xn[:, half, :], K.x[:, half, :], ACT.Square,
                                           accum_out=K.stat[:, half:half + 1]))
                act.wait_ge(squared.sem, squared.count(0, half + 1))
                own.inc(act.activation(K.stat[:, 2 + half:3 + half], K.stat[:, half:half + 1], ACT.Ln, bias=K.eps[:, 0:1],
                                       scale=1.0 / D))
                act.wait_ge(own.sem, own.count(0, 2 * half + 1))
                own.inc(act.activation(K.stat[:, 4 + half:5 + half], K.stat[:, 2 + half:3 + half], ACT.Exp, scale=-0.5))
                if embed and half == 0:
                    act.wait_ge(p_in.sem, p_in.count(0, 16))
                    p_hi.inc(act.activation(pt_hi[:, :, :], pt[:, :, :], ACT.Copy))
            if embed:
                for k in range(1, K.chunks + 1):
                    K.split_act(act, 0, k)
                for t in range(4):
                    K.acc_wait(act, 0, t // 2)
                    act.activation(out[:, :, t * NC:(t + 1) * NC], K.acc2(t), ACT.Copy).then_inc(K.acc_free.sem, 1)
            for i in range(KT // 2):
                act.wait_ge(turned.sem, turned.count(0, i + 1))
                for kk in range(2):
                    k = 2 * i + kk
                    src = bank(i)[:, kk * SEQ:(kk + 1) * SEQ]
                    dst = plain if plain is not None else hi
                    ins = act.activation(dst[:, k, :], src, ACT.Copy, scale=K.col(gcol[0], gcol[1] + k))
                his.inc(ins)

        @block.vector
        def _(dve):
            if embed:
                dve.wait_ge(p_hi.sem, p_hi.count(0, 1))
                p_lo.inc(dve.tensor_tensor(pt_lo[:, :, :], pt[:, :, :], pt_hi[:, :, :].bitcast(F32), ALU.subtract))
                for k in range(1, K.chunks + 1):
                    K.split_dve(dve, 0, k)
            for half in range(NT):
                dve.wait_ge(own.sem, own.count(0, 2 * half + 2))
                scaled.inc(dve.tensor_scalar(xn[:, half, :], K.x[:, half, :], K.stat[:, 4 + half:5 + half], None,
                                             ALU.mult))
            for i in range(KT // 2 if plain is None else 0):
                dve.wait_ge(his.sem, his.count(0, i + 1))
                for kk in range(2):
                    k = 2 * i + kk
                    src = bank(i)[:, kk * SEQ:(kk + 1) * SEQ]
                    ins = dve.scalar_tensor_tensor(out=lo[:, k, :], in0=src, scalar=K.col(gcol[0], gcol[1] + k),
                                                   in1=hi[:, k, :].bitcast(F32), op0=ALU.mult, op1=ALU.subtract)
                los.inc(ins)

        @block.tensor
        def _(pe):
            if embed:
                pe.wait_ge(p_lo.sem, p_lo.count(0, 1))
                for t in range(4):
                    K.acc_open(pe, 0, t)
                    K.product(pe, 0, t // 2, t, pt_hi, pt_lo, (0, 1), at=t % 2 * NC, step=2 * NC, release=t % 2 == 1)
            for i0 in range(0, KT // 2, 4):
                for half in range(NT):
                    pe.wait_ge(scaled.sem, scaled.count(0, half + 1))
                    for i in range(i0, i0 + 4):
                        if i >= 4 and half == 0:
                            pe.wait_ge(read.sem, read.count(0, i - 3))
                        for kk in range(2):
                            c = kk * SEQ + half * P
                            k = 2 * i + kk
                            mm = pe.transpose(bank(i)[:, c:c + P], xn[:, half, k * P:(k + 1) * P], K.con_("ident", P))
                        if half == NT - 1:
                            turned.inc(mm)
    K.end()


def gate_stage(K, no, hi, lo, pp):
    nc = K.nc
    K.begin(no, 2)
    expd = K.sig("gate_sigmoid", 2)
    act_steps, steps = K.sig("gate_act_steps", 4), K.sig("gate_pool_steps", 4)
    if steps.base == 0:
        steps.base = 1
    with ExitStack() as st:
        e = K.sb("gate_e", [P, 2, NT, NC], ctx=st)
        block = st.enter_context(nc.Block())

        @block.sync
        def _(sp):
            K.stream(sp, K.turns)

        @block.scalar
        def _(act):
            def turn(g):
                for t in range(2):
                    for k in range(4 * t + 1, 4 * t + 5):
                        K.split_act(act, g, k)
                    K.acc_was_read(act, g, t)
                    sigmoid(K, Turn(act, g, act_steps), e[:, t, :, :], expd)

            K.loop(act, turn)

        @block.vector
        def _(dve):
            def turn(g):
                for t in range(2):
                    for k in range(4 * t + 1, 4 * t + 5):
                        K.split_dve(dve, g, k)
                    K.acc_wait(dve, g, 4 * t + 3)
                    if t == 0:
                        dve.wait_ge(steps.sem, steps.count(g, 0))
                    dve.tensor_scalar(e[:, t, :, :], K.acc2(t), -LN_LIMIT, None, ALU.max).then_inc(K.acc_free.sem, 1)

            K.loop(dve, turn)

        @block.gpsimd
        def _(pool):
            def turn(g):
                tp = Turn(pool, g, steps)
                for t in range(2):
                    tp.wait(expd, t + 1)
                    c = bass.ds(g * 2 * NC + t * NC, NC)
                    et = e[:, t, :, :]
                    tp.step(pool.tensor_tensor(et, et, pp[:, :, c], ALU.mult))
                    tp.step(pool.tensor_tensor(K.x[:, :, c], K.x[:, :, c], et, ALU.add))

            if steps.base == 1:
                pool.memset(K.stat[:, 6:7], 0.0).then_inc(steps.sem, 1)
            K.loop(pool, turn)

        @block.tensor
        def _(pe):
            def turn(g):
                for t in range(2):
                    K.acc_open(pe, g, t)
                    for c in range(4):
                        K.product(pe, g, 4 * t + c, t, hi, lo, range(4 * c, 4 * c + 4), first=c == 0, last=c == 3)

            K.loop(pe, turn)
    K.end()


def final_stage(K):
    nc = K.nc
    g_in, squared, steps, out_done = K.sem("final_g_landed"), K.sem("final_squared"), K.sem("final_steps"), K.sem("out_done")
    scaled = K.sem("final_scaled")
    with ExitStack() as st:
        y = K.sb("y", [P, NT, D], ctx=st)
        gain = K.sb("gain", [P, D], ctx=st)
        block = st.enter_context(nc.Block())

        @block.sync
        def _(sp):
            sp.dma_start(gain[:, :], K.t["final_norm_g"].partition_broadcast(P)).then_inc(g_in, 16)
            out = K.t["out"].rearrange("(t p) d -> t p d", p=P)
            for half in range(NT):
                sp.wait_ge(scaled, half + 1)
                sp.dma_start(out[half], y[:, half, :]).then_inc(out_done, 16)
            sp.wait_ge(out_done, 16 * NT)

        @block.scalar
        def _(act):
            for half in range(NT):
                act.activation(y[:, half, :], K.x[:, half, :], ACT.Square,
                               accum_out=K.stat[:, half:half + 1]).then_inc(squared, 1)
            act.wait_ge(squared, NT)
            act.activation(K.stat[:, 2:4], K.stat[:, 0:2], ACT.Ln, bias=K.eps[:, 0:1], scale=1.0 / D).then_inc(steps, 1)
            act.wait_ge(steps, 1)
            act.activation(K.stat[:, 4:6], K.stat[:, 2:4], ACT.Exp, scale=-0.5).then_inc(steps, 1)

        @block.vector
        def _(dve):
            dve.wait_ge(g_in, 16)
            dve.wait_ge(steps, 2)
            for half in range(NT):
                dve.scalar_tensor_tensor(out=y[:, half, :], in0=K.x[:, half, :], scalar=K.stat[:, 4 + half:5 + half],
                                         in1=gain[:, :], op0=ALU.mult, op1=ALU.mult).then_inc(scaled, 1)


def attention_stage(K, no, layer_a, lam_init, hi, lo, cs):
    nc = K.nc
    K.begin(no, 8)
    SC = A_HD ** -0.5
    roped = K.sig("a_roped", 2)
    qk_t = K.sig("a_qk_turned", 2)
    qk_t_out = K.sig("a_qk_turned_out", 2)
    scored = K.sig("a_scored", 1)
    maxed = K.sig("a_maxed", 1)
    expd = K.sig("a_exp", 1)
    mixed = K.sig("a_mixed", 1)
    mixed_t = K.sig("a_mixed_turned", 1)
    mixed_t_out = K.sig("a_mixed_turned_out", 1)
    attended = K.sig("a_attended", 1)
    rstd_done = K.sig("a_rstd", 1)
    gated = K.sig("a_gated", 1)
    out_t = K.sig("a_out_turned", 1)
    out_hi, out_lo = K.sig("a_out_hi", 1), K.sig("a_out_lo", 1)
    z_held, z_sig = K.sig("a_z_held", 1), K.sig("a_z_sig", 1)
    act_steps = K.sig("a_act_steps", 14)
    dve_steps = K.sig("a_dve_steps", 9)
    lam_in, lam_steps = K.sem(f"lambda_landed{layer_a}"), K.sem(f"lambda_steps{layer_a}")
    with ExitStack() as st:
        def sb(name, shape, dt=F32):
            return K.sb(name, shape, dt, ctx=st)
        q, k_, v, z = (sb(n, [P, NT, NC]) for n in ("a_q", "a_k", "a_v", "a_z"))
        ez = sb("a_ez", [P, NT, NC])
        rot = sb("a_rot", [P, 4, NT, A_HC, ROT_HALF])
        q_t, k_t = sb("a_qt", [P, A_HC, SEQ]), sb("a_kt", [P, A_HC, SEQ])
        s = sb("a_s", [P, A_HC, 3 * P])
        mx, sums, coef = (sb(n, [P, 2 * A_HC]) for n in ("a_mx", "a_sums", "a_coef"))
        m_t = sb("a_mt", [P, 2, 3 * P])
        o = sb("a_o", [P, NT, NC])
        ss = sb("a_ss", [P, 4])
        rs = sb("a_rs", [P, 4])
        o_hi, o_lo = sb("a_ohi", [P, CK, SEQ], F32R), sb("a_olo", [P, CK, SEQ], F32R)
        lam = sb("a_lam", [P, 4, A_HD])
        lv = sb("a_lv", [P, 8])
        sg = sb("a_sg", [P, 2])
        block = st.enter_context(nc.Block())
        bank = [K.psum[:, 4 + i, :] for i in range(4)]

        @block.sync
        def _(sp):
            sp.dma_start(lam[:, :, :].rearrange("p a d -> p (a d)"),
                         K.t["a_lam"][layer_a].partition_broadcast(P)).then_inc(lam_in, 16)
            K.stream(sp, K.turns)

        @block.scalar
        def _(act):
            act.wait_ge(lam_steps, 4)
            act.activation(lv[:, 2:4], lv[:, 0:2], ACT.Exp).then_inc(lam_steps, 1)

            def turn(g):
                def step(ins):
                    act.wait_ge(act_steps.sem, act_steps.count(g, act_steps.inc(ins)))

                def split(*ks):
                    for k in ks:
                        K.split_act(act, g, k)

                def read_out(t, dst):
                    K.acc_wait(act, g, 4 * t + 3)
                    act.activation(dst[:, :, :], K.acc2(t), ACT.Copy).then_inc(K.acc_free.sem, 1)

                for t, dst in enumerate((q, k_)):
                    split(*range(4 * t + 1, 4 * t + 5))
                    read_out(t, dst)
                split(9, 10)
                for n, dst in enumerate((q_t, k_t)):
                    act.wait_ge(qk_t.sem, qk_t.count(g, n + 1))
                    qk_t_out.inc(act.activation(dst[:, :, :], K.psum[:, 4 + 2 * n:6 + 2 * n, :], ACT.Copy))
                split(11, 12)
                act.wait_ge(maxed.sem, maxed.count(g, 1))
                for hc in range(A_HC):
                    for qt in range(NT):
                        c = slice(0, P) if qt == 0 else slice(P, 3 * P)
                        i = 2 * hc + qt
                        ins = act.activation(s[:, hc, c], s[:, hc, c], ACT.Exp, bias=mx[:, i:i + 1], scale=SC,
                                             accum_out=sums[:, i:i + 1])
                        if i < 2 * A_HC - 1:
                            act_steps.inc(ins)
                        else:
                            expd.inc(ins)
                split(13)
                read_out(2, z)
                split(14)
                act.wait_ge(z_held.sem, z_held.count(g, 1))
                sigmoid(K, Turn(act, g, act_steps), ez[:, :, :], z_sig)
                split(15, 16)
                read_out(3, v)
                act.wait_ge(attended.sem, attended.count(g, 1))
                for h in range(2):
                    for qt in range(NT):
                        i = 2 * h + qt
                        src = bank[2 + h][:, qt * A_VD:(qt + 1) * A_VD]
                        ins = act.activation(o[:, qt, h * A_VD:(h + 1) * A_VD], src, ACT.Square,
                                             accum_out=ss[:, i:i + 1])
                        act_steps.inc(ins)
                act.wait_ge(act_steps.sem, act_steps.count(g, act_steps.n))
                step(act.activation(rs[:, :], ss[:, :], ACT.Ln, bias=K.eps[:, 1:2], scale=1.0 / A_VD))
                rstd_done.inc(act.activation(rs[:, :], rs[:, :], ACT.Exp, scale=-0.5))
                act.wait_ge(out_t.sem, out_t.count(g, 1))
                for kt in range(CK):
                    ins = act.activation(o_hi[:, kt, :], bank[kt // 2][:, kt % 2 * SEQ:(kt % 2 + 1) * SEQ], ACT.Copy,
                                         scale=sg[:, kt % 2:kt % 2 + 1])
                out_hi.inc(ins)
                for k in (17, 18, 19, 20):
                    K.split_act(act, g, k)

            K.loop(act, turn)

        @block.vector
        def _(dve):
            n = [0]

            def first_step(ins):
                n[0] += 1
                ins.then_inc(lam_steps, 1)
                dve.wait_ge(lam_steps, n[0])

            dve.wait_ge(lam_in, 16)
            first_step(dve.tensor_tensor(lam[:, 0, :], lam[:, 0, :], lam[:, 1, :], ALU.mult))
            first_step(dve.tensor_tensor(lam[:, 2, :], lam[:, 2, :], lam[:, 3, :], ALU.mult))
            first_step(dve.tensor_reduce(lv[:, 0:1], lam[:, 0, :], AX.X, ALU.add))
            first_step(dve.tensor_reduce(lv[:, 1:2], lam[:, 2, :], AX.X, ALU.add))
            dve.wait_ge(lam_steps, 5)
            n[0] = 5
            first_step(dve.tensor_tensor(lv[:, 4:5], lv[:, 3:4], lv[:, 2:3], ALU.subtract))
            first_step(dve.tensor_scalar(lv[:, 5:6], lv[:, 4:5], -lam_init, None, ALU.add))
            first_step(dve.tensor_scalar(sg[:, :], K.col("subln_g", 2 * layer_a, 2), 1.0 - lam_init, None, ALU.mult))
            first_step(dve.memset(m_t[:, :, :], 0.0))

            def turn(g):
                def step(ins):
                    dve.wait_ge(dve_steps.sem, dve_steps.count(g, dve_steps.inc(ins)))

                def split(*ks):
                    for k in ks:
                        K.split_dve(dve, g, k)

                cos = [cs[:, 0, half, :].unsqueeze(1).broadcast_to([P, A_HC, ROT_HALF]) for half in range(NT)]
                sin = [cs[:, 1, half, :].unsqueeze(1).broadcast_to([P, A_HC, ROT_HALF]) for half in range(NT)]
                for t, src in enumerate((q, k_)):
                    split(*range(4 * t + 1, 4 * t + 5))
                    K.acc_was_read(dve, g, t)
                    parts = []
                    for half in range(NT):
                        m = src[:, half, :].rearrange("p (a d) -> p a d", a=A_HC)
                        parts.append((m[:, :, 0:ROT_HALF], m[:, :, ROT_HALF:2 * ROT_HALF]))
                        t1, t2 = parts[half]
                        for i, (a, b) in enumerate(((t1, cos), (t2, sin), (t2, cos), (t1, sin))):
                            ins = dve.tensor_tensor(rot[:, i, half, :, :], a, b[half], ALU.mult)
                    step(ins)
                    for half, (t1, t2) in enumerate(parts):
                        dve.tensor_tensor(t1, rot[:, 0, half, :, :], rot[:, 1, half, :, :], ALU.subtract)
                        ins = dve.tensor_tensor(t2, rot[:, 2, half, :, :], rot[:, 3, half, :, :], ALU.add)
                    roped.inc(ins)
                split(9, 10, 11, 12)
                dve.wait_ge(scored.sem, scored.count(g, 1))
                for hc in range(A_HC):
                    ins = dve.tensor_tensor(s[:, hc, :], bank[hc][:, 0:3 * P], K.con_("negmask", 3 * P), ALU.add)
                step(ins)
                mxv = mx[:, :].rearrange("p (a t) -> p a t", t=NT)
                dve_steps.inc(dve.tensor_reduce(mxv[:, :, 0], s[:, :, 0:P], AX.X, ALU.max))
                step(dve.tensor_reduce(mxv[:, :, 1], s[:, :, P:3 * P], AX.X, ALU.max))
                maxed.inc(dve.tensor_scalar(mx[:, :], mx[:, :], -SC, None, ALU.mult))
                split(13)
                dve.wait_ge(expd.sem, expd.count(g, 1))
                step(dve.reciprocal(coef[:, :], sums[:, :]))
                cv = coef[:, :].rearrange("p (h c t) -> p h c t", h=2, c=2)
                step(dve.tensor_scalar(cv[:, :, 1, :], cv[:, :, 1, :], lv[:, 5:6], None, ALU.mult))
                for h in range(2):
                    for qt in range(NT):
                        c = slice(0, P) if qt == 0 else slice(P, 3 * P)
                        i = 4 * h + qt
                        ins = dve.tensor_scalar(s[:, 2 * h, c], s[:, 2 * h, c], coef[:, i:i + 1], None, ALU.mult)
                step(ins)
                for h in range(2):
                    for qt in range(NT):
                        c = slice(0, P) if qt == 0 else slice(P, 3 * P)
                        i = 4 * h + qt
                        ins = dve.scalar_tensor_tensor(out=s[:, 2 * h, c], in0=s[:, 2 * h + 1, c],
                                                       scalar=coef[:, i + 2:i + 3], in1=s[:, 2 * h, c],
                                                       op0=ALU.mult, op1=ALU.add)
                mixed.inc(ins)
                split(14)
                K.acc_was_read(dve, g, 2)
                z_held.inc(dve.tensor_scalar(ez[:, :, :], z[:, :, :], -LN_LIMIT, None, ALU.max))
                split(15)
                dve.wait_ge(mixed_t.sem, mixed_t.count(g, 1))
                mixed_t_out.inc(dve.tensor_copy(m_t[:, :, :], K.psum[:, 4:6, 0:3 * P]))
                dve.wait_ge(z_sig.sem, z_sig.count(g, 1))
                step(dve.tensor_tensor(z[:, :, :], z[:, :, :], ez[:, :, :], ALU.mult))
                split(16)
                dve.wait_ge(rstd_done.sem, rstd_done.count(g, 1))
                for h in range(2):
                    for qt in range(NT):
                        i = 2 * h + qt
                        c = slice(h * A_VD, (h + 1) * A_VD)
                        ins = dve.scalar_tensor_tensor(out=o[:, qt, c], in0=bank[2 + h][:, qt * A_VD:(qt + 1) * A_VD],
                                                       scalar=rs[:, i:i + 1], in1=z[:, qt, c], op0=ALU.mult,
                                                       op1=ALU.mult)
                gated.inc(ins)
                dve.wait_ge(out_hi.sem, out_hi.count(g, 1))
                for kt in range(CK):
                    ins = dve.scalar_tensor_tensor(out=o_lo[:, kt, :], in0=bank[kt // 2][:, kt % 2 * SEQ:(kt % 2 + 1) * SEQ],
                                                   scalar=sg[:, kt % 2:kt % 2 + 1], in1=o_hi[:, kt, :].bitcast(F32),
                                                   op0=ALU.mult, op1=ALU.subtract)
                out_lo.inc(ins)
                for t in range(4):
                    split(17 + t)
                    K.acc_wait(dve, g, 16 + t)
                    xs = K.x[:, :, t * NC:(t + 1) * NC]
                    dve.tensor_tensor(xs, K.acc2(4 + t), xs, ALU.add).then_inc(K.acc_free.sem, 1)

            K.loop(dve, turn)

        @block.tensor
        def _(pe):
            ident = K.con_("ident", P)

            def turn(g):
                def project(k, t):
                    K.product(pe, g, k, t, hi, lo, range(k % 4 * 4, k % 4 * 4 + 4), first=k % 4 == 0, last=k % 4 == 3)

                for t in range(2):
                    K.acc_open(pe, g, t)
                    for c in range(4):
                        project(4 * t + c, t)
                K.acc_open(pe, g, 2)
                project(8, 2)
                project(9, 2)
                for n, src in enumerate((q, k_)):
                    pe.wait_ge(roped.sem, roped.count(g, n + 1))
                    for hc in range(A_HC):
                        for half in range(NT):
                            c = hc % 2 * SEQ + half * P
                            mm = pe.transpose(bank[2 * n + hc // 2][:, c:c + P], src[:, half, hc * P:(hc + 1) * P], ident)
                    qk_t.inc(mm)
                project(10, 2)
                pe.wait_ge(qk_t_out.sem, qk_t_out.count(g, 2))
                for hc in range(A_HC):
                    pe.matmul(bank[hc][:, 0:P], q_t[:, hc, 0:P], k_t[:, hc, 0:P], start=True, stop=True)
                    mm = pe.matmul(bank[hc][:, P:3 * P], q_t[:, hc, P:SEQ], k_t[:, hc, :], start=True, stop=True)
                scored.inc(mm)
                project(11, 2)
                K.acc_open(pe, g, 3)
                for k in (12, 13, 14):
                    project(k, 3)
                pe.wait_ge(mixed.sem, mixed.count(g, 1))
                for h in range(2):
                    for b in range(3):
                        mm = pe.transpose(bank[h][:, b * P:(b + 1) * P], s[:, 2 * h, b * P:(b + 1) * P], ident)
                mixed_t.inc(mm)
                project(15, 3)
                pe.wait_ge(mixed_t_out.sem, mixed_t_out.count(g, 1))
                K.acc_was_read(pe, g, 3)
                for h in range(2):
                    vh = slice(h * A_VD, (h + 1) * A_VD)
                    pe.matmul(bank[2 + h][:, 0:A_VD], m_t[:, h, 0:P], v[:, 0, vh], start=True, stop=True)
                    pe.matmul(bank[2 + h][:, A_VD:2 * A_VD], m_t[:, h, P:2 * P], v[:, 0, vh], start=True, stop=False)
                    mm = pe.matmul(bank[2 + h][:, A_VD:2 * A_VD], m_t[:, h, 2 * P:3 * P], v[:, 1, vh], start=False,
                                   stop=True)
                attended.inc(mm)
                pe.wait_ge(gated.sem, gated.count(g, 1))
                for kt in range(CK):
                    for half in range(NT):
                        c = kt % 2 * SEQ + half * P
                        mm = pe.transpose(bank[kt // 2][:, c:c + P], o[:, half, kt * P:(kt + 1) * P], ident)
                out_t.inc(mm)
                pe.wait_ge(out_lo.sem, out_lo.count(g, 1))
                for t in range(4):
                    K.acc_open(pe, g, 4 + t)
                    K.product(pe, g, 16 + t, 4 + t, o_hi, o_lo, range(CK))

            K.loop(pe, turn)
    K.end()


def plan_rwkv(t):
    w = t["b_w_rkvg"]

    def lora(k, g):
        if k % 2 == 0:
            w1 = t[("b_w_w1", "b_w_a1")[k // 2]][0].rearrange("(k p) n -> p k n", p=P)
            return lambda slot: (slot[:, 0:KT * B_LORA].rearrange("p (k n) -> p k n", k=KT), w1)
        w2 = t[("b_w_w2", "b_w_a2")[k // 2]][0]
        return lambda slot: (slot[0:B_LORA, :], w2)

    def rkvg(k, g):
        rows = w[0].rearrange("c k n -> (c k) n")
        return dma_parts(rows, g * KT + k % 4 * 4, 4, k // 4 * NC)

    return [(4, 1, lora), (16, 4, rkvg), (4, B_GROUPS, lambda k, g: dma_parts(t["b_w_out"][0], g * CK, CK, k * NC))]


def rows_of(scratch, c, c0):
    return scratch[bass.ds(c * SEQ, SEQ), bass.ds(c0, NC)].rearrange("(t p) d -> p t d", p=P)


def rwkv_lora_stage(K, no, h, xx, scratch):
    nc = K.nc
    K.begin(no, 10)
    mixed, mixed_hi, mixed_lo = K.sig("bl_mixed", 2), K.sig("bl_hi", 2), K.sig("bl_lo", 2)
    in_hi, in_lo = K.sig("bl_inner_hi", 2), K.sig("bl_inner_lo", 2)
    bias_in, tile_done = K.sig("bl_bias_landed", 32), K.sig("bl_tile_done", 6)
    held = K.sig("bl_held", 8)
    ready, stored = K.sig("bl_ready", 8), [K.sig(f"rows_stored{i}", 4 * 16) for i in range(2)]
    act_steps, dve_steps = K.sig("bl_act_steps", 2 + 16), K.sig("bl_dve_steps", 2)
    with ExitStack() as st:
        def sb(name, shape, dt=F32):
            return K.sb(name, shape, dt, ctx=st)
        xc = sb("bl_xc", [P, KT, SEQ])
        hi, lo = sb("bl_xhi", [P, KT, SEQ], F32R), sb("bl_xlo", [P, KT, SEQ], F32R)
        u = sb("bl_u", [P, 2, SEQ])
        u_hi, u_lo = sb("bl_uhi", [P, 2, SEQ], F32R), sb("bl_ulo", [P, 2, SEQ], F32R)
        y = sb("bl_y", [P, 2, NT, NC])
        bias = sb("bl_bias", [P, 2, D])
        block = st.enter_context(nc.Block())

        @block.sync
        def _(sp):
            for n, name in enumerate(("b_w0", "b_a0")):
                bias_in.inc(sp.dma_start(bias[:, n, :], K.t[name][0].partition_broadcast(P)), 16)
            K.stream(sp)

        @block.gpsimd
        def _(pool):
            tp = Turn(pool, 0, None)
            for n in range(8):
                tp.wait(ready, n + 1)
                stored[n % 2].inc(pool.dma_start(rows_of(scratch, 4 + n // 4, n % 4 * NC), y[:, n % 2, :, :]), 16)
            for s in stored:
                tp.wait(s, 4 * 16)

        @block.scalar
        def _(act):
            ta = Turn(act, 0, act_steps)
            for n in range(2):
                if n == 1:
                    K.acc_wait(act, 0, 0)
                ta.wait(mixed, n + 1)
                mixed_hi.inc(act.activation(hi[:, :, :], xc[:, :, :], ACT.Copy))
                K.split_act(act, 0, 2 * n + 1)
                K.acc_wait(act, 0, 2 * n)
                ta.step(act.activation(u[0:B_LORA, n, :], K.acc(5 * n, 0)[0:B_LORA, 0:SEQ],
                                       ACT.Tanh if n == 0 else ACT.Copy))
                in_hi.inc(act.activation(u_hi[0:B_LORA, n, :], u[0:B_LORA, n, :], ACT.Copy))
                if n == 0:
                    act.preload_act_table_set("natural_log_exp_and_others")
                K.split_act(act, 0, 2 * n + 2)
                for m in range(4):
                    i = 4 * n + m
                    ta.wait(held, i + 1)
                    sigmoid(K, ta, y[:, i % 2, :, :], ready)

        @block.vector
        def _(dve):
            td = Turn(dve, 0, dve_steps)
            td.step(dve.tensor_tensor(xx[:, :, 1:SEQ], h[:, :, 0:SEQ - 1], h[:, :, 1:SEQ], ALU.subtract))
            td.step(dve.tensor_scalar(xx[:, :, 0:1], h[:, :, 0:1], -1.0, None, ALU.mult))
            for n, c in enumerate((1, 4)):
                if n == 1:
                    td.wait(mixed_lo, 1)
                for kt in range(KT):
                    ins = dve.scalar_tensor_tensor(out=xc[:, kt, :], in0=xx[:, kt, :],
                                                   scalar=K.col("mu", c * KT + kt), in1=h[:, kt, :],
                                                   op0=ALU.mult, op1=ALU.add)
                mixed.inc(ins)
                td.wait(mixed_hi, n + 1)
                td.wait(mixed, n + 1)
                mixed_lo.inc(dve.tensor_tensor(lo[:, :, :], xc[:, :, :], hi[:, :, :].bitcast(F32), ALU.subtract))
                K.split_dve(dve, 0, 2 * n + 1)
                td.wait(in_hi, n + 1)
                in_lo.inc(dve.tensor_tensor(u_lo[0:B_LORA, n, :], u[0:B_LORA, n, :],
                                            u_hi[0:B_LORA, n, :].bitcast(F32), ALU.subtract))
                dve.memset(K.stat[:, 7:8], 0.0).then_inc(K.acc_free.sem, 1)
                K.split_dve(dve, 0, 2 * n + 2)
                if n == 0:
                    td.wait(bias_in, 32)
                for m in range(4):
                    i = 4 * n + m
                    yi = y[:, i % 2, :, :]
                    if m < 3:
                        td.wait(tile_done, 3 * n + m + 1)
                    else:
                        K.acc_wait(dve, 0, 2 * n + 1)
                    if i >= 2:
                        td.wait(stored[i % 2], 16 * (i // 2))
                    row = bias[:, n, m * NC:(m + 1) * NC].unsqueeze(1).broadcast_to([P, NT, NC])
                    dve.tensor_tensor(yi, K.acc2(5 * n + 1 + m), row, ALU.add).then_inc(K.acc_free.sem, 1)
                    K.acc_was_read(dve, 0, 5 * n + 1 + m)
                    held.inc(dve.tensor_scalar(yi, yi, -LN_LIMIT, None, ALU.max))

        @block.tensor
        def _(pe):
            tt = Turn(pe, 0, None)
            for n in range(2):
                k, s = 2 * n, (K.pos + 2 * n) % SPLIT
                tt.wait(mixed_lo, n + 1)
                K.acc_open(pe, 0, 5 * n)
                pe.wait_ge(K.split_lo.sem, K.halves(0, k + 1))
                o = K.acc(5 * n, 0)[0:B_LORA, 0:SEQ]
                for kt in range(KT):
                    c = slice(kt * B_LORA, (kt + 1) * B_LORA)
                    pe.matmul(o, K.whi[:, s, c], hi[:, kt, :], start=kt == 0, stop=False)
                    pe.matmul(o, K.wlo[:, s, c], hi[:, kt, :], start=False, stop=False)
                    mm = pe.matmul(o, K.whi[:, s, c], lo[:, kt, :], start=False, stop=kt == KT - 1)
                mm.then_inc(K.used.sem, 2)
                tt.wait(in_lo, n + 1)
                for m in range(4):
                    K.acc_open(pe, 0, 5 * n + 1 + m)
                    mm = K.product(pe, 0, k + 1, 5 * n + 1 + m, u_hi, u_lo, (n,), rows=B_LORA, at=m * NC,
                                   release=m == 3)
                    if m < 3:
                        tile_done.inc(mm)
    K.end()


def rwkv_rkvg_stage(K, no, h, xx, scratch):
    nc = K.nc
    K.begin(no, 4)
    Q = 4
    mixed, mixed_hi, mixed_lo = K.sig("bp_mixed", Q), K.sig("bp_hi", Q), K.sig("bp_lo", Q)
    copied, stored = K.sig("bp_copied", 4), K.sig("rows_stored0", 4 * 16)
    with ExitStack() as st:
        xc = K.sb("bp_xc", [P, KT, SEQ], ctx=st)
        hi, lo = K.sb("bp_xhi", [P, KT, SEQ], F32R, ctx=st), K.sb("bp_xlo", [P, KT, SEQ], F32R, ctx=st)
        y = K.sb("bp_y", [P, 4, NT, NC], ctx=st)
        mu = K.sb("bp_mu", [P, 4 * KT], ctx=st)
        mu_set = K.sem("bp_mu_set")
        block = st.enter_context(nc.Block())

        @block.sync
        def _(sp):
            K.stream(sp, K.turns)

        @block.gpsimd
        def _(pool):
            def turn(g):
                tp = Turn(pool, g, None)
                for m in range(4):
                    tp.wait(copied, m + 1)
                    stored.inc(pool.dma_start(rows_of(scratch, g, m * NC), y[:, m, :, :]), 16)
                tp.wait(stored, 4 * 16)

            K.loop(pool, turn)

        @block.scalar
        def _(act):
            def turn(g):
                ta = Turn(act, g, None)
                for i in range(Q):
                    ta.wait(mixed, i + 1)
                    c = slice(4 * i, 4 * i + 4)
                    mixed_hi.inc(act.activation(hi[:, c, :], xc[:, c, :], ACT.Copy))
                for m in range(4):
                    for k in range(4 * m + 1, 4 * m + 5):
                        K.split_act(act, g, k)
                    K.acc_wait(act, g, 4 * m + 3)
                    ta.wait(stored, 0)
                    copied.inc(act.activation(y[:, m, :, :], K.acc2(m), ACT.Copy))

            K.loop(act, turn)

        @block.vector
        def _(dve):
            for i, c in enumerate((0, 2, 3, 5)):
                dve.tensor_copy(mu[:, i * KT:(i + 1) * KT], K.col("mu", c * KT, KT)).then_inc(mu_set, 1)
            dve.wait_ge(mu_set, 4)

            def mix(g):
                for i in range(Q):
                    for kt in range(4 * i, 4 * i + 4):
                        ins = dve.scalar_tensor_tensor(out=xc[:, kt, :], in0=xx[:, kt, :],
                                                       scalar=mu[:, bass.ds(g * KT + kt, 1)], in1=h[:, kt, :],
                                                       op0=ALU.mult, op1=ALU.add)
                    mixed.inc(ins)

            def turn(g, ahead):
                td = Turn(dve, g, None)
                for i in range(Q):
                    td.wait(mixed_hi, i + 1)
                    c = slice(4 * i, 4 * i + 4)
                    mixed_lo.inc(dve.tensor_tensor(lo[:, c, :], xc[:, c, :], hi[:, c, :].bitcast(F32), ALU.subtract))
                for m in range(4):
                    for k in range(4 * m + 1, 4 * m + 5):
                        K.split_dve(dve, g, k)
                    if m == 3 and ahead:
                        mix(g + 1)
                    td.wait(copied, m + 1)
                    dve.memset(K.stat[:, 7:8], 0.0).then_inc(K.acc_free.sem, 1)

            mix(0)
            mixed.n = 0
            with dve.Fori(0, K.turns - 1) as g:
                turn(g, True)
            mixed_lo.n = 0
            turn(K.turns - 1, False)

        @block.tensor
        def _(pe):
            def turn(g):
                tt = Turn(pe, g, None)
                for m in range(4):
                    K.acc_open(pe, g, m)
                    for c in range(4):
                        if m == 0:
                            tt.wait(mixed_lo, c + 1)
                        K.product(pe, g, 4 * m + c, m, hi, lo, range(4 * c, 4 * c + 4), first=c == 0, last=c == 3)

            K.loop(pe, turn)
    K.end()


def rwkv_heads_stage(K, no, scratch):
    nc = K.nc
    K.begin(no, 4)
    NH, NPAIR, HALVES = 8, 4, 2

    def sig(name, per=1):
        return K.sig("bh_" + name, per)
    loaded, late = sig("loaded", 7 * 16), sig("late", 4 * 16)
    sum_rk, g_done = sig("sum_rk"), sig("g_done")
    pool_steps = sig("pool_steps", 1)
    kk_raw, kk_sq, kk_ss, kk_rn = sig("kk_raw"), sig("kk_sq"), sig("kk_ss"), sig("kk_rn")
    cum, exps = sig("cum"), sig("exps", 3)
    arrays = sig("arrays", 4)
    turned, turned_a, turned_v = sig("turned", 2), sig("turned_a"), sig("turned_v")
    sums, masked = sig("products", 16), sig("masked", 16)
    inv_pe, inv_dve = sig("inv_pe", HALVES * 2 * 13), sig("inv_dve", HALVES * 2 * 13)
    rhs, rhs_out, sa, sa_out = sig("rhs", 4), sig("rhs_out", 4), sig("sa", 4), sig("sa_out", 4)
    decay, decay_out, state, state_out = sig("decay"), sig("decay_out"), sig("state", 2), sig("state_out", 2)
    o_done, o_out = sig("o", 4), sig("o_out", 4)
    cen, cen_sq, var, gn = sig("centred"), sig("centred_sq"), sig("variance"), sig("gn_rstd")
    g_held, g_sig, gated = sig("g_held"), sig("g_sigmoid"), sig("gated")
    out_t, out_hi, out_lo = sig("out_turned"), sig("out_hi"), sig("out_lo")
    act_steps, dve_steps = sig("act_steps", 5), sig("dve_steps", 20)
    zeroed = K.sem("bh_zeroed")
    with ExitStack() as st:
        def sb(name, shape, dt=F32):
            return K.sb("bh_" + name, shape, dt, ctx=st)
        ld = sb("ld", [P, 6, NT, NC])
        r, k_, v, g_in, w, a = (ld[:, i, :, :] for i in range(6))
        pr = sb("params", [P, 5, NC])
        kk, t1, t2 = (sb(n, [P, NT, NC]) for n in ("kk", "t1", "t2"))
        o = kk
        stat = sb("stat", [P, 4, 2 * NH])
        arr = sb("arr", [P, NT, 4, NC])
        g_sg, bonus = arr[:, 1, 0:2, :], arr[:, 1, 2:4, :]
        tr = sb("tr", [P, NPAIR, NT, 4, P])
        gm = sb("gm", [P, 8, 4 * P])
        ym = sb("ym", [P, 8, P])
        tm, xm = (a_[:, :, :].rearrange("p t (m c) -> p (t m) c", c=P) for a_ in (t1, t2))
        rh, nsa = sb("rh", [P, NT, 4, B_HD]), sb("nsa", [P, NT, 4, B_HD])
        sblk = sb("sblk", [P, NPAIR, P])
        dec = sb("dec", [P, NPAIR])
        o_hi, o_lo = sb("ohi", [P, CK, SEQ], F32R), sb("olo", [P, CK, SEQ], F32R)
        aside = sb("aside", [P, 16])
        block = st.enter_context(nc.Block())
        bank = [K.psum[:, i, :] for i in range(8)]
        ident = K.con_("ident", P)

        def bc(row):
            return row.unsqueeze(1).broadcast_to([P, NT, NC])

        def heads(ap):
            return ap.rearrange("p t (h c) -> p (t h) c", c=B_HD)

        def per_head(col):
            return col.unsqueeze(2).broadcast_to([P, 2 * NH, B_HD])

        @block.sync
        def _(sp):
            def load_rows(to, g, arrays_, rows_):
                for i, c in arrays_:
                    to.inc(sp.dma_start(ld[:, i, :, :], rows_of(scratch, c, g * NC)), 16)
                for n in rows_:
                    name = ("b_k_k", "b_k_a", "b_r_k", "b_ln_w", "b_ln_b")[n]
                    to.inc(sp.dma_start(pr[:, n, :], K.t[name][0][bass.ds(g * NC, NC)].partition_broadcast(P)), 16)

            def turn(g):
                tp = Turn(sp, g, None)
                tp.wait(gated, 0)
                load_rows(late, g, ((2, 2), (3, 3)), (3, 4))
                if not isinstance(g, int):
                    tp.wait(sum_rk)
                    tp.wait(decay)
                    load_rows(loaded, g + 1, ((1, 1), (5, 5), (0, 0), (4, 4)), (0, 1, 2))
                for k in range(RAW, 2 * RAW):
                    if isinstance(g, int):
                        src = K.following(k - RAW)
                        if src is not None:
                            K.load(sp, g, k, src)
                    else:
                        K.load(sp, g, k, K.source(k - RAW, g + 1))

            load_rows(loaded, 0, ((1, 1), (5, 5), (0, 0), (4, 4)), (0, 1, 2))
            loaded.n = 0
            with sp.Fori(0, K.turns - 1) as g:
                turn(g)
            late.n = 0
            turn(K.turns - 1)

        @block.gpsimd
        def _(pool):
            def turn(g):
                tp = Turn(pool, g, pool_steps)
                tp.wait(late, 4 * 16)
                tp.wait(turned, 2)
                tp.wait(sum_rk)
                tp.step(pool.tensor_tensor(heads(bonus), heads(v), per_head(stat[:, 1, :]), ALU.mult))
                pool.tensor_tensor(bonus, bonus, bc(pr[:, 4, :]), ALU.add)
                tp.wait(g_sig)
                g_done.inc(pool.tensor_tensor(g_in, g_in, g_sg, ALU.mult))

            K.loop(pool, turn)

        @block.scalar
        def _(act):
            def turn(g):
                ta = Turn(act, g, act_steps)
                ta.wait(kk_raw)
                kk_sq.inc(act.activation(t1[:, :, :], kk[:, :, :], ACT.Square))
                ta.wait(kk_ss)
                ta.step(act.activation(stat[:, 0, :], stat[:, 0, :], ACT.Ln, bias=K.eps[:, 0:1]))
                kk_rn.inc(act.activation(stat[:, 0, :], stat[:, 0, :], ACT.Exp, scale=-0.5))
                ta.wait(cum)
                for n, (b, s) in enumerate(((4, -B_C), (6, -B_C), (6, B_C))):
                    exps.inc(act.activation(arr[:, :, n, :], K.psum[:, b:b + 2, :], ACT.Exp, scale=s))
                ta.wait(turned, 1)
                turned_a.inc(act.activation(tr[:, 0:2, :, :, :], K.psum[:, 0:4, :], ACT.Copy))
                ta.wait(decay)
                decay_out.inc(act.activation(dec[:, :], bank[7][:, 0:NPAIR], ACT.Exp, scale=-B_C))
                ta.wait(g_held)
                sigmoid(K, ta, g_sg, g_sig)
                for hf in range(HALVES):
                    for tt in range(NT):
                        n = 2 * hf + tt + 1
                        ta.wait(rhs, n)
                        rhs_out.inc(act.activation(rh[:, tt, :, :], bank[6 + tt][:, 0:4 * B_HD], ACT.Copy))
                        ta.wait(sa, n)
                        sa_out.inc(act.activation(nsa[:, tt, :, :], bank[0 + 3 * tt][:, 0:4 * B_HD], ACT.Copy, scale=-1.0))
                        if tt == 0:
                            ta.wait(state, hf + 1)
                            for p in range(2):
                                for u in range(2):
                                    rows, c = slice(64 * u, 64 * u + 64), slice(64 * u, 64 * u + 64)
                                    ins = act.activation(sblk[rows, 2 * hf + p, c],
                                                         bank[2][rows, p * P + 64 * u:p * P + 64 * u + 64], ACT.Copy,
                                                         scale=dec[rows, 2 * hf + p:2 * hf + p + 1])
                            state_out.inc(ins)
                        ta.wait(o_done, n)
                        o_out.inc(act.activation(o[:, tt, hf * SEQ:(hf + 1) * SEQ], bank[1 + 3 * tt][:, 0:4 * B_HD],
                                                 ACT.Copy))
                ta.wait(cen)
                cen_sq.inc(act.activation(t1[:, :, :], o[:, :, :], ACT.Square))
                ta.wait(var)
                ta.step(act.activation(stat[:, 2, :], stat[:, 2, :], ACT.Ln, bias=K.eps[:, 2:3], scale=1.0 / B_HD))
                gn.inc(act.activation(stat[:, 2, :], stat[:, 2, :], ACT.Exp, scale=-0.5))
                ta.wait(out_t)
                ta.step(act.activation(o_hi[:, 0:2, :], bank[4], ACT.Copy))
                out_hi.inc(act.activation(o_hi[:, 2:4, :], bank[5], ACT.Copy))
                for k in (1, 2, 3, 4):
                    K.split_act(act, g, k)

            K.loop(act, turn)

        @block.vector
        def _(dve):
            dve.memset(gm[:, :, :], 0.0).then_inc(zeroed, 1)
            dve.memset(sblk[:, :, :], 0.0).then_inc(zeroed, 1)
            dve.wait_ge(zeroed, 2)
            mask = K.con_("mask4", 4 * P).bitcast(I32)
            eye4 = ident.unsqueeze(1).broadcast_to([P, 4, P])

            def level(n, name="levels"):
                return K.con[:, CON[name] + n * P:CON[name] + (n + 1) * P].unsqueeze(1).broadcast_to([P, 4, P])

            def turn(g):
                td = Turn(dve, g, dve_steps)
                td.wait(loaded, 7 * 16)
                kk_raw.inc(dve.tensor_tensor(kk[:, :, :], k_, bc(pr[:, 0, :]), ALU.mult))
                td.step(dve.scalar_tensor_tensor(out=t2[:, :, :], in0=a, scalar=1.0, in1=bc(pr[:, 1, :]),
                                                 op0=ALU.subtract, op1=ALU.mult))
                td.step(dve.scalar_tensor_tensor(out=k_, in0=t2[:, :, :], scalar=1.0, in1=k_, op0=ALU.add, op1=ALU.mult))
                td.wait(kk_sq)
                kk_ss.inc(dve.tensor_reduce(stat[:, 0, :], heads(t1[:, :, :]), AX.X, ALU.add))
                td.wait(kk_rn)
                td.step(dve.tensor_tensor(heads(kk[:, :, :]), heads(kk[:, :, :]), per_head(stat[:, 0, :]), ALU.mult))
                td.step(dve.tensor_tensor(t1[:, :, :], kk[:, :, :], a, ALU.mult))
                td.wait(exps, 3)
                for n, (dst, e, src) in enumerate(((3, 2, k_), (2, 2, t1[:, :, :]), (0, 0, kk[:, :, :]), (1, 1, r))):
                    ins = dve.tensor_tensor(arr[:, :, dst, :], arr[:, :, e, :], src, ALU.mult)
                    arrays.inc(ins)
                td.wait(turned, 2)
                turned_v.inc(dve.tensor_copy(tr[:, 2:4, :, :, :], K.psum[:, 4:8, :]))
                td.step(dve.tensor_tensor(t2[:, :, :], r, k_, ALU.mult))
                td.step(dve.tensor_tensor(t2[:, :, :], t2[:, :, :], bc(pr[:, 2, :]), ALU.mult))
                sum_rk.inc(dve.tensor_reduce(stat[:, 1, :], heads(t2[:, :, :]), AX.X, ALU.add))
                td.wait(late, 4 * 16)
                g_held.inc(dve.tensor_scalar(g_sg, g_in, -LN_LIMIT, None, ALU.max))
                for hf in range(HALVES):
                    for i in range(8):
                        td.wait(sums, 8 * hf + i + 1)
                        dve.memset(aside[:, 8 * hf + i:8 * hf + i + 1], 0.0)
                        masked.inc(dve.copy_predicated(gm[:, i, :], mask, bank[i]))
                    for b in range(2):
                        q = slice(4 * b, 4 * b + 4)
                        base = 26 * hf
                        td.wait(inv_pe, base + b + 1)
                        td.step(dve.scalar_tensor_tensor(out=xm[:, q, :], in0=bank[3 * b], scalar=-1.0, in1=level(0),
                                                         op0=ALU.mult, op1=ALU.mult))
                        td.step(dve.scalar_tensor_tensor(out=ym[:, q, :], in0=gm[:, q, 0:P], scalar=-1.0,
                                                         in1=level(0, "level1_t"), op0=ALU.mult, op1=ALU.mult))
                        dve.tensor_tensor(xm[:, q, :], xm[:, q, :], eye4, ALU.add)
                        inv_dve.inc(dve.tensor_tensor(ym[:, q, :], ym[:, q, :], eye4, ALU.add))
                    for lv in range(1, 7):
                        for b in range(2):
                            q = slice(4 * b, 4 * b + 4)
                            td.wait(inv_pe, base + 4 * lv - 2 + b + 1)
                            inv_dve.inc(dve.tensor_tensor(tm[:, q, :], bank[3 * b], level(lv), ALU.mult))
                        for b in range(2):
                            q = slice(4 * b, 4 * b + 4)
                            td.wait(inv_pe, base + 4 * lv + b + 1)
                            x1, y2 = first(xm[:, q, :], lv), second(ym[:, q, :], lv)
                            if lv < 6:
                                dve.tensor_tensor(x1, x1, first(four(bank[3 * b + 1]), lv), ALU.subtract)
                            inv_dve.inc(dve.tensor_tensor(y2, y2, second(four(bank[3 * b + 2]), lv), ALU.subtract))
                td.wait(o_out, 4)
                td.step(dve.tensor_reduce(stat[:, 3, :], heads(o[:, :, :]), AX.X, ALU.add))
                td.step(dve.tensor_scalar(stat[:, 3, :], stat[:, 3, :], 1.0 / B_HD, None, ALU.mult))
                cen.inc(dve.tensor_tensor(heads(o[:, :, :]), heads(o[:, :, :]), per_head(stat[:, 3, :]), ALU.subtract))
                td.wait(cen_sq)
                var.inc(dve.tensor_reduce(stat[:, 2, :], heads(t1[:, :, :]), AX.X, ALU.add))
                td.wait(gn)
                td.step(dve.tensor_tensor(heads(o[:, :, :]), heads(o[:, :, :]), per_head(stat[:, 2, :]), ALU.mult))
                td.step(dve.tensor_tensor(o[:, :, :], o[:, :, :], bc(pr[:, 3, :]), ALU.mult))
                td.wait(g_done)
                td.step(dve.tensor_tensor(o[:, :, :], o[:, :, :], bonus, ALU.add))
                gated.inc(dve.tensor_tensor(o[:, :, :], o[:, :, :], g_in, ALU.mult))
                td.wait(out_hi)
                td.step(dve.tensor_tensor(o_lo[:, 0:2, :], bank[4], o_hi[:, 0:2, :].bitcast(F32), ALU.subtract))
                out_lo.inc(dve.tensor_tensor(o_lo[:, 2:4, :], bank[5], o_hi[:, 2:4, :].bitcast(F32), ALU.subtract))
                for t in range(4):
                    K.split_dve(dve, g, 1 + t)
                    K.acc_wait(dve, g, t)
                    xs = K.x[:, :, t * NC:(t + 1) * NC]
                    dve.tensor_tensor(xs, K.acc2(t), xs, ALU.add).then_inc(K.acc_free.sem, 1)

            K.loop(dve, turn)

        @block.tensor
        def _(pe):
            def turn(g):
                tt_ = Turn(pe, g, None)
                K.acc_open(pe, g, 0)
                K.acc_open(pe, g, 1)
                tt_.wait(loaded, 7 * 16)
                for half in range(NT):
                    pe.matmul(bank[4 + half], K.con_("tri_excl_mid", P), w[:, half, :], start=True, stop=True)
                    mm = pe.matmul(bank[6 + half], K.con_("tri_incl_mid", P), w[:, half, :], start=True, stop=True)
                cum.inc(mm)
                tt_.wait(arrays, 4)
                for p in range(NPAIR):
                    for half in range(NT):
                        for i in range(4):
                            mm = pe.transpose(bank[2 * p + half][:, i * P:(i + 1) * P],
                                              arr[:, half, i, p * P:(p + 1) * P], ident)
                    if p % 2 == 1:
                        turned.inc(mm)
                tt_.wait(turned_v)
                for p in range(NPAIR):
                    pe.matmul(bank[7][:, p:p + 1], w[:, 0, p * P:(p + 1) * P], K.con_("second_half", 1),
                              start=p == 0, stop=False, skip_group_check=True)
                    mm = pe.matmul(bank[7][:, p:p + 1], w[:, 1, p * P:(p + 1) * P], K.con_("first_half", 1),
                                   start=False, stop=True, skip_group_check=True)
                decay.inc(mm)
                tt_.wait(turned_a)
                tt_.wait(decay_out)
                for hf in range(HALVES):
                    for i in range(8):
                        half, hh = i // 4, i % 4
                        p, rows = 2 * hf + hh // 2, slice(64 * (hh % 2), 64 * (hh % 2) + 64)
                        if hf == 1 and i == 0:
                            tt_.wait(o_out, 2)
                        both = tr[rows, p, half, 0:2, :]
                        pe.matmul(bank[i][:, 0:2 * P], tr[rows, p, half, 2, :], both, start=True, stop=True)
                        sums.inc(pe.matmul(bank[i][:, 2 * P:4 * P], tr[rows, p, half, 3, :], both, start=True, stop=True))
                    base, mbase = 26 * hf, 8 * hf
                    for b in range(2):
                        tt_.wait(masked, mbase + 8)
                        for j in range(4):
                            mm = pe.transpose(bank[3 * b][:, j * P:(j + 1) * P], gm[:, 4 * b + j, 0:P], ident)
                        inv_pe.inc(mm)
                    for lv in range(1, 7):
                        for b in range(2):
                            tt_.wait(inv_dve, base + 4 * (lv - 1) + b + 1)
                            for j in range(4):
                                mm = pe.matmul(bank[3 * b][:, j * P:(j + 1) * P], gm[:, 4 * b + j, 0:P],
                                               xm[:, 4 * b + j, :], start=True, stop=True)
                            inv_pe.inc(mm)
                        for b in range(2):
                            tt_.wait(inv_dve, base + 4 * lv - 2 + b + 1)
                            for j in range(4):
                                c = slice(j * P, (j + 1) * P)
                                if lv < 6:
                                    pe.matmul(bank[3 * b + 1][:, c], ym[:, 4 * b + j, :], tm[:, 4 * b + j, :],
                                              start=True, stop=True)
                                mm = pe.matmul(bank[3 * b + 2][:, c], tm[:, 4 * b + j, :], ym[:, 4 * b + j, :],
                                               start=True, stop=True)
                            inv_pe.inc(mm)
                    for half in range(NT):
                        n = 2 * hf + half + 1
                        i0 = 4 * half
                        tt_.wait(inv_dve, base + 26)
                        tt_.wait(late, 4 * 16)
                        for j in range(4):
                            ch = slice((4 * hf + j) * B_HD, (4 * hf + j + 1) * B_HD)
                            mm = pe.matmul(bank[6 + half][:, j * B_HD:(j + 1) * B_HD], gm[:, i0 + j, 2 * P:3 * P],
                                           v[:, half, ch], start=j == 0, stop=half == 0, skip_group_check=True)
                        if half == 1:
                            tt_.wait(state_out, hf + 1)
                            for p in range(2):
                                mm = pe.matmul(bank[7][:, p * P:(p + 1) * P], tr[:, 2 * hf + p, 1, 0, :],
                                               sblk[:, 2 * hf + p, :], start=False, stop=True, skip_group_check=True)
                        rhs.inc(mm)
                        tt_.wait(rhs_out, n)
                        for j in range(4):
                            mm = pe.matmul(bank[3 * half][:, j * B_HD:(j + 1) * B_HD], ym[:, i0 + j, :],
                                           rh[:, half, j, :], start=True, stop=True)
                        sa.inc(mm)
                        tt_.wait(sa_out, n)
                        if half == 0:
                            for p in range(2):
                                ch = slice((2 * hf + p) * P, (2 * hf + p + 1) * P)
                                o_ = bank[2][:, p * P:(p + 1) * P]
                                pe.matmul(o_, arr[:, 0, 3, ch], v[:, 0, ch], start=True, stop=False)
                                mm = pe.matmul(o_, arr[:, 0, 2, ch], nsa[:, 0, 2 * p:2 * p + 2, :], start=False, stop=True)
                            state.inc(mm)
                        for j in range(4):
                            ch = slice((4 * hf + j) * B_HD, (4 * hf + j + 1) * B_HD)
                            o_ = bank[1 + 3 * half][:, j * B_HD:(j + 1) * B_HD]
                            pe.matmul(o_, gm[:, i0 + j, P:2 * P], nsa[:, half, j, :], start=j == 0, stop=False,
                                      skip_group_check=True)
                            mm = pe.matmul(o_, gm[:, i0 + j, 3 * P:4 * P], v[:, half, ch], start=False, stop=half == 0,
                                           skip_group_check=True)
                        if half == 1:
                            for p in range(2):
                                mm = pe.matmul(bank[4][:, p * P:(p + 1) * P], tr[:, 2 * hf + p, 1, 1, :],
                                               sblk[:, 2 * hf + p, :], start=False, stop=True, skip_group_check=True)
                        o_done.inc(mm)
                tt_.wait(gated)
                for kt in range(CK):
                    for half in range(NT):
                        c = kt % 2 * SEQ + half * P
                        mm = pe.transpose(bank[4 + kt // 2][:, c:c + P], o[:, half, kt * P:(kt + 1) * P], ident)
                out_t.inc(mm)
                tt_.wait(out_lo)
                for t in range(4):
                    if t >= 2:
                        K.acc_open(pe, g, t)
                    K.product(pe, g, t, t, o_hi, o_lo, range(CK))

            K.loop(pe, turn)
    K.end()


def rwkv(K, no, layer):
    scratch = K.nc.dram_tensor("rwkv_rows", (6 * SEQ, D), F32).ap()
    with ExitStack() as hs:
        h, xx = K.sb("h", [P, KT, SEQ], ctx=hs), K.sb("xx", [P, KT, SEQ], ctx=hs)
        norm_stage(K, None, ("norm_g", layer * KT), None, None, plain=h)
        rwkv_lora_stage(K, no, h, xx, scratch)
        rwkv_rkvg_stage(K, no + 1, h, xx, scratch)
    rwkv_heads_stage(K, no + 2, scratch)
    return no + 3


def plan_deltanet(t):
    w, wo = t["c_w_in"][0], t["c_w_out"][0]

    def gates(k, g):
        src = w[:, 2 * C_QK + 2 * C_VW:2 * C_QK + 2 * C_VW + 2 * C_VH].rearrange("(k p) n -> p k n", p=P)
        return lambda slot: (slot[:, 0:KT * 2 * C_VH].rearrange("p (k n) -> p k n", k=KT), src)

    def source(k, g):
        if k < 24:
            tile, k0 = k // 4, k % 4 * 4
            start = (0, C_QK, 2 * C_QK, 2 * C_QK + NC, 2 * C_QK + C_VW, 2 * C_QK + C_VW + NC)[tile]
            return dma_parts(w, k0, 4, g * (NC if tile < 2 else 2 * NC) + start)
        k -= 24
        return dma_parts(wo, g * 2 * CK + k // 4 * CK, CK, k % 4 * NC)

    return [(1, 1, gates), (32, C_GROUPS, source)]


def deltanet_gates_stage(K, no, hi, lo, G):
    nc = K.nc
    K.begin(no, 1)
    H = C_VH
    rows_in = K.sig("cg_rows", 32)
    d1, a1, d2, a2, d3 = (K.sig("cg_" + n, 1) for n in ("held", "exp", "plus_one", "log", "g"))
    cum, cum_out, e_out = K.sig("cg_cum", 1), K.sig("cg_cum_out", 1), K.sig("cg_e", 1)
    dve_steps, act_steps = K.sig("cg_dve_steps", 5), K.sig("cg_act_steps", 1)
    with ExitStack() as st:
        ab = K.sb("cg_ab", [P, NT, 2 * H], ctx=st)
        e = K.sb("cg_e", [P, NT, 2 * H], ctx=st)
        rows = K.sb("cg_rows", [P, 2, H], ctx=st)
        block = st.enter_context(nc.Block())

        def bc(row):
            return row.unsqueeze(1).broadcast_to([P, NT, H])

        @block.sync
        def _(sp):
            for n, name in enumerate(("c_A_log", "c_dt_bias")):
                rows_in.inc(sp.dma_start(rows[:, n, :], K.t[name][0].partition_broadcast(P)), 16)
            K.stream(sp)

        @block.scalar
        def _(act):
            ta = Turn(act, 0, act_steps)
            K.split_act(act, 0, 1)
            ta.wait(rows_in, 32)
            ta.step(act.activation(rows[:, 0, :], rows[:, 0, :], ACT.Exp))
            ta.wait(d1)
            a1.inc(act.activation(e[:, :, :], e[:, :, :], ACT.Exp, scale=-1.0))
            ta.wait(d2)
            a2.inc(act.activation(e[:, :, H:2 * H], e[:, :, H:2 * H], ACT.Ln))
            ta.wait(cum)
            cum_out.inc(act.activation(G["gc"][:, :, :], K.psum[:, 4, 0:NT * H], ACT.Copy))
            e_out.inc(act.activation(G["egc"][:, :, :], K.psum[:, 4, 0:NT * H], ACT.Exp))

        @block.vector
        def _(dve):
            td = Turn(dve, 0, dve_steps)
            K.split_dve(dve, 0, 1)
            K.acc_wait(dve, 0, 0)
            td.wait(rows_in, 32)
            dve.tensor_copy(ab[:, :, :], K.acc2(0)[:, :, 0:2 * H]).then_inc(K.acc_free.sem, 1)
            K.acc_was_read(dve, 0, 0)
            a_, b_ = ab[:, :, H:2 * H], ab[:, :, 0:H]
            ea = e[:, :, H:2 * H]
            td.step(dve.tensor_tensor(a_, a_, bc(rows[:, 1, :]), ALU.add))
            td.step(dve.scalar_tensor_tensor(out=ea, in0=a_, scalar=-1.0, in1=a_, op0=ALU.mult, op1=ALU.max))
            d1.inc(dve.tensor_scalar(e[:, :, 0:H], b_, -LIMIT, None, ALU.max))
            td.wait(a1)
            d2.inc(dve.tensor_scalar(e[:, :, :], e[:, :, :], 1.0, None, ALU.add))
            td.wait(d2)
            dve.reciprocal(G["beta"][:, :, :], e[:, :, 0:H])
            td.wait(a2)
            td.step(dve.scalar_tensor_tensor(out=ea, in0=a_, scalar=0.0, in1=ea, op0=ALU.max, op1=ALU.add))
            d3.inc(dve.scalar_tensor_tensor(out=G["g"][:, :, :], in0=ea, scalar=-1.0, in1=bc(rows[:, 0, :]), op0=ALU.mult,
                                            op1=ALU.mult))
            td.wait(e_out)
            td.step(dve.tensor_scalar(G["negegc"][:, :, :], G["egc"][:, :, :], -1.0, None, ALU.mult))
            td.wait(cum_out)
            td.step(dve.memset(K.stat[:, 7:8], 0.0))

        @block.tensor
        def _(pe):
            tt = Turn(pe, 0, None)
            K.acc_open(pe, 0, 0)
            K.product(pe, 0, 0, 0, hi, lo, range(KT), cols=2 * H)
            tt.wait(d3)
            for half in range(NT):
                mm = pe.matmul(K.psum[:, 4, half * H:(half + 1) * H], K.con_("tri", P), G["g"][:, half, :], start=True,
                               stop=True)
            cum.inc(mm)
    K.end()


def deltanet_heads_stage(K, no, hi, lo, G):
    nc = K.nc
    K.begin(no, 14)
    QS = C_HD ** -0.5

    def sig(name, per=1):
        return K.sig("ch_" + name, per)
    conv, sigm, silu = sig("conv", 4), sig("sigmoid", 4), sig("silu", 4)
    squared, normsum, rnorm, qk_done = sig("squared", 2), sig("normsum", 2), sig("rnorm", 2), sig("qk_done", 2)
    k_turned, k_tok = sig("k_turned"), sig("k_tok")
    v_turned, v_tok = sig("v_turned", 2), sig("v_tok", 2)
    z_held, z_sig, z_done = sig("z_held", 2), sig("z_sigmoid", 2), sig("z_done", 2)
    kq, kq_out, rows, rows_out, dec = sig("kq", 4), sig("kq_out", 4), sig("rows", 4), sig("rows_out", 4), sig("decay", 4)
    n_done, g_spread = sig("n", 4), sig("g_spread", 2)
    inv_pe, inv_dve = sig("inv_pe", 2 * 26), sig("inv_dve", 2 * 26)
    u_, vnew = sig("u", 4), sig("vnew", 4)
    vs_, s_, s_out, o1 = sig("vs", 2), sig("state", 2), sig("state_out", 2), sig("o1", 4)
    o_out, ks, rhs = sig("o_out", 2), sig("ks", 2), sig("rhs", 2)
    o_full, o_sq, o_ss, o_rs, gated = sig("o_full", 2), sig("o_sq", 2), sig("o_ss", 2), sig("o_rstd", 2), sig("gated", 2)
    out_t, out_hi, out_lo = sig("out_turned", 2), sig("out_hi", 2), sig("out_lo", 2)
    act_steps, dve_steps = sig("act_steps", 18), sig("dve_steps", 74)
    with ExitStack() as st:
        def sb(name, shape, dt=F32):
            return K.sb("ch_" + name, shape, dt, ctx=st)
        q_t, k_t, v_t, e = (sb(n, [P, 4, SEQ]) for n in ("qt", "kt", "vt", "e"))
        v, z = sb("v", [P, NT, 2 * NC]), sb("z", [P, NT, 2 * NC])
        ktok = sb("ktok", [P, NC])
        kqm = sb("kqm", [P, NT, 2, 2 * P])
        dm, nm, pm, xm, ym, tm = (sb(n, [P, 8, P]) for n in ("d", "n", "p", "x", "y", "t"))
        rh, vn, vs, state = (sb(n, [P, 4, P]) for n in ("rhs", "vnew", "vs", "state"))
        o = sb("o", [P, NT, NC])
        stat = sb("stat", [P, 2 * 4])
        g_wide = tm[:, :, :]
        o_hi, o_lo = sb("ohi", [P, CK, SEQ], F32R), sb("olo", [P, CK, SEQ], F32R)
        block = st.enter_context(nc.Block())
        bank = [K.psum[:, 4 + i, :] for i in range(4)]
        ident = K.con_("ident", P)

        def ebuf():
            return e[:, :, :].rearrange("p a b -> p (a b)").rearrange("p (t c) -> p t c", t=NT)

        def gate(name, g, hf, half):
            return G[name][:, half, bass.ds(g * 8 + hf * 4, 4)]

        def per_head(col):
            return col.unsqueeze(2).broadcast_to([P, 4, P])

        def t1_bank(lv, b):
            return (0 if lv % 2 else 2) + b

        def xy_bank(lv, b):
            return ((2 if lv % 2 else 0) if b == 0 else (0 if lv % 2 else 2))

        @block.sync
        def _(sp):
            K.stream(sp, K.turns)

        @block.scalar
        def _(act):
            def turn(g):
                ta = Turn(act, g, act_steps)

                def split(*ks_):
                    for k in ks_:
                        K.split_act(act, g, k)

                def after(t):
                    k = 4 * t + 4
                    split(k + 1, k + 2)
                    ta.wait(conv, t + 1)
                    sigmoid(K, ta, e[:, :, :], sigm)
                    split(k + 3)
                    ta.wait(silu, t + 1)
                    if t < 2:
                        squared.inc(act.activation(e[:, :, :], (q_t, k_t)[t][:, :, :], ACT.Square))
                        split(k + 4)
                        ta.wait(normsum, t + 1)
                        ta.step(act.activation(ebuf(), K.psum[:, 4:6, :], ACT.Ln, bias=K.eps[:, 0:1]))
                        rnorm.inc(act.activation(e[:, :, :], e[:, :, :], ACT.Exp, scale=-0.5))
                    else:
                        ta.wait(v_turned, t - 1)
                        c = slice((t - 2) * NC, (t - 1) * NC)
                        v_tok.inc(act.activation(v[:, :, c], K.psum[:, 4:6, :], ACT.Copy))
                        split(k + 4)

                def z_copy(n):
                    K.acc_wait(act, g, 19 + 4 * n)
                    act.activation(z[:, :, n * NC:(n + 1) * NC], K.acc2(4 + n), ACT.Copy).then_inc(K.acc_free.sem, 1)

                def z_sigmoid(n):
                    ta.wait(z_held, n + 1)
                    sigmoid(K, ta, ebuf(), z_sig)

                split(1, 2, 3, 4)
                for t in range(4):
                    after(t)
                ta.wait(k_turned)
                k_tok.inc(act.activation(ktok[:, :], bank[2], ACT.Copy))
                for hf in range(2):
                    for half in range(NT):
                        ta.wait(rows_out, 2 * hf + half + 1)
                        d = dm[:, 4 * half:4 * half + 4, :]
                        dec.inc(act.activation(d, d, ACT.Exp))
                    z_copy(hf)
                    z_sigmoid(hf)
                    split(21 + 4 * hf)
                    split(22 + 4 * hf)
                    ta.wait(s_, hf + 1)
                    s_out.inc(act.activation(state[:, :, :], bank[2], ACT.Copy))
                    ta.wait(o1, 2 * hf + 1)
                    o_out.inc(act.activation(o[:, 0, :], bank[1], ACT.Copy))
                    split(23 + 4 * hf)
                    ta.wait(o_full, hf + 1)
                    o_sq.inc(act.activation(ebuf(), o[:, :, :], ACT.Square))
                    ta.wait(o_ss, hf + 1)
                    ta.step(act.activation(stat[:, :], stat[:, :], ACT.Ln, bias=K.eps[:, 0:1], scale=1.0 / C_HD))
                    o_rs.inc(act.activation(stat[:, :], stat[:, :], ACT.Exp, scale=-0.5))
                    split(24 + 4 * hf)
                    ta.wait(out_t, hf + 1)
                    act_steps.inc(act.activation(o_hi[:, 0:2, :], bank[0], ACT.Copy, scale=K.col("c_norm_g", 0)))
                    out_hi.inc(act.activation(o_hi[:, 2:4, :], bank[1], ACT.Copy, scale=K.col("c_norm_g", 0)))
                for n in range(4):
                    split(29 + n)

            K.loop(act, turn)

        @block.vector
        def _(dve):
            mask2 = K.con_("mask4", 2 * P).unsqueeze(1).broadcast_to([P, 2, 2 * P])
            eye4 = ident.unsqueeze(1).broadcast_to([P, 4, P])

            def level(n, name="levels"):
                return K.con[:, CON[name] + n * P:CON[name] + (n + 1) * P].unsqueeze(1).broadcast_to([P, 4, P])

            def turn(g):
                td = Turn(dve, g, dve_steps)

                def split(*ks_):
                    for k in ks_:
                        K.split_dve(dve, g, k)

                def taps(t, dst, cts):
                    first = (0, 16, 32, 36)[t]
                    written = {}
                    for j in range(C_TAPS - 1, -1, -1):
                        for ct in cts:
                            src = K.acc(t, ct // 2)[:, ct % 2 * SEQ:ct % 2 * SEQ + SEQ]
                            w = K.cols[:, bass.ds(g * (16 if t < 2 else 32) + (COL["conv"] + (first + ct) * C_TAPS + j), 1)]
                            lag = C_TAPS - 1 - j
                            if lag == 0:
                                ins = dve.tensor_scalar(dst[:, ct, :], src, w, None, ALU.mult)
                            else:
                                td.wait(dve_steps, written[ct])
                                ins = dve.scalar_tensor_tensor(out=dst[:, ct, lag:SEQ], in0=src[:, 0:SEQ - lag], scalar=w,
                                                               in1=dst[:, ct, lag:SEQ], op0=ALU.mult, op1=ALU.add)
                            if ct == 3 and j == 0:
                                ins.then_inc(K.acc_free.sem, 1)
                            else:
                                written[ct] = dve_steps.inc(ins)
                    if 3 in cts:
                        td.wait(dve_steps, dve_steps.n)
                        K.acc_was_read(dve, g, t)

                def after(t):
                    k = 4 * t + 4
                    dst = (q_t, k_t, v_t, v_t)[t]
                    K.acc_wait(dve, g, 4 * t + 3)
                    if t == 3:
                        td.wait(v_turned, 1)
                    taps(t, dst, (0, 1))
                    split(k + 1)
                    taps(t, dst, (2, 3))
                    conv.inc(dve.tensor_scalar(e[:, :, :], dst[:, :, :], -LN_LIMIT, None, ALU.max))
                    split(k + 2)
                    td.wait(sigm, t + 1)
                    silu.inc(dve.tensor_tensor(dst[:, :, :], dst[:, :, :], e[:, :, :], ALU.mult))
                    split(k + 3)
                    split(k + 4)
                    if t < 2:
                        td.wait(rnorm, t + 1)
                        qk_done.inc(dve.scalar_tensor_tensor(out=dst[:, :, :], in0=dst[:, :, :], scalar=(QS, 1.0)[t],
                                                             in1=e[:, :, :], op0=ALU.mult, op1=ALU.mult))

                def between(hf, n):
                    if hf == 1:
                        K.acc_wait(dve, g, 24 + n)
                        xs = K.x[:, :, n * NC:(n + 1) * NC]
                        dve.tensor_tensor(xs, K.acc2(6 + n), xs, ALU.add).then_inc(K.acc_free.sem, 1)
                    if n < 3:
                        split(22 + 4 * hf + n)

                def z_hold(n):
                    K.acc_was_read(dve, g, 4 + n)
                    z_held.inc(dve.tensor_scalar(ebuf(), z[:, :, n * NC:(n + 1) * NC], -LN_LIMIT, None, ALU.max))

                def z_mult(n):
                    td.wait(z_sig, n + 1)
                    zt = z[:, :, n * NC:(n + 1) * NC]
                    z_done.inc(dve.tensor_tensor(zt, zt, ebuf(), ALU.mult))

                split(1, 2, 3, 4)
                for t in range(4):
                    after(t)
                for hf in range(2):
                    gh = G["g"][:, :, bass.ds(g * 8 + hf * 4, 4)].unsqueeze(3).broadcast_to([P, NT, 4, P])
                    g_spread.inc(dve.tensor_copy(g_wide.rearrange("p (t h) c -> p t h c", t=NT), gh))
                    for half in range(NT):
                        n = 2 * hf + half + 1
                        td.wait(kq, n)
                        kq_out.inc(dve.tensor_tensor(kqm[:, half, :, :], bank[half].rearrange("p (a b) -> p a b", a=2),
                                                     mask2, ALU.mult))
                        td.wait(rows, n)
                        for j in range(4):
                            i = 4 * half + j
                            ins = dve.tensor_scalar(dm[:, i, :], bank[2 + half][:, j * P:(j + 1) * P],
                                                    G["gc"][:, half, bass.ds(g * 8 + hf * 4 + j, 1)], 0.0,
                                                    ALU.subtract, ALU.min)
                        rows_out.inc(ins)
                    z_hold(hf)
                    for half in range(NT):
                        n = 2 * hf + half + 1
                        td.wait(dec, n)
                        td.wait(kq_out, n)
                        for j in range(4):
                            i = 4 * half + j
                            dve.scalar_tensor_tensor(out=nm[:, i, :], in0=kqm[:, half, j // 2, 0:P],
                                                     scalar=G["beta"][:, half, bass.ds(g * 8 + hf * 4 + j, 1)],
                                                     in1=dm[:, i, :], op0=ALU.mult, op1=ALU.mult)
                        for kh in range(2):
                            i = 4 * half + 2 * kh
                            qk = kqm[:, half, kh, P:2 * P].unsqueeze(1).broadcast_to([P, 2, P])
                            ins = dve.tensor_tensor(pm[:, i:i + 2, :], dm[:, i:i + 2, :], qk, ALU.mult)
                        n_done.inc(ins)
                    z_mult(hf)
                    base = 26 * hf
                    for b in range(2):
                        q = slice(4 * b, 4 * b + 4)
                        td.wait(inv_pe, base + b + 1)
                        td.wait(n_done, 2 * hf + b + 1)
                        td.step(dve.scalar_tensor_tensor(out=xm[:, q, :], in0=bank[t1_bank(0, b)], scalar=-1.0, in1=level(0),
                                                         op0=ALU.mult, op1=ALU.mult))
                        td.step(dve.scalar_tensor_tensor(out=ym[:, q, :], in0=nm[:, q, :], scalar=-1.0,
                                                         in1=level(0, "level1_t"), op0=ALU.mult, op1=ALU.mult))
                        dve.tensor_tensor(xm[:, q, :], xm[:, q, :], eye4, ALU.add)
                        inv_dve.inc(dve.tensor_tensor(ym[:, q, :], ym[:, q, :], eye4, ALU.add))
                    for lv in range(1, 7):
                        if lv == 3:
                            split(21 + 4 * hf)
                        for b in range(2):
                            q = slice(4 * b, 4 * b + 4)
                            td.wait(inv_pe, base + 4 * lv - 2 + b + 1)
                            inv_dve.inc(dve.tensor_tensor(tm[:, q, :], bank[t1_bank(lv, b)], level(lv), ALU.mult))
                        for b in range(2):
                            q = slice(4 * b, 4 * b + 4)
                            td.wait(inv_pe, base + 4 * lv + b + 1)
                            x1, y2 = first(xm[:, q, :], lv), second(ym[:, q, :], lv)
                            if lv < 6:
                                dve.tensor_tensor(x1, x1, first(four(bank[xy_bank(lv, b)]), lv), ALU.subtract)
                            inv_dve.inc(dve.tensor_tensor(y2, y2, second(four(bank[xy_bank(lv, b) + 1]), lv), ALU.subtract))
                    c4 = slice(hf * NC, (hf + 1) * NC)

                    td.wait(u_, 2 * hf + 1)
                    vnew.inc(dve.tensor_tensor(vn[:, :, :], four(bank[0]), per_head(gate("beta", g, hf, 0)), ALU.mult))
                    td.wait(vnew, 2 * hf + 1)
                    last = dm[:, 0:4, P - 1:P].broadcast_to([P, 4, P])
                    vs_.inc(dve.tensor_tensor(vs[:, :, :], vn[:, :, :], last, ALU.mult))
                    between(hf, 0)
                    td.wait(ks, hf + 1)
                    td.step(dve.tensor_tensor(rh[:, :, :], four(bank[3]), per_head(gate("negegc", g, hf, 1)), ALU.mult))
                    rhs.inc(dve.tensor_tensor(rh[:, :, :], rh[:, :, :], four(v[:, 1, c4]), ALU.add))
                    td.step(dve.tensor_tensor(vs[:, :, :], four(bank[0]), per_head(gate("egc", g, hf, 1)), ALU.mult))
                    between(hf, 1)
                    td.wait(u_, 2 * hf + 2)
                    vnew.inc(dve.tensor_tensor(vn[:, :, :], four(bank[1]), per_head(gate("beta", g, hf, 1)), ALU.mult))
                    td.wait(o1, 2 * hf + 2)
                    td.wait(o_out, hf + 1)
                    o_full.inc(dve.tensor_tensor(four(o[:, 1, :]), vs[:, :, :], four(bank[2]), ALU.add))
                    ov = o[:, :, :].rearrange("p t (h c) -> p (t h) c", c=P)
                    td.wait(o_sq, hf + 1)
                    o_ss.inc(dve.tensor_reduce(stat[:, :], ebuf().rearrange("p t (h c) -> p (t h) c", c=P), AX.X, ALU.add))
                    td.wait(o_rs, hf + 1)
                    td.step(dve.tensor_tensor(ov, ov, stat[:, :].unsqueeze(2).broadcast_to([P, 8, P]), ALU.mult))
                    gated.inc(dve.tensor_tensor(o[:, :, :], o[:, :, :], z[:, :, c4], ALU.mult))
                    between(hf, 2)
                    if hf == 1:
                        between(hf, 3)
                    td.wait(out_hi, hf + 1)
                    for i in range(2):
                        ins = dve.scalar_tensor_tensor(out=o_lo[:, 2 * i:2 * i + 2, :], in0=bank[i].rearrange("p (a b) -> p a b", a=2),
                                                       scalar=K.col("c_norm_g", 0),
                                                       in1=o_hi[:, 2 * i:2 * i + 2, :].bitcast(F32), op0=ALU.mult,
                                                       op1=ALU.subtract)
                    out_lo.inc(ins)
                    if hf == 0:
                        between(hf, 3)
                for t in range(4):
                    split(29 + t)
                    K.acc_wait(dve, g, 28 + t)
                    xs = K.x[:, :, t * NC:(t + 1) * NC]
                    dve.tensor_tensor(xs, K.acc2(10 + t), xs, ALU.add).then_inc(K.acc_free.sem, 1)

            K.loop(dve, turn)

        @block.tensor
        def _(pe):
            def turn(g):
                tt = Turn(pe, g, None)

                def project(k, t):
                    f = K.product_t if t < 4 else K.product
                    f(pe, g, k, t, hi, lo, range(k % 4 * 4, k % 4 * 4 + 4), first=k % 4 == 0, last=k % 4 == 3)

                def after(t):
                    if t < 2:
                        tt.wait(squared, t + 1)
                        for i in range(2):
                            mm = pe.matmul(bank[i], K.con_("ones", P), e[:, 2 * i:2 * i + 2, :], start=True, stop=True)
                        normsum.inc(mm)
                    else:
                        tt.wait(silu, t + 1)
                        for half in range(NT):
                            for ct in range(4):
                                mm = pe.transpose(bank[half][:, ct * P:(ct + 1) * P], v_t[:, ct, half * P:(half + 1) * P],
                                                  ident)
                        v_turned.inc(mm)

                def between(hf, n):
                    if hf == 0:
                        if n == 0:
                            K.acc_open(pe, g, 5)
                        project(20 + n, 5)
                    else:
                        K.acc_open(pe, g, 6 + n)
                        K.product(pe, g, 24 + n, 6 + n, o_hi, o_lo, range(CK))

                for t in range(5):
                    K.acc_open(pe, g, t)
                    for c in range(4):
                        if c == 3 and t > 0:
                            after(t - 1)
                        project(4 * t + c, t)
                tt.wait(qk_done, 2)
                for ct in range(4):
                    mm = pe.transpose(bank[2][:, ct * P:(ct + 1) * P], k_t[:, ct, 0:P], ident)
                k_turned.inc(mm)
                tt.wait(v_tok, 2)
                tt.wait(k_tok)
                for hf in range(2):
                    for half in range(NT):
                        tok = slice(half * P, (half + 1) * P)
                        for kh in range(2):
                            h = 2 * hf + kh
                            o_ = bank[half][:, kh * 2 * P:(kh + 1) * 2 * P]
                            pe.matmul(o_[:, 0:P], k_t[:, h, tok], k_t[:, h, tok], start=True, stop=True)
                            mm = pe.matmul(o_[:, P:2 * P], k_t[:, h, tok], q_t[:, h, tok], start=True, stop=True)
                        kq.inc(mm)
                        tt.wait(g_spread, hf + 1)
                        for j in range(4):
                            mm = pe.matmul(bank[2 + half][:, j * P:(j + 1) * P], g_wide[:, 4 * half + j, :], K.con_("tri", P),
                                           start=True, stop=True)
                        rows.inc(mm)
                    base = 26 * hf
                    for b in range(2):
                        tt.wait(n_done, 2 * hf + b + 1)
                        tt.wait(rows_out, 2 * hf + 2)
                        for j in range(4):
                            mm = pe.transpose(bank[t1_bank(0, b)][:, j * P:(j + 1) * P], nm[:, 4 * b + j, :], ident)
                        inv_pe.inc(mm)
                    for lv in range(1, 7):
                        for b in range(2):
                            tt.wait(inv_dve, base + 4 * (lv - 1) + b + 1)
                            for j in range(4):
                                mm = pe.matmul(bank[t1_bank(lv, b)][:, j * P:(j + 1) * P], nm[:, 4 * b + j, :],
                                               xm[:, 4 * b + j, :], start=True, stop=True)
                            inv_pe.inc(mm)
                        for b in range(2):
                            tt.wait(inv_dve, base + 4 * lv - 2 + b + 1)
                            for j in range(4):
                                c = slice(j * P, (j + 1) * P)
                                if lv < 6:
                                    pe.matmul(bank[xy_bank(lv, b)][:, c], ym[:, 4 * b + j, :], tm[:, 4 * b + j, :],
                                              start=True, stop=True)
                                mm = pe.matmul(bank[xy_bank(lv, b) + 1][:, c], tm[:, 4 * b + j, :], ym[:, 4 * b + j, :],
                                               start=True, stop=True)
                            inv_pe.inc(mm)
                    tt.wait(inv_dve, base + 26)
                    for j in range(4):
                        c = slice(j * P, (j + 1) * P)
                        mm = pe.matmul(bank[0][:, c], ym[:, j, :], v[:, 0, hf * NC + j * P:hf * NC + (j + 1) * P], start=True,
                                       stop=True)
                    u_.inc(mm)
                    between(hf, 0)
                    tt.wait(vs_, hf + 1)
                    for j in range(4):
                        h = 2 * hf + j // 2
                        mm = pe.matmul(bank[2][:, j * P:(j + 1) * P], ktok[:, h * P:(h + 1) * P], vs[:, j, :], start=True,
                                       stop=True)
                    s_.inc(mm)
                    for j in range(4):
                        mm = pe.matmul(bank[1][:, j * P:(j + 1) * P], pm[:, j, :], vn[:, j, :], start=True, stop=True)
                    o1.inc(mm)
                    between(hf, 1)
                    tt.wait(s_out, hf + 1)
                    for src, b in ((k_t, 3), (q_t, 0)):
                        for kh in range(2):
                            mm = pe.matmul(bank[b][:, kh * 2 * P:(kh + 1) * 2 * P], src[:, 2 * hf + kh, P:2 * P],
                                           state[:, 2 * kh:2 * kh + 2, :], start=True, stop=True)
                    ks.inc(mm)
                    tt.wait(rhs, hf + 1)
                    tt.wait(o_out, hf + 1)
                    for j in range(4):
                        mm = pe.matmul(bank[1][:, j * P:(j + 1) * P], ym[:, 4 + j, :], rh[:, j, :], start=True, stop=True)
                    u_.inc(mm)
                    tt.wait(vnew, 2 * hf + 2)
                    for j in range(4):
                        mm = pe.matmul(bank[2][:, j * P:(j + 1) * P], pm[:, 4 + j, :], vn[:, j, :], start=True, stop=True)
                    o1.inc(mm)
                    between(hf, 2)
                    if hf == 1:
                        between(hf, 3)
                    tt.wait(gated, hf + 1)
                    for kt in range(CK):
                        for half in range(NT):
                            c = kt % 2 * SEQ + half * P
                            mm = pe.transpose(bank[kt // 2][:, c:c + P], o[:, half, kt * P:(kt + 1) * P], ident)
                    out_t.inc(mm)
                    if hf == 0:
                        between(hf, 3)
                    tt.wait(out_lo, hf + 1)
                for t in range(4):
                    K.acc_open(pe, g, 10 + t)
                    K.product(pe, g, 28 + t, 10 + t, o_hi, o_lo, range(CK))

            K.loop(pe, turn)
    K.end()


def deltanet(K, no, layer, st):
    hi, lo = K.sb("h_hi", [P, KT, SEQ], F32R, ctx=st), K.sb("h_lo", [P, KT, SEQ], F32R, ctx=st)
    G = {n: K.sb("c_" + n, [P, NT, C_VH], ctx=st) for n in ("beta", "g", "gc", "egc", "negegc")}
    norm_stage(K, None, ("norm_g", layer * KT), hi, lo)
    deltanet_gates_stage(K, no, hi, lo, G)
    deltanet_heads_stage(K, no + 1, hi, lo, G)
    return no + 2


def plan_attention(t, a):
    w, wo = t["a_w_in"][a], t["a_w_out"][a]

    def source(k, g):
        if k < 16:
            return dma_parts(w, k % 4 * 4, 4, (0, 1, 3, 2)[k // 4] * D + g * NC)
        return dma_parts(wo, g * CK, CK, (k - 16) * NC)
    return (20, A_GROUPS, source)


def plan_embed(t, layer):
    return ((2, 1, lambda k, g: dma_parts(t["pe_w_proj"][layer], 0, 2, k * 2 * NC, 2 * NC)),
            (8, 2, lambda k, g: dma_parts(t["pe_w_gate"][layer], k % 4 * 4, 4, g * 2 * NC + k // 4 * NC)))


def trunk(nc, t, depth=DEPTH):
    with ExitStack() as ctx:
        K = Kernel(nc, ctx, t)
        K.plan = []
        for i in range(depth):
            if i % 3 == 0:
                K.plan.append(plan_attention(t, i // 3))
            elif i % 3 == 1:
                K.plan += plan_rwkv(t)
            else:
                K.plan += plan_deltanet(t)
            K.plan += plan_embed(t, i)
        cs = K.sb("cs", [P, 2, NT, ROT_HALF])
        start_stage(K, cs)
        no = 0
        for i in range(depth):
            j = i // 3
            with ExitStack() as st:
                if i % 3 == 0:
                    hi, lo = K.sb("h_hi", [P, KT, SEQ], F32R, ctx=st), K.sb("h_lo", [P, KT, SEQ], F32R, ctx=st)
                    norm_stage(K, None, ("norm_g", i * KT), hi, lo)
                    attention_stage(K, no, j, 0.8 - 0.6 * math.exp(-0.3 * i), hi, lo, cs)
                    no += 1
                elif i % 3 == 1:
                    no = rwkv(K, no, i)
                else:
                    no = deltanet(K, no, i, st)
            with ExitStack() as st:
                hi, lo = K.sb("h_hi", [P, KT, SEQ], F32R, ctx=st), K.sb("h_lo", [P, KT, SEQ], F32R, ctx=st)
                pp = K.sb("pp", [P, NT, D], ctx=st)
                norm_stage(K, no, ("pe_norm_g", i * KT), hi, lo, embed=(i, pp))
                gate_stage(K, no + 1, hi, lo, pp)
                no += 2
        final_stage(K)


OUT = (1, SEQ, D)
WHOLE = ["pe_w_gate", "pe_w_proj", "final_norm_g", "a_w_in", "a_w_out", "b_w_rkvg", "b_w_w1", "b_w_w2", "b_w_a1",
         "b_w_a2", "b_w_out", "c_w_in", "c_w_out", "b_w0", "b_a0", "b_k_k", "b_k_a", "b_ln_w", "b_ln_b", "c_A_log",
         "c_dt_bias"]


def lay_out(inputs):
    a = {n: np.ascontiguousarray(inputs[n]) for n in WHOLE}
    a["x"] = np.ascontiguousarray(inputs["x"]).reshape(SEQ, D)
    a["p_t"] = np.ascontiguousarray(np.asarray(inputs["p"]).reshape(DEPTH, SEQ, PLE).transpose(0, 2, 1))
    a["positions"] = np.ascontiguousarray(np.asarray(inputs["positions"]).reshape(NT, P).T)
    a["a_lam"] = np.ascontiguousarray(inputs["a_lam"]).reshape(2, 4 * A_HD)
    a["b_r_k"] = np.ascontiguousarray(inputs["b_r_k"]).reshape(1, D)

    def per_partition(name):
        v = np.asarray(inputs[name])
        return v.reshape(-1, P).T

    conv = np.asarray(inputs["c_conv_w"]).reshape(C_TAPS, 64, P).transpose(2, 1, 0).reshape(P, 64 * C_TAPS)
    parts = [per_partition(n) for n in ("norm_g", "pe_norm_g", "b_mu", "a_subln_g", "c_norm_g")] + [conv]
    a["cols"] = np.ascontiguousarray(np.concatenate(parts, 1))
    a["con"] = constants()
    return a


def build(nc, arrays, depth=DEPTH):
    t = {n: nc.dram_tensor(f"in_{n}", a.shape, mybir.dt.from_np(a.dtype), kind="ExternalInput").ap()
         for n, a in arrays.items()}
    t["out"] = nc.dram_tensor("out", (SEQ, D), F32, kind="ExternalOutput").ap()
    trunk(nc, t, depth)


def kernel(**inputs):
    import concourse.bacc as bacc
    from concourse.bass_utils import run_bass_kernel_spmd

    nc = bacc.Bacc("TRN2", target_bir_lowering=False, num_devices=1)
    arrays = lay_out(inputs)
    build(nc, arrays)
    r = run_bass_kernel_spmd(nc, [{f"in_{n}": a for n, a in arrays.items()}], core_ids=[0])
    return r.results[0]["out"].reshape(OUT)
```
